# Optimizing a Trainium2 kernel written in Bass

```python
import math
import jax, jax.numpy as jnp
from jax import lax
import numpy as np

D_MODEL = 1024
BATCH = 1
SEQ = 1024
DEPTH = 1

CHUNK = 64
N_MEM = 256

MLA_HEADS = 8
MLA_NOPE = 64
MLA_ROPE = 32
MLA_V = 64
Q_LORA = 256
KV_LORA = 128
ROPE_THETA = 10000.0
Q_BLOCK = 128

SWA_HEADS = 8
SWA_KV_HEADS = 2
SWA_HEAD_DIM = 64
WINDOW = 128
WINDOW_CHUNKS = WINDOW // CHUNK

MIX_WIDTH = MLA_HEADS * MLA_V + SWA_HEADS * SWA_HEAD_DIM
IN_SPLITS = [Q_LORA, KV_LORA, MLA_ROPE, SWA_HEADS * SWA_HEAD_DIM, SWA_KV_HEADS * SWA_HEAD_DIM, SWA_KV_HEADS * SWA_HEAD_DIM]
IN_COLS = sum(IN_SPLITS)

MEM_HEADS = 4
MEM_HEAD_DIM = 128

N_GROUPS = 4
EXPERTS_PER_GROUP = 8
N_EXPERTS = N_GROUPS * EXPERTS_PER_GROUP
TOP_K = 2
D_EXPERT = 512
MOE_BLOCK = 128

ALPHA = (2 * DEPTH) ** 0.25
BETA = (8 * DEPTH) ** -0.25
LN_EPS = 1e-5
RMS_EPS = 1e-6

kernel_name = "hybrid_mla_swa_sink_hmoe_deepnorm"

def layer_norm(x, g, b):
    xf = x.astype(jnp.float32)
    mu = jnp.mean(xf, -1, keepdims=True)
    var = jnp.mean(jnp.square(xf - mu), -1, keepdims=True)
    y = (xf - mu) * lax.rsqrt(var + LN_EPS) * g.astype(jnp.float32) + b.astype(jnp.float32)
    return y.astype(x.dtype)

def rms_norm(x, g):
    xf = x.astype(jnp.float32)
    y = xf * lax.rsqrt(jnp.mean(xf * xf, -1, keepdims=True) + RMS_EPS) * g.astype(jnp.float32)
    return y.astype(x.dtype)

def rope_tables(positions):
    inv = ROPE_THETA ** (-jnp.arange(0, MLA_ROPE, 2, dtype=jnp.float32) / MLA_ROPE)
    ang = positions.astype(jnp.float32)[..., None] * inv
    return jnp.cos(ang), jnp.sin(ang)

def apply_rope(x, cos, sin):
    xf = x.astype(jnp.float32)
    x1, x2 = jnp.split(xf, 2, axis=-1)
    return jnp.concatenate([x1 * cos - x2 * sin, x1 * sin + x2 * cos], axis=-1).astype(x.dtype)

def alibi_slopes(n):
    return 2.0 ** (-8.0 * jnp.arange(1, n + 1, dtype=jnp.float32) / n)

def mla_attention(c_q, c_kv, k_rope, positions, g_q, w_uq, g_kv, w_ukv):
    B, S, _ = c_q.shape
    q = (rms_norm(c_q, g_q) @ w_uq).reshape(B, S, MLA_HEADS, MLA_NOPE + MLA_ROPE)
    q_nope, q_pe = q[..., :MLA_NOPE], q[..., MLA_NOPE:]
    kv = (rms_norm(c_kv, g_kv) @ w_ukv).reshape(B, S, MLA_HEADS, MLA_NOPE + MLA_V)
    k_nope, v = kv[..., :MLA_NOPE], kv[..., MLA_NOPE:]
    cos, sin = rope_tables(positions)
    q_pe = apply_rope(q_pe, cos[:, :, None], sin[:, :, None])
    k_pe = apply_rope(k_rope, cos, sin)
    scale = (MLA_NOPE + MLA_ROPE) ** -0.5
    chunk_id = jnp.arange(S) // CHUNK
    outs = []
    for start in range(0, S, Q_BLOCK):
        end = start + Q_BLOCK
        s = (jnp.einsum('bqhd,bkhd->bhqk', q_nope[:, start:end], k_nope[:, :end])
             + jnp.einsum('bqhr,bkr->bhqk', q_pe[:, start:end], k_pe[:, :end]))
        s = s.astype(jnp.float32) * scale
        mask = chunk_id[start:end, None] >= chunk_id[None, :end]
        p = jax.nn.softmax(jnp.where(mask, s, -jnp.inf), axis=-1).astype(v.dtype)
        outs.append(jnp.einsum('bhqk,bkhd->bqhd', p, v[:, :end]))
    return jnp.concatenate(outs, axis=1).reshape(B, S, MLA_HEADS * MLA_V)

def swa_sink_attention(q, k, v, sinks):
    B, S, _ = q.shape
    NC = S // CHUNK
    G = SWA_HEADS // SWA_KV_HEADS
    BAND = WINDOW_CHUNKS * CHUNK
    qc = q.reshape(B, NC, CHUNK, SWA_KV_HEADS, G, SWA_HEAD_DIM)
    kc = k.reshape(B, NC, CHUNK, SWA_KV_HEADS, SWA_HEAD_DIM)
    vc = v.reshape(B, NC, CHUNK, SWA_KV_HEADS, SWA_HEAD_DIM)

    def band(t):
        tp = jnp.concatenate([jnp.zeros_like(t[:, :WINDOW_CHUNKS - 1]), t], axis=1)
        return jnp.concatenate([tp[:, i:i + NC] for i in range(WINDOW_CHUNKS)], axis=2)

    kb, vb = band(kc), band(vc)
    s = jnp.einsum('bcqkgd,bcskd->bckgqs', qc, kb).astype(jnp.float32) * (SWA_HEAD_DIM ** -0.5)
    i = jnp.arange(CHUNK)
    j = jnp.arange(BAND)
    dist = jnp.abs(i[:, None] + (WINDOW_CHUNKS - 1) * CHUNK - j[None, :]).astype(jnp.float32)
    slopes = alibi_slopes(SWA_HEADS).reshape(SWA_KV_HEADS, G)
    s = s - slopes[:, :, None, None] * dist
    key_chunk = jnp.arange(NC)[:, None] - (WINDOW_CHUNKS - 1) + j[None, :] // CHUNK
    s = jnp.where((key_chunk >= 0)[None, :, None, None, None, :], s, -jnp.inf)
    sink = sinks.astype(jnp.float32).reshape(SWA_KV_HEADS, G)[None, None, :, :, None, None]
    sink = jnp.broadcast_to(sink, s.shape[:-1] + (1,))
    p = jax.nn.softmax(jnp.concatenate([s, sink], axis=-1), axis=-1)[..., :-1].astype(v.dtype)
    o = jnp.einsum('bckgqs,bcskd->bcqkgd', p, vb)
    return o.reshape(B, S, SWA_HEADS * SWA_HEAD_DIM)

def hybrid_mixer(h, positions, w_in, g_q, w_uq, g_kv, w_ukv, sinks, w_o):
    proj = h @ w_in
    c_q, c_kv, k_rope, q_s, k_s, v_s = jnp.split(proj, np.cumsum(IN_SPLITS)[:-1].tolist(), axis=-1)
    y_mla = mla_attention(c_q, c_kv, k_rope, positions, g_q, w_uq, g_kv, w_ukv)
    y_swa = swa_sink_attention(q_s, k_s, v_s, sinks)
    return jnp.concatenate([y_mla, y_swa], axis=-1) @ w_o

def memory_cross_attention(h, mem, w_mq, w_mk, w_mv, w_mo):
    B, S, _ = h.shape
    M = mem.shape[1]
    q = (h @ w_mq).reshape(B, S, MEM_HEADS, MEM_HEAD_DIM)
    k = (mem @ w_mk).reshape(B, M, MEM_HEADS, MEM_HEAD_DIM)
    v = (mem @ w_mv).reshape(B, M, MEM_HEADS, MEM_HEAD_DIM)
    s = jnp.einsum('bqhd,bmhd->bhqm', q, k).astype(jnp.float32) * (MEM_HEAD_DIM ** -0.5)
    p = jax.nn.softmax(s, axis=-1).astype(v.dtype)
    o = jnp.einsum('bhqm,bmhd->bqhd', p, v).reshape(B, S, MEM_HEADS * MEM_HEAD_DIM)
    return o @ w_mo

def hierarchical_moe(h, w_group, b_group, w_expert, b_expert, w_gate_up, w_down):
    B, S, D = h.shape
    xt = h.reshape(-1, D)
    T = xt.shape[0]
    group_probs = jax.nn.softmax((xt @ w_group).astype(jnp.float32) + b_group.astype(jnp.float32), axis=-1)
    g_prob, g_idx = lax.top_k(group_probs, 1)
    expert_logits = ((xt @ w_expert).astype(jnp.float32) + b_expert.astype(jnp.float32)).reshape(T, N_GROUPS, EXPERTS_PER_GROUP)
    sel = jnp.take_along_axis(expert_logits, jnp.broadcast_to(g_idx[:, :, None], (T, 1, EXPERTS_PER_GROUP)), axis=1)[:, 0]
    e_prob, e_local = lax.top_k(jax.nn.softmax(sel, axis=-1), TOP_K)
    e_prob = e_prob / jnp.sum(e_prob, -1, keepdims=True)
    gates = g_prob * e_prob
    expert_idx = g_idx * EXPERTS_PER_GROUP + e_local

    A = T * TOP_K
    flat_e = expert_idx.reshape(A)
    flat_tok = jnp.repeat(jnp.arange(T, dtype=jnp.int32), TOP_K)
    flat_w = gates.reshape(A)
    order = jnp.argsort(flat_e)
    se = flat_e[order]
    counts = jax.ops.segment_sum(jnp.ones((A,), jnp.int32), flat_e, num_segments=N_EXPERTS)
    starts = jnp.cumsum(counts) - counts
    padded = (counts + MOE_BLOCK - 1) // MOE_BLOCK * MOE_BLOCK
    pad_ends = jnp.cumsum(padded)
    pad_starts = pad_ends - padded
    dest = pad_starts[se] + jnp.arange(A, dtype=jnp.int32) - starts[se]
    n_blocks = -(-(A + N_EXPERTS * (MOE_BLOCK - 1)) // MOE_BLOCK)
    n_rows = n_blocks * MOE_BLOCK
    row_tok = jnp.zeros((n_rows,), jnp.int32).at[dest].set(flat_tok[order])
    row_w = jnp.zeros((n_rows,), jnp.float32).at[dest].set(flat_w[order])
    block_expert = jnp.minimum(
        jnp.searchsorted(pad_ends, jnp.arange(n_blocks, dtype=jnp.int32) * MOE_BLOCK, side='right'),
        N_EXPERTS - 1)
    xs = xt[row_tok].reshape(n_blocks, MOE_BLOCK, D)

    def expert_block(args):
        xb, e = args
        gate, up = jnp.split(xb @ w_gate_up[e], 2, axis=-1)
        return (jax.nn.silu(gate) * up) @ w_down[e]

    ys = lax.map(expert_block, (xs, block_expert)).reshape(n_rows, D)
    out = jax.ops.segment_sum(ys * row_w[:, None].astype(ys.dtype), row_tok, num_segments=T)
    return out.reshape(B, S, D)

def setup_inputs(seed: int = 0) -> dict:
    key = jax.random.key(seed)
    ks = jax.random.split(key, 32)
    f32 = jnp.float32

    def nrm(k, shape, scale):
        return jax.random.normal(k, shape, f32) * scale

    def gain(k, shape):
        return 1.0 + 0.02 * jax.random.normal(k, shape, f32)

    L, D = DEPTH, D_MODEL
    offsets = jax.random.randint(ks[0], (BATCH, 1), 0, 65536, dtype=jnp.int32)
    positions = offsets + jnp.arange(SEQ, dtype=jnp.int32)[None, :]
    return {
        "x": jax.random.normal(ks[1], (BATCH, SEQ, D), f32),
        "positions": positions,
        "mem": jax.random.normal(ks[2], (BATCH, N_MEM, D), f32),
        "ln_in_g": gain(ks[3], (D,)),
        "ln_in_b": nrm(ks[4], (D,), 0.02),
        "w_in": nrm(ks[5], (L, D, IN_COLS), D ** -0.5),
        "g_q": gain(ks[6], (L, Q_LORA)),
        "w_uq": nrm(ks[7], (L, Q_LORA, MLA_HEADS * (MLA_NOPE + MLA_ROPE)), Q_LORA ** -0.5),
        "g_kv": gain(ks[8], (L, KV_LORA)),
        "w_ukv": nrm(ks[9], (L, KV_LORA, MLA_HEADS * (MLA_NOPE + MLA_V)), KV_LORA ** -0.5),
        "sinks": nrm(ks[10], (L, SWA_HEADS), 1.0),
        "w_o": nrm(ks[11], (L, MIX_WIDTH, D), MIX_WIDTH ** -0.5 * BETA),
        "ln1_g": gain(ks[12], (L, D)),
        "ln1_b": nrm(ks[13], (L, D), 0.02),
        "w_mq": nrm(ks[14], (L, D, MEM_HEADS * MEM_HEAD_DIM), D ** -0.5),
        "w_mk": nrm(ks[15], (L, D, MEM_HEADS * MEM_HEAD_DIM), D ** -0.5),
        "w_mv": nrm(ks[16], (L, D, MEM_HEADS * MEM_HEAD_DIM), D ** -0.5),
        "w_mo": nrm(ks[17], (L, MEM_HEADS * MEM_HEAD_DIM, D), (MEM_HEADS * MEM_HEAD_DIM) ** -0.5 * BETA),
        "ln2_g": gain(ks[18], (L, D)),
        "ln2_b": nrm(ks[19], (L, D), 0.02),
        "w_group": nrm(ks[20], (L, D, N_GROUPS), D ** -0.5),
        "b_group": nrm(ks[21], (L, N_GROUPS), 0.01),
        "w_expert": nrm(ks[22], (L, D, N_EXPERTS), D ** -0.5),
        "b_expert": nrm(ks[23], (L, N_EXPERTS), 0.01),
        "w_gate_up": nrm(ks[24], (L, N_EXPERTS, D, 2 * D_EXPERT), D ** -0.5),
        "w_down": nrm(ks[25], (L, N_EXPERTS, D_EXPERT, D), D_EXPERT ** -0.5 * BETA),
        "ln3_g": gain(ks[26], (L, D)),
        "ln3_b": nrm(ks[27], (L, D), 0.02),
    }

def reference(x, positions, mem, ln_in_g, ln_in_b, w_in, g_q, w_uq, g_kv, w_ukv, sinks, w_o,
              ln1_g, ln1_b, w_mq, w_mk, w_mv, w_mo, ln2_g, ln2_b,
              w_group, b_group, w_expert, b_expert, w_gate_up, w_down, ln3_g, ln3_b):
    h = layer_norm(x, ln_in_g, ln_in_b)
    for l in range(DEPTH):
        mix = hybrid_mixer(h, positions, w_in[l], g_q[l], w_uq[l], g_kv[l], w_ukv[l], sinks[l], w_o[l])
        h = layer_norm(ALPHA * h + mix, ln1_g[l], ln1_b[l])
        xat = memory_cross_attention(h, mem, w_mq[l], w_mk[l], w_mv[l], w_mo[l])
        h = layer_norm(ALPHA * h + xat, ln2_g[l], ln2_b[l])
        ffn = hierarchical_moe(h, w_group[l], b_group[l], w_expert[l], b_expert[l], w_gate_up[l], w_down[l])
        h = layer_norm(ALPHA * h + ffn, ln3_g[l], ln3_b[l])
    return h


_drawn_inputs = setup_inputs


def setup_inputs(seed=0):
    import zlib

    import numpy as np

    out = dict(_drawn_inputs(seed))
    spreads = {}
    factors = {'g_q': 8.0,
     'g_kv': 8.0,
     'b_group': 33.619,
     'b_expert': 19.828,
     'ln3_g': 7.803,
     'ln3_b': 8.727,
     'sinks': 6.845}
    for name, (base, spread) in spreads.items():
        noise = np.random.default_rng([zlib.crc32(name.encode()), seed]).standard_normal(out[name].shape)
        drawn = base * np.exp(spread * noise) if base else spread * noise
        out[name] = __import__('jax').numpy.asarray(drawn.astype(out[name].dtype))
    for name, factor in factors.items():
        out[name] = (out[name] * factor).astype(out[name].dtype)
    return out
```

```python
import numpy as np
from contextlib import ExitStack

import concourse.bass as bass
from concourse import mybir

F32 = mybir.dt.float32
I32 = mybir.dt.int32
ALU = mybir.AluOpType
ACT = mybir.ActivationFunctionType
X = mybir.AxisListType.X

P = 128
SEQ, D = 1024, 1024
NT, KC = SEQ // P, D // P
HALF = 512
N_MEM, MEM_HEADS, MEM_DIM = 256, 4, 128
MLA_HEADS, NOPE, ROPE, MLA_V = 8, 64, 32, 64
QK = NOPE + ROPE
Q_LORA, KV_LORA = 256, 128
SWA_HEADS, SWA_KV, SWA_DIM, CHUNK = 8, 2, 64, 64
GQ = SWA_HEADS // SWA_KV
BAND = 3 * CHUNK
N_GROUPS, PER_GROUP = 4, 8
N_EXP = N_GROUPS * PER_GROUP
F_EXP = 512
TOP_K = 2
ROUTE = N_GROUPS + N_EXP
MAX_ITEMS = SEQ * TOP_K // P + N_EXP
ALPHA = 2.0 ** 0.25
LN_EPS, RMS_EPS = 1e-5, 1e-6
MASKED = -1e30
NO_ROW = 1 << 20
IN_COLS = Q_LORA + KV_LORA + ROPE + (SWA_HEADS + 2 * SWA_KV) * SWA_DIM
TWO_PI_1 = 6.28125
TWO_PI_2 = 0.0019350051879882812
TWO_PI_3 = 2 * np.pi - TWO_PI_1 - TWO_PI_2
ROUNDER = 1.5 * 2.0 ** 23
C_KV, C_QS, C_KS, C_KR = Q_LORA, Q_LORA + KV_LORA, Q_LORA + KV_LORA + 512, Q_LORA + KV_LORA + 640


def attention_units():
    units = [("q", 0, 0)]
    for j in range(NT):
        for h in range(MLA_HEADS):
            units.append(("m", j, h))
            if h == 3 and j:
                units.append(("y", j - 1, 0))
            if h == 6 and j + 1 < NT:
                units.append(("q", j + 1, 0))
        units += [("s", j, 0), ("s", j, 1)]
    return units + [("gap", 0, 0), ("y", NT - 1, 0)]


UNITS = attention_units()
SCORED = [u for u in UNITS if u[0] in "qms"]
SOFTMAXED = [u for u in UNITS if u[0] in "ms"]
N_SCORE = {u: n for n, u in enumerate(SCORED)}
N_SOFT = {u: n for n, u in enumerate(SOFTMAXED)}


def chunks_of(u):
    kind, j, _ = u
    if kind == "m":
        return 1 if j < 4 else 2
    if kind == "s":
        return 1 if j == 0 else 2
    return 2 if kind == "y" else 0


def number_chunks():
    keys = [("mem", t, c) for t in range(2) for c in range(2)]
    keys += [("x", j, c) for j in range(NT) for c in range(2)]
    keys += [("kpe", 0, c) for c in range(2)]
    keys += [(u, c) for u in UNITS for c in range(chunks_of(u))]
    for s in range(NT + 3):
        if 0 <= s - 2 < NT:
            keys += [("p8", s - 2, c) for c in range(2)]
        if 0 <= s - 1 < NT:
            keys += [("h1", s - 1, c) for c in range(2)]
        if 0 <= s - 2 < NT:
            keys += [("o8", s - 2, 0)]
        if 0 <= s - 3 < NT:
            keys += [("h2", s - 3, c) for c in range(2)]
    return {k: n for n, k in enumerate(keys)}


CHUNK_NO = number_chunks()
N_CHUNKS = len(CHUNK_NO)


def number_projections():
    uses = []
    for s in range(NT + 3):
        if s < NT:
            uses.append(("A", s))
        if 0 <= s - 2 < NT:
            uses.append(("E", s - 2))
    return {k: n for n, k in enumerate(uses)}


PROJ_NO = number_projections()
LN_NO = {("in", j): j for j in range(NT)}
LN_NO |= {(k, j): NT + n for (k, j), n in PROJ_NO.items()}
LN_NO |= {("out", j): 3 * NT + j for j in range(NT)}



def build_program(nc, a, o):
    h0_d = nc.dram_tensor("h0_scratch", [SEQ, D], F32).ap()
    h2_d = nc.dram_tensor("h2_scratch", [SEQ, D], F32).ap()
    ye_d = nc.dram_tensor("expert_rows_scratch", [SEQ * TOP_K, D], F32).ap()
    table_d = nc.dram_tensor("table_scratch", [(MAX_ITEMS + 2) * P, 4], I32).ap()
    ctx = ExitStack()
    with ctx:
        kib = 1024
        base = nc.sbuf_base + (-nc.sbuf_base) % 64

        def at(name, shape, off, dt=F32):
            return nc.alloc_sbuf_tensor_at(name, shape, dt, offset=base + int(off * kib))

        def sem(name):
            return ctx.enter_context(nc.semaphore(name))

        hring = at("hring", [P, 4, D], 0)
        hT = at("hT", [P, KC, SEQ], 16)
        yT = at("yT", [P, KC, SEQ], 16)
        w_in = at("w_in_sb", [P, KC, IN_COLS], 48)
        kcat = at("kcat", [QK, MLA_HEADS, SEQ], 48)
        w_mq = at("w_mq_sb", [P, KC, 512], 48)
        w_mo = at("w_mo_sb", [P, MEM_HEADS, D], 64)
        tri = at("tri", [P, P], 80)
        ones = at("ones", [P, P], 80.5)
        iotas = at("iotas", [P, N_EXP + MAX_ITEMS], 81)
        rows = at("rows", [P, NT, TOP_K, 4], 81.5, I32)
        route_b = at("route_b", [P, ROUTE], 82)
        w_route = at("w_route_sb", [P, KC, ROUTE], 82.25)
        w_mk = at("w_mk_sb", [P, KC, 512], 85)
        w_mv = at("w_mv_sb", [P, KC, 512], 101)
        vmla = at("vmla", [P, NT, 512], 85)
        qs = at("qs", [P, GQ, SEQ], 101)
        w_o = at("w_o_sb", [P, KC, D], 85)
        wq = at("wq", [P, 2, MLA_HEADS, P], 117)
        wukv = at("wukv", [P, 2, MLA_HEADS, NOPE], 125)
        cq = at("cq", [P, 2, SEQ], 129)
        gb2 = at("gb2", [P, 2, D], 129)
        ckv = at("ckv", [P, SEQ], 137)
        om = at("om", [P, 512], 137)
        omT = at("omT", [P, MEM_HEADS, P], 139)
        memT = at("memT", [P, KC, N_MEM], 141)
        qcat = at("qcat", [QK, 2, MLA_HEADS, P], 141)
        h1T = at("h1T", [P, 2, KC, P], 141)
        ks = at("ks", [P, SEQ], 149)
        qm = at("qm", [P, MEM_HEADS, P], 149)
        krvs = at("krvs", [P, NT, ROPE + P], 153)
        h2T = at("h2T", [P, KC, P], 153)
        mem_sb = at("mem_sb", [P, 2, D], 158)
        prob = at("prob", [P, 2, D], 158)
        sq = at("sq", [P, 3, SEQ], 158)
        wuq = at("wuq_raw", [P, 2, MLA_HEADS, QK], 168)
        probT = at("probT", [P, 2, KC, P], 166)
        pos_all = at("pos_all", [P, SEQ], 174, I32)
        alibi = at("alibi", [P, SWA_HEADS, BAND], 174)
        trig_t = at("trig_t", [P, SEQ], 180)
        y = at("y", [P, D], 180)
        vm = at("vm", [P, 2, 512], 184)
        kmT = at("kmT", [P, MEM_HEADS, N_MEM], 188)
        cs = at("cos_sin", [P, SEQ], 192)
        gb1 = at("gb1", [P, 2, D], 196)
        w_gu = [at("w_gu0", [P, KC, 2 * F_EXP], 16), at("w_gu1", [P, KC, 2 * F_EXP], 85)]
        w_dn = [at("w_dn0", [P, 4, D], 48), at("w_dn1", [P, 4, D], 64)]
        xg = [at("xg0", [P, D], 129), at("xg1", [P, D], 133)]
        xgT = [at("xgT0", [P, KC, P], 141), at("xgT1", [P, KC, P], 145)]
        gate_s = at("gate_s", [P, F_EXP], 137)
        act = [at("act0", [P, F_EXP], 139), at("act1", [P, F_EXP], 149)]
        actT = [at("actT0", [P, 4, P], 151), at("actT1", [P, 4, P], 153)]
        ye = [at("ye0", [P, D], 158), at("ye1", [P, D], 162)]
        tab_x = [at("tab_x0", [P, 4], 155, I32), at("tab_x1", [P, 4], 155.25, I32)]
        tab_y = [at("tab_y0", [P, 4], 155.5, I32), at("tab_y1", [P, 4], 155.75, I32)]
        pair = [at("pair0", [P, 2, D], 166), at("pair1", [P, 2, D], 174)]
        small_at = [117.0]

        def scratch(name, shape, dt=F32):
            off = small_at[0]
            small_at[0] += -(-int(np.prod(shape[1:])) * 4 // 64) * 64 / kib
            return at(name, shape, off, dt)

        TE = [P, NT, N_EXP]
        elm, eqx, oh1, oh2, rank, place = (scratch(n, TE) for n in ("elm", "eqx", "oh1", "oh2", "rank", "place"))
        oh_sum, tot = scratch("oh_sum", TE), scratch("tot", TE)
        gl, eg, gpen = (scratch(n, [P, NT, N_GROUPS]) for n in ("gl", "eg", "gpen"))
        t8 = [scratch(f"t8_{i}", [P, NT]) for i in range(10)]
        cnt, nblk, incl = (scratch(n, [P, N_EXP]) for n in ("cnt", "nblk", "incl"))
        posf, posi = scratch("posf", [P, NT, TOP_K]), scratch("posi", [P, NT, TOP_K], I32)
        assert small_at[0] <= 129
        item_cmp = at("item_cmp", [1, MAX_ITEMS, N_EXP], 158)
        small_at[0] = 204.0
        ident = scratch("ident", [P, P])
        logits = scratch("logits", [P, NT, ROUTE])
        stats, mv = scratch("stats", [P, 2, 2, 6]), scratch("mv", [P, 2, 2])
        var, rstd = scratch("var", [P, 4 * NT]), scratch("rstd", [P, 4 * NT])
        neghalf = scratch("neghalf", [P, 16])
        neg_max = scratch("neg_max", [P, 4, 4])
        sums_m, sums_s = scratch("sums_m", [P, 2, 8]), scratch("sums_s", [P, 2, 8])
        sums_x = scratch("sums_x", [P, 4])
        sink_e, sink_d, sink = (scratch(n, [P, 2, 8]) for n in ("sink_e", "sink_d", "sink"))
        rinv, rmax = scratch("rinv", [P, 8]), scratch("rmax", [P, 4])
        one_col, item_f = scratch("one_col", [P, 1]), scratch("item_f", [1, MAX_ITEMS])
        gq, gkv = scratch("gq", [P, 4]), scratch("gkv", [P, 1])
        rope_f = scratch("rope_f", [P, 4])
        ms, rms = scratch("ms", [P, 16]), scratch("rms", [P, 16])
        item_exp, n_items_t = scratch("item_exp", [1, MAX_ITEMS], I32), scratch("n_items_t", [1, 1], I32)
        assert base + small_at[0] * kib <= nc.sbuf_usable_end, small_at
        pos_t, posf_t = at("pos_t", [P, NT], 178, I32), at("posf_t", [P, NT], 178.25)
        inv_b = at("inv_b", [P, 16], 178.5)
        kang, kang_t = at("kang", [P, 2, NT, 16], 180), at("kang_t", [P, NT, 16], 181)
        krot, krot_t = at("krot", [P, NT, ROPE], 182), at("krot_t", [P, NT, 16], 183)

        psT = ctx.enter_context(nc.psum_tensor("psT", [P, 2, 512], F32))
        psS = ctx.enter_context(nc.psum_tensor("psS", [P, 2, D], F32))
        psM = ctx.enter_context(nc.psum_tensor("psM", [P, 512], F32))
        psN = ctx.enter_context(nc.psum_tensor("psN", [P, 512], F32))

        def bank(i):
            return [psT[:, 0, :], psT[:, 1, :], psS[:, 0, 0:512], psS[:, 0, 512:D],
                    psS[:, 1, 0:512], psS[:, 1, 512:D], psM[:, :], psN[:, :]][i]

        ld_ident, ld_gb1, ld_gb2, ld_wup, ld_pos, ld_small = (sem(n) for n in (
            "ld_ident", "ld_gb1", "ld_gb2", "ld_wup", "ld_pos", "ld_small"))
        ld_mem, ld_mk, ld_mv, ld_win, ld_alibi, ld_late = (sem(n) for n in (
            "ld_mem", "ld_mk", "ld_mv", "ld_win", "ld_alibi", "ld_late"))
        ld_x = [sem(f"ld_x{s}") for s in range(4)]
        ld_h0 = [sem(f"ld_h0_{s}") for s in range(4)]
        st_h0 = [sem(f"st_h0_{s}") for s in range(4)]
        st_h2 = [sem(f"st_h2_{s}") for s in range(4)]
        ld_wo, ld_wmq, ld_wmo = sem("ld_wo"), sem("ld_wmq"), sem("ld_wmo")
        v_done, var_ready, rstd_ready, ln_done = (sem(n) for n in ("v_done", "var_ready", "rstd_ready", "ln_done"))
        t_full = sem("t_full")
        t_free = [sem("t_free0"), sem("t_free1")]
        mem_full, mem_free = sem("mem_full"), sem("mem_free")
        pj_full, pj_free, kv_full, kv_free = (sem(n) for n in ("pj_full", "pj_free", "kv_full", "kv_free"))
        pool_const, wq_ready, sq_ready, ss_full, ms_ready, rms_ready = (sem(n) for n in (
            "pool_const", "wq_ready", "sq_ready", "ss_full", "ms_ready", "rms_ready"))
        rb_full, cqn_ready, kn_full, kn_free, vv_full, vv_free = (sem(n) for n in (
            "rb_full", "cqn_ready", "kn_full", "kn_free", "vv_full", "vv_free"))
        trig_ready, trig_done, krot_ready, kpe_all = (sem(n) for n in ("trig_ready", "trig_done", "krot_ready", "kpe_all"))
        s_full = sem("s_full")
        s_free = [sem("s_free0"), sem("s_free1")]
        rope_read, rope_done, mx_ready, p_ready = (sem(n) for n in ("rope_read", "rope_done", "mx_ready", "p_ready"))
        pv_full, y_ready = sem("pv_full"), sem("y_ready")
        ae_full, ae_free, qm_full, qm_ready, c_full, nm8_ready, p8_ready = (sem(n) for n in (
            "ae_full", "ae_free", "qm_full", "qm_ready", "c_full", "nm8_ready", "p8_ready"))
        o8_full, om_ready, r_full, r_ready = (sem(n) for n in ("o8_full", "om_ready", "r_full", "r_ready"))
        oh_ready, rank_full, g_exp_in, g_exp_out, pos_ready, items_ready = (sem(n) for n in (
            "oh_ready", "rank_full", "g_exp_in", "g_exp_out", "pos_ready", "items_ready"))
        pool_ready = sem("pool_ready")
        fill_done, table_done, rows_done = sem("fill_done"), sem("table_done"), sem("rows_done")
        gu_loaded = [[sem(f"gu_loaded{s}{h}") for h in range(2)] for s in range(2)]
        dn_loaded = [sem(f"dn_loaded{s}") for s in range(2)]
        tokens_loaded = [sem("tokens_loaded0"), sem("tokens_loaded1")]
        places_loaded = [sem("places_loaded0"), sem("places_loaded1")]
        x_loaded = [sem("x_loaded0"), sem("x_loaded1")]
        xT_full, xT_ready = [sem("xT_full0"), sem("xT_full1")], [sem("xT_ready0"), sem("xT_ready1")]
        gu_full, silu_done, act_ready = sem("gu_full"), sem("silu_done"), sem("act_ready")
        aT_full, aT_ready, y_full, ye_ready = sem("aT_full"), sem("aT_ready"), sem("y_full"), [sem("ye_ready0"), sem("ye_ready1")]
        ye_stored = [sem("ye_stored0"), sem("ye_stored1")]
        ld_pair = [sem("ld_pair0"), sem("ld_pair1")]
        ld_h2 = [sem(f"ld_h2_{s}") for s in range(4)]
        st_out = [sem(f"st_out{s}") for s in range(4)]
        pair_free = sem("pair_free")

        def ktile(w):
            return w.rearrange("(k p) n -> p k n", p=P)

        def bcast(v):
            return v.to_broadcast([P, v.shape[1]])

        LAST_SOFT = len(SOFTMAXED)
        FREE_S = [(len(SCORED) + 1 - s) // 2 for s in range(2)]

        block = ctx.enter_context(nc.Block())

        @block.sync
        def _(sp):
            sp.dma_start(mem_sb[:, :, :], a["mem"].rearrange("(t p) d -> p t d", p=P)).then_inc(ld_mem, 16)
            sp.dma_start(w_mk[:, :, :], ktile(a["w_mk"])).then_inc(ld_mk, 16)
            sp.dma_start(hring[:, 0, :], a["x"][0:P, :]).then_inc(ld_x[0], 16)
            sp.dma_start(w_mv[:, :, :], ktile(a["w_mv"])).then_inc(ld_mv, 16)
            for j in range(1, 4):
                sp.dma_start(hring[:, j, :], a["x"][j * P:(j + 1) * P, :]).then_inc(ld_x[j], 16)
            w_src = ktile(a["w_in"])
            kr = Q_LORA + KV_LORA
            for dst, src, n in ((0, 0, kr), (C_QS, kr + ROPE, 640), (C_KR, kr, ROPE), (C_KR + ROPE, kr + ROPE + 640, P)):
                sp.dma_start(w_in[:, :, dst:dst + n], w_src[:, :, src:src + n]).then_inc(ld_win, 16)
            for j in range(NT):
                sp.wait_ge(ln_done, LN_NO["in", j] + 1)
                sp.dma_start(h0_d[j * P:(j + 1) * P, :], hring[:, j % 4, :]).then_inc(st_h0[j % 4], 16)
                if j + 4 < NT:
                    sp.wait_ge(st_h0[j % 4], 16)
                    sp.wait_ge(t_full, CHUNK_NO["x", j, 1] + 1)
                    sp.dma_start(hring[:, j % 4, :], a["x"][(j + 4) * P:(j + 5) * P, :]).then_inc(ld_x[j % 4], 16)
            sp.dma_start(gb1[:, 0, :], bcast(a["ln1_g"])).then_inc(ld_gb1, 16)
            sp.dma_start(gb1[:, 1, :], bcast(a["ln1_b"])).then_inc(ld_gb1, 16)
            for j in range(4):
                sp.wait_ge(t_full, CHUNK_NO["x", j + 4, 1] + 1)
                sp.wait_ge(st_h0[j], 32)
                sp.dma_start(hring[:, j, :], h0_d[j * P:(j + 1) * P, :]).then_inc(ld_h0[j], 16)
            sp.wait_ge(pj_full, 16)
            sp.wait_ge(kv_full, NT)
            sp.dma_start(tri[:, :], a["c_tri"]).then_inc(ld_late, 16)
            sp.dma_start(iotas[:, :], bcast(a["c_iotas"])).then_inc(ld_late, 16)
            sp.dma_start(rows[:, :, :, :], a["c_rows"].rearrange("p (j k f) -> p j k f", j=NT, k=TOP_K)).then_inc(ld_late, 16)
            sp.dma_start(route_b[:, 0:N_GROUPS], bcast(a["b_group"])).then_inc(ld_late, 16)
            sp.dma_start(route_b[:, N_GROUPS:ROUTE], bcast(a["b_expert"])).then_inc(ld_late, 16)
            sp.dma_start(w_route[:, :, 0:N_GROUPS], ktile(a["w_group"])).then_inc(ld_late, 16)
            sp.dma_start(w_route[:, :, N_GROUPS:ROUTE], ktile(a["w_expert"])).then_inc(ld_late, 16)
            sp.wait_ge(krot_ready, 1)
            sp.dma_start(alibi[:, :, :], a["c_alibi"].rearrange("p (h w) -> p h w", w=BAND)).then_inc(ld_alibi, 16)
            sp.wait_ge(pv_full, LAST_SOFT)
            sp.dma_start(w_o[:, 0:4, :], ktile(a["w_o"])[:, 0:4, :]).then_inc(ld_wo, 16)
            sp.dma_start(w_o[:, 4:8, :], ktile(a["w_o"])[:, 4:8, :]).then_inc(ld_wo, 16)
            sp.dma_start(w_mq[:, :, :], ktile(a["w_mq"])).then_inc(ld_wmq, 16)
            sp.dma_start(gb2[:, 0, :], bcast(a["ln2_g"])).then_inc(ld_gb2, 16)
            sp.dma_start(gb2[:, 1, :], bcast(a["ln2_b"])).then_inc(ld_gb2, 16)
            sp.dma_start(w_mo[:, :, :], ktile(a["w_mo"])).then_inc(ld_wmo, 16)
            for j in range(NT):
                s = j % 4
                sp.wait_ge(ln_done, LN_NO["E", j] + 1)
                sp.dma_start(h2_d[j * P:(j + 1) * P, :], hring[:, s, :]).then_inc(st_h2[s], 16)
                if j + 4 < NT:
                    sp.wait_ge(st_h2[s], 16)
                    sp.wait_ge(t_full, CHUNK_NO["h2", j, 1] + 1)
                    sp.dma_start(hring[:, s, :], h0_d[(j + 4) * P:(j + 5) * P, :]).then_inc(ld_h0[s], 16)
            sp.dma_start(gb1[:, 0, :], bcast(a["ln3_g"])).then_inc(ld_gb1, 16)
            sp.dma_start(gb1[:, 1, :], bcast(a["ln3_b"])).then_inc(ld_gb1, 16)
            sp.wait_ge(items_ready, 1)
            n_items = sp.value_load(n_items_t[0:1, 0:1], min_val=1, max_val=MAX_ITEMS)

            def load_weights(s, item, earlier):
                e = sp.value_load(item_exp[0:1, bass.ds(item, 1)], min_val=0, max_val=N_EXP - 1)
                gu = a["w_gate_up"][bass.ds(e, 1), :, :].rearrange("e (k p) n -> (e p) k n", p=P)
                dn = a["w_down"][bass.ds(e, 1), :, :].rearrange("e (k p) n -> (e p) k n", p=P)
                if earlier:
                    sp.wait_ge(gu_full, item - 1)
                for h in range(2):
                    sp.dma_start(w_gu[s][:, 4 * h:4 * h + 4, :], gu[:, 4 * h:4 * h + 4, :]).then_inc(gu_loaded[s][h], 16)
                if earlier:
                    sp.wait_ge(y_full, item * 2 - 2)
                sp.dma_start(w_dn[s][:, :, :], dn).then_inc(dn_loaded[s], 16)

            for s in range(2):
                load_weights(s, s, False)
            with sp.Fori(1, MAX_ITEMS // 2) as r:
                for s in range(2):
                    with sp.If(r * 2 + s < n_items):
                        load_weights(s, r * 2 + s, True)
            sp.wait_ge(rows_done, 1)
            for j in range(NT):
                if j < 4:
                    if j == 0:
                        for s in range(4):
                            sp.wait_ge(st_h2[s], 32)
                        sp.wait_ge(t_full, N_CHUNKS)
                else:
                    sp.wait_ge(st_out[j % 4], 16)
                sp.dma_start(hring[:, j % 4, :], h2_d[j * P:(j + 1) * P, :]).then_inc(ld_h2[j % 4], 16)
                if j >= 2:
                    sp.wait_ge(pair_free, j - 1)
                sp.dma_start(pair[j % 2][:, :, :], ye_d[j * 2 * P:(j + 1) * 2 * P, :].rearrange("(p k) d -> p k d", k=TOP_K)).then_inc(ld_pair[j % 2], 16)
                if j >= 2:
                    sp.wait_ge(ln_done, LN_NO["out", j - 2] + 1)
                    sp.dma_start(o[(j - 2) * P:(j - 1) * P, :], hring[:, (j - 2) % 4, :]).then_inc(st_out[(j - 2) % 4], 16)
            for j in range(NT - 2, NT):
                sp.wait_ge(ln_done, LN_NO["out", j] + 1)
                sp.dma_start(o[j * P:(j + 1) * P, :], hring[:, j % 4, :]).then_inc(st_out[j % 4], 16)
            for s in range(4):
                sp.wait_ge(st_out[s], 32)

        @block.gpsimd
        def _(pool):
            nc.gpsimd.memset(neghalf[:, :], -0.5).then_inc(pool_const, 1)
            nc.gpsimd.memset(sq[:, 2, 0:MAX_ITEMS * 4].bitcast(I32), NO_ROW).then_inc(pool_const, 1)
            nc.gpsimd.memset(one_col[:, :], 1.0).then_inc(pool_const, 1)
            pool.wait_ge(pool_const, 2)
            pool.dma_start(table_d[0:MAX_ITEMS * P, :].rearrange("(p r) f -> p (r f)", p=P), sq[:, 2, 0:MAX_ITEMS * 4].bitcast(I32)).then_inc(fill_done, 16)

            def rsqrt_of_variance(key):
                n = LN_NO[key]
                pool.wait_ge(var_ready, n + 1)
                nc.gpsimd.tensor_tensor(rstd[:, n:n + 1], var[:, n:n + 1], neghalf[:, 0:1], ALU.pow).then_inc(rstd_ready, 1)

            for j in range(NT):
                rsqrt_of_variance(("in", j))
            pool.wait_ge(ld_wup, 16 * 5)
            nc.gpsimd.tensor_scalar(gq[:, 0:2], gq[:, 0:2], QK ** -0.5, None, ALU.mult).then_inc(pool_const, 1)
            pool.wait_ge(pool_const, 4)
            nc.gpsimd.tensor_scalar(gq[:, 2:4], gq[:, 0:2], -1.0, None, ALU.mult).then_inc(pool_const, 1)
            pool.wait_ge(pool_const, 5)
            for k in range(2):
                nc.gpsimd.tensor_scalar(wq[:, k, :, 0:QK], wuq[:, k, :, :], gq[:, k:k + 1], None, ALU.mult)
                nc.gpsimd.tensor_scalar(wq[:, k, :, QK:QK + 16], wuq[:, k, :, NOPE + 16:QK], gq[:, 2 + k:3 + k], None, ALU.mult)
                nc.gpsimd.tensor_scalar(wq[:, k, :, QK + 16:P], wuq[:, k, :, NOPE:NOPE + 16], gq[:, k:k + 1], None, ALU.mult).then_inc(wq_ready, 1)
            nc.gpsimd.tensor_scalar(wukv[:, :, :, :], wukv[:, :, :, :], gkv[:, 0:1], None, ALU.mult).then_inc(wq_ready, 1)
            pool.wait_ge(wq_ready, 3)
            pool.wait_ge(fill_done, 16)
            pool.wait_ge(t_full, CHUNK_NO["mem", 1, 1] + 1)
            for hf in range(2):
                cols = slice(hf * HALF, (hf + 1) * HALF)
                for c in range(3):
                    pool.wait_ge(pj_free, hf * 8 + c + 1)
                    src = cq[:, c, cols] if c < 2 else ckv[:, cols]
                    nc.gpsimd.tensor_tensor(sq[:, c, cols], src, src, ALU.mult).then_inc(sq_ready, 1)
            pool.wait_ge(ms_ready, 1)
            nc.gpsimd.tensor_tensor(rms[:, :], ms[:, :], neghalf[:, :], ALU.pow).then_inc(rms_ready, 1)
            for c in range(2):
                n = CHUNK_NO["kpe", 0, c]
                pool.wait_ge(t_free[n % 2], n // 2 + 1)
            for h in range(1, MLA_HEADS):
                nc.gpsimd.tensor_copy(kcat[NOPE:QK, h, :], kcat[NOPE:QK, 0, :]).then_inc(kpe_all, 1)
            for key in PROJ_NO:
                rsqrt_of_variance(key)
            pool.wait_ge(pos_ready, 1)
            for j in range(NT):
                for k in range(TOP_K):
                    c = j * TOP_K + k
                    pool.indirect_dma_start(table_d, bass.IndirectOffsetOnAxis(ap=posi[:, j, k:k + 1], axis=0),
                                            rows[:, j, k, :], None, bounds_check=MAX_ITEMS * P - 1,
                                            oob_is_err=False).then_inc(table_done, 16)
            for s in range(2):
                nc.gpsimd.memset(xg[s][:, :], 0.0).then_inc(pool_const, 1)
            pool.wait_ge(pool_const, 7)
            pool.wait_ge(table_done, 16 * NT * TOP_K)
            for s in range(4):
                pool.wait_ge(st_h2[s], 32)
            pool.wait_ge(items_ready, 1)
            n_items = pool.value_load(n_items_t[0:1, 0:1], min_val=1, max_val=MAX_ITEMS)

            last_token, last_row = pool.to_reg(SEQ - 1), pool.to_reg(SEQ * TOP_K - 1)

            def gather(s, item, before):
                first = item * P if isinstance(item, int) else pool.snap(item * P)
                if not isinstance(before, int) or before:
                    pool.wait_ge(xT_ready[s], before)
                pool.dma_start(tab_x[s][:, :], table_d[bass.ds(first, P), :]).then_inc(tokens_loaded[s], 16)
                pool.wait_ge(tokens_loaded[s], (before + 1) * 16)
                pool.sem_inc(pool_ready, 1)
                pool.indirect_dma_start(xg[s][:, :], None, h2_d, bass.IndirectOffsetOnAxis(ap=tab_x[s][:, 0:1], axis=0),
                                        bounds_check=last_token, oob_is_err=False).then_inc(x_loaded[s], 16)

            def load_places(s, item, before):
                first = item * P if isinstance(item, int) else pool.snap(item * P)
                if not isinstance(before, int) or before:
                    pool.wait_ge(ye_stored[s], before * 16)
                pool.dma_start(tab_y[s][:, :], table_d[bass.ds(first, P), :]).then_inc(places_loaded[s], 16)

            def scatter(s, before):
                pool.wait_ge(places_loaded[s], (before + 1) * 16)
                pool.wait_ge(ye_ready[s], before + 1)
                pool.sem_inc(pool_ready, 1)
                pool.indirect_dma_start(ye_d, bass.IndirectOffsetOnAxis(ap=tab_y[s][:, 1:2], axis=0), ye[s][:, :], None,
                                        bounds_check=last_row, oob_is_err=False).then_inc(ye_stored[s], 16)

            gather(0, 0, 0)
            gather(1, 1, 0)
            load_places(0, 0, 0)
            for s in range(2):
                gather(s, s + 2, 1)
                load_places(1 - s, s + 1, s)
                scatter(s, 0)
            with pool.Fori(1, MAX_ITEMS // 2) as r:
                for s in range(2):
                    with pool.If(r * 2 + (s + 2) < n_items):
                        gather(s, r * 2 + (s + 2), r + 1)
                    with pool.If(r * 2 + (s + 1) < n_items):
                        load_places(1 - s, r * 2 + (s + 1), r + s)
                    with pool.If(r * 2 + s < n_items):
                        scatter(s, r)
            n0 = pool.snap((n_items + 1) // 2 * 16)
            n1 = pool.snap(n_items // 2 * 16)
            pool.wait_ge(ye_stored[0], n0)
            pool.wait_ge(ye_stored[1], n1)
            pool.sem_inc(rows_done, 1)
            for j in range(NT):
                rsqrt_of_variance(("out", j))

        @block.scalar
        def _(actq):
            actq.dma_start(ident[:, :], a["c_ident"]).then_inc(ld_ident, 16)
            actq.dma_start(gb1[:, 0, :], bcast(a["ln_in_g"])).then_inc(ld_gb1, 16)
            actq.dma_start(gb1[:, 1, :], bcast(a["ln_in_b"])).then_inc(ld_gb1, 16)
            actq.dma_start(wuq[:, :, :, :], a["w_uq"].rearrange("(k p) (h n) -> p k h n", p=P, n=QK)).then_inc(ld_wup, 16)
            for t in range(2):
                actq.dma_start(wukv[:, t, :, :], a["w_ukv"].rearrange("p (h t n) -> p t h n", t=2, n=NOPE)[:, t, :, :]).then_inc(ld_wup, 16)
            actq.dma_start(gq[:, 0:2], a["g_q"].rearrange("a (k p) -> p (a k)", p=P), allow_slow_non_contiguous=True).then_inc(ld_wup, 16)
            actq.dma_start(gkv[:, :], a["g_kv"].rearrange("a p -> p a"), allow_slow_non_contiguous=True).then_inc(ld_wup, 16)
            actq.dma_start(pos_all[NOPE:P, :], a["positions"].to_broadcast([P - NOPE, SEQ])).then_inc(ld_pos, 16)
            actq.dma_start(pos_t[:, :], a["positions"].rearrange("a (j p) -> p (a j)", p=P), allow_slow_non_contiguous=True).then_inc(ld_pos, 16)
            actq.dma_start(rope_f[:, :], a["c_rope"]).then_inc(ld_pos, 16)
            actq.dma_start(inv_b[:, :], bcast(a["c_inv"])).then_inc(ld_pos, 16)
            for r in range(2):
                actq.dma_start(sink[:, r, :], bcast(a["sinks"])).then_inc(ld_small, 16)

            def evac(key, dst, src_cols=None):
                n = CHUNK_NO[key]
                actq.wait_ge(t_full, n + 1)
                src = psT[:, n % 2, :] if src_cols is None else src_cols(psT[:, n % 2, :])
                nc.scalar.copy(dst, src).then_inc(t_free[n % 2], 1)

            four = lambda v: v.rearrange("p (k n) -> p k n", n=P)
            for t in range(2):
                for c in range(2):
                    evac(("mem", t, c), memT[:, 4 * c:4 * c + 4, t * P:(t + 1) * P], four)
            for i in range(4):
                actq.wait_ge(mem_full, i + 1)
                dst = kmT[:, 2 * i:2 * i + 2, :] if i < 2 else vm[:, i - 2, :]
                src = bank(2 + i).rearrange("p (h n) -> p h n", h=2) if i < 2 else bank(2 + i)
                nc.scalar.copy(dst, src).then_inc(mem_free, 1)
            for hf in range(2):
                for j in range(4 * hf, 4 * hf + 4):
                    for c in range(2):
                        evac(("x", j, c), hT[:, 4 * c:4 * c + 4, j * P:(j + 1) * P], four)
                cols = slice(hf * HALF, (hf + 1) * HALF)
                for c in range(8):
                    i = hf * 8 + c
                    actq.wait_ge(pj_full, i + 1)
                    src = bank(2 + i % 4)
                    if c < 3:
                        nc.scalar.copy(cq[:, c, cols] if c < 2 else ckv[:, cols], src).then_inc(pj_free, 1)
                    elif c < 7:
                        g = (c - 3) // 2 * SWA_DIM
                        for b in range(2):
                            ins = nc.scalar.mul(qs[g:g + SWA_DIM, (2 * (c - 3) + b) % GQ, cols],
                                                src[b * SWA_DIM:(b + 1) * SWA_DIM, :], SWA_DIM ** -0.5)
                        ins.then_inc(pj_free, 1)
                    else:
                        nc.scalar.copy(ks[:, cols], src).then_inc(pj_free, 1)
                for j in range(4 * hf, 4 * hf + 4):
                    actq.wait_ge(kv_full, j + 1)
                    nc.scalar.copy(krvs[:, j, :], bank(6 + j % 2)[:, 0:ROPE + P]).then_inc(kv_free, 1)
            actq.wait_ge(trig_ready, 1)
            nc.scalar.activation(cs[NOPE:P, :], cs[NOPE:P, :], ACT.Sin).then_inc(trig_done, 1)
            actq.wait_ge(trig_ready, 2)
            nc.scalar.activation(kang[:, :, :, :], kang[:, :, :, :], ACT.Sin).then_inc(trig_done, 1)
            for i in range(8):
                p, hf = i // 2, i % 2
                actq.wait_ge(kn_full, i + 1)
                cols = slice(hf * HALF, (hf + 1) * HALF)
                nc.scalar.copy(kcat[0:NOPE, 2 * p, cols], bank(6 + i % 2)[0:NOPE, :])
                nc.scalar.copy(kcat[0:NOPE, 2 * p + 1, cols], bank(6 + i % 2)[NOPE:P, :]).then_inc(kn_free, 1)
            for c in range(2):
                n = CHUNK_NO["kpe", 0, c]
                actq.wait_ge(t_full, n + 1)
                nc.scalar.copy(kcat[NOPE:QK, 0, c * HALF:(c + 1) * HALF], psT[0:ROPE, n % 2, :]).then_inc(t_free[n % 2], 1)

            def softmax(u):
                kind, j, h = u
                n = N_SCORE[u]
                if kind == "q":
                    for c in range(2):
                        actq.wait_ge(rope_read, 2 * j + c + 1)
                        ins = nc.scalar.copy(qcat[0:NOPE, j % 2, 4 * c:4 * c + 4, :], four(psS[0:NOPE, n % 2, c * 512:(c + 1) * 512]))
                    ins.then_inc(s_free[n % 2], 1)
                    return
                m = N_SOFT[u]
                actq.wait_ge(mx_ready, m + 1)
                if m >= 2:
                    prev = SOFTMAXED[m - 2]
                    actq.wait_ge(t_full, CHUNK_NO[prev, chunks_of(prev) - 1] + 1)
                if kind == "m":
                    w = (j + 1) * P
                    nc.scalar.activation(prob[:, m % 2, 0:w], psS[:, n % 2, 0:w], ACT.Exp, bias=neg_max[:, m % 4, 0:1],
                                         accum_out=sums_m[:, j % 2, h:h + 1]).then_inc(s_free[n % 2], 1)
                else:
                    lo = CHUNK if j == 0 else 0
                    for i in range(GQ):
                        p = prob[:, m % 2, i * BAND + lo:(i + 1) * BAND]
                        nc.scalar.activation(p, p, ACT.Exp, bias=neg_max[:, m % 4, i:i + 1],
                                             accum_out=sums_s[:, j % 2, h * GQ + i:h * GQ + i + 1])
                    nc.scalar.activation(sink_e[:, j % 2, h * GQ:(h + 1) * GQ], sink_d[:, j % 2, h * GQ:(h + 1) * GQ],
                                         ACT.Exp).then_inc(p_ready, 1)

            def evac_odd(u):
                kind, j, h = u
                for c in range(chunks_of(u)):
                    n = CHUNK_NO[u, c]
                    if n % 2 == 0:
                        continue
                    m = N_SOFT.get(u)
                    if m is not None and m >= 2:
                        actq.wait_ge(pv_full, m - 1)
                    evac_attention(actq, nc.scalar.copy, u, c)

            def evac_attention(eng, copy, u, c):
                kind, j, h = u
                n = CHUNK_NO[u, c]
                m = N_SOFT.get(u)
                eng.wait_ge(t_full, n + 1)
                src = psT[:, n % 2, :]
                if kind == "m":
                    k = min(4, j + 1 - 4 * c)
                    copy(probT[:, m % 2, 4 * c:4 * c + k, :], four(src)[:, 0:k, :]).then_inc(t_free[n % 2], 1)
                elif kind == "s" and c == 0:
                    copy(probT[:, m % 2, 0:4, :], four(src)).then_inc(t_free[n % 2], 1)
                elif kind == "s":
                    copy(probT[CHUNK:P, m % 2, 4:8, :], four(src)[0:CHUNK, :, :]).then_inc(t_free[n % 2], 1)
                else:
                    copy(yT[:, 4 * c:4 * c + 4, j * P:(j + 1) * P], four(src)).then_inc(t_free[n % 2], 1)

            actq.wait_ge(ld_small, 32)
            for t in range(len(UNITS) + 1):
                if t < len(UNITS) and UNITS[t] in N_SCORE:
                    softmax(UNITS[t])
                if t:
                    evac_odd(UNITS[t - 1])

            for s in range(NT + 3):
                j = s - 2
                if 0 <= j < NT:
                    for c in range(2):
                        evac(("p8", j, c), probT[:, 0, 4 * c:4 * c + 4, :], four)
                j = s - 1
                if 0 <= j < NT:
                    for c in range(2):
                        evac(("h1", j, c), h1T[:, j % 2, 4 * c:4 * c + 4, :], four)
                    actq.wait_ge(qm_full, j + 1)
                    nc.scalar.mul(qm[:, :, :], four(psM[:, :]), MEM_DIM ** -0.5).then_inc(qm_ready, 1)
                j = s - 2
                if 0 <= j < NT:
                    evac(("o8", j, 0), omT[:, :, :], four)
                j = s - 1
                if 0 <= j < NT:
                    actq.wait_ge(nm8_ready, j + 1)
                    for h in range(MEM_HEADS):
                        ins = nc.scalar.activation(prob[:, 0, h * N_MEM:(h + 1) * N_MEM], psS[:, 0, h * N_MEM:(h + 1) * N_MEM], ACT.Exp,
                                                   bias=neg_max[:, j % 2, h:h + 1], accum_out=sums_x[:, h:h + 1])
                    ins.then_inc(p8_ready, 1)
                j = s - 3
                if 0 <= j < NT:
                    for c in range(2):
                        evac(("h2", j, c), h2T[:, 4 * c:4 * c + 4, :], four)
                    actq.wait_ge(r_full, j + 1)
                    nc.scalar.copy(logits[:, j, :], psN[:, 0:ROUTE]).then_inc(r_ready, 1)
            actq.wait_ge(g_exp_in, 1)
            nc.scalar.activation(eg[:, :, :], gl[:, :, :], ACT.Exp).then_inc(g_exp_out, 1)
            actq.wait_ge(g_exp_in, 2)
            nc.scalar.activation(t8[3][:, :], t8[2][:, :], ACT.Exp).then_inc(g_exp_out, 1)
            actq.wait_ge(items_ready, 1)
            n_items = actq.value_load(n_items_t[0:1, 0:1], min_val=1, max_val=MAX_ITEMS)

            def evac_x(s, count):
                actq.wait_ge(xT_full[s], count * 2 - 1)
                nc.scalar.copy(xgT[s][:, 0:4, :], four(psT[:, 0, :]))
                actq.wait_ge(xT_full[s], count * 2)
                nc.scalar.copy(xgT[s][:, 4:8, :], four(psT[:, 1, :])).then_inc(xT_ready[s], 1)

            evac_x(0, 1)
            with actq.Fori(0, MAX_ITEMS // 2) as r:
                for s in range(2):
                    i = r * 2 + s
                    with actq.If(i < n_items):
                        actq.wait_ge(gu_full, i + 1)
                        nc.scalar.activation(gate_s[:, :], bank(2), ACT.Silu).then_inc(silu_done, 1)
                    with actq.If(i + 1 < n_items):
                        evac_x(1 - s, r + (1 + s))
                    with actq.If(i < n_items):
                        actq.wait_ge(aT_full, i + 1)
                        nc.scalar.copy(actT[s][:, :, :], four(psM[:, :])).then_inc(aT_ready, 1)

        @block.vector
        def _(dve):
            settled = [0]

            def settle(ins):
                settled[0] += 1
                ins.then_inc(v_done, 1)
                dve.wait_ge(v_done, settled[0])

            V = nc.vector
            four = lambda v: v.rearrange("p (k n) -> p k n", n=P)

            def layer_norm(key, t, gb):
                n = LN_NO[key]
                r = n % 2
                V.bn_stats(stats[:, r, 0, :], t[:, 0:512])
                settle(V.bn_stats(stats[:, r, 1, :], t[:, 512:D]))
                settle(V.bn_aggr(mv[:, r, :], stats[:, r, :, :]))
                V.tensor_scalar(var[:, n:n + 1], mv[:, r, 1:2], LN_EPS, None, ALU.add).then_inc(var_ready, 1)
                settle(V.scalar_tensor_tensor(t, t, mv[:, r, 0:1], gb[:, 0, :], ALU.subtract, ALU.mult))
                dve.wait_ge(rstd_ready, n + 1)
                V.scalar_tensor_tensor(t, t, rstd[:, n:n + 1], gb[:, 1, :], ALU.mult, ALU.add).then_inc(ln_done, 1)

            def reduce_angle(ang, t, turns, phase):
                settle(V.tensor_scalar(t, ang, 1 / (2 * np.pi), turns, ALU.mult, ALU.add))
                settle(V.tensor_scalar(t, t, ROUNDER, None, ALU.add))
                settle(V.tensor_scalar(t, t, ROUNDER, None, ALU.subtract))
                for part in (TWO_PI_1, TWO_PI_2, TWO_PI_3):
                    settle(V.scalar_tensor_tensor(ang, t, -part, ang, ALU.mult, ALU.add))
                settle(V.tensor_scalar(ang, ang, phase, 3.1415925, ALU.add, ALU.min))
                return V.tensor_scalar(ang, ang, -3.1415925, None, ALU.max)

            dve.wait_ge(ld_gb1, 32)
            for j in range(NT):
                dve.wait_ge(ld_x[j % 4], 16 * (j // 4 + 1))
                layer_norm(("in", j), hring[:, j % 4, :], gb1)
            dve.wait_ge(ld_pos, 64)
            lo = slice(NOPE, P)
            settle(V.tensor_scalar(cs[lo, :], pos_all[lo, :], rope_f[lo, 0:1], None, ALU.mult))
            reduce_angle(cs[lo, :], trig_t[lo, :], rope_f[lo, 1:2], rope_f[lo, 2:3]).then_inc(trig_ready, 1)
            settle(V.tensor_copy(posf_t[:, :], pos_t[:, :]))
            for c, (turns, phase) in enumerate(((0.25, np.pi / 2), (0.0, 0.0))):
                settle(V.tensor_tensor(kang[:, c, :, :], posf_t[:, :].unsqueeze(2).to_broadcast([P, NT, 16]),
                                       inv_b[:, :].unsqueeze(1).to_broadcast([P, NT, 16]), ALU.mult))
                last = reduce_angle(kang[:, c, :, :], kang_t[:, :, :], turns, phase)
            last.then_inc(trig_ready, 1)
            dve.wait_ge(ss_full, 1)
            V.tensor_scalar(ms[:, 0:8], bank(2)[:, 0:8], 1.0 / Q_LORA, RMS_EPS, ALU.mult, ALU.add)
            V.tensor_scalar(ms[:, 8:16], bank(2)[:, 8:16], 1.0 / KV_LORA, RMS_EPS, ALU.mult, ALU.add).then_inc(ms_ready, 1)
            for hf in range(2):
                cols = slice(hf * HALF, (hf + 1) * HALF)
                dve.wait_ge(rb_full, 2 * hf + 1)
                for c in range(2):
                    V.tensor_tensor(cq[:, c, cols], cq[:, c, cols], bank(2 + 2 * hf), ALU.mult).then_inc(cqn_ready, 1)
                dve.wait_ge(rb_full, 2 * hf + 2)
                V.tensor_tensor(ckv[:, cols], ckv[:, cols], bank(3 + 2 * hf), ALU.mult).then_inc(cqn_ready, 1)
            dve.wait_ge(trig_done, 2)
            dve.wait_ge(kv_free, NT)
            x1, x2 = krvs[:, :, 0:16], krvs[:, :, 16:ROPE]
            V.tensor_tensor(krot[:, :, 0:16], x1, kang[:, 0, :, :], ALU.mult)
            settle(V.tensor_tensor(krot_t[:, :, :], x2, kang[:, 1, :, :], ALU.mult))
            settle(V.tensor_tensor(krot[:, :, 0:16], krot[:, :, 0:16], krot_t[:, :, :], ALU.subtract))
            V.tensor_tensor(krot[:, :, 16:ROPE], x1, kang[:, 1, :, :], ALU.mult)
            settle(V.tensor_tensor(krot_t[:, :, :], x2, kang[:, 0, :, :], ALU.mult))
            V.tensor_tensor(krot[:, :, 16:ROPE], krot[:, :, 16:ROPE], krot_t[:, :, :], ALU.add).then_inc(krot_ready, 1)
            for j in range(NT):
                dve.wait_ge(vv_full, j + 1)
                V.tensor_copy(vmla[:, j, :], bank(2 + j % 4)).then_inc(vv_free, 1)

            def scores(u):
                kind, j, h = u
                n = N_SCORE[u]
                dve.wait_ge(s_full, n + 1)
                if kind == "q":
                    cos, sin = (cs[x, j * P:(j + 1) * P].unsqueeze(1).to_broadcast([ROPE, 4, P]) for x in (slice(NOPE, QK), slice(QK, P)))
                    for c in range(2):
                        ps = psS[:, n % 2, c * 512:(c + 1) * 512]
                        dst = qcat[NOPE:QK, j % 2, 4 * c:4 * c + 4, :]
                        V.tensor_tensor(dst, four(ps[NOPE:QK, :]), cos, ALU.mult)
                        settle(V.tensor_tensor(four(ps[QK:P, :]), four(ps[QK:P, :]), sin, ALU.mult))
                        V.tensor_tensor(dst, dst, four(ps[QK:P, :]), ALU.add).then_inc(rope_read, 1)
                    return
                m = N_SOFT[u]
                if kind == "m":
                    w = (j + 1) * P
                    settle(V.memset(psS[0:CHUNK, n % 2, w - CHUNK:w], MASKED))
                    V.tensor_reduce(neg_max[:, m % 4, 0:1], psS[:, n % 2, 0:w], X, ALU.max, negate=True).then_inc(mx_ready, 1)
                    return
                lo = CHUNK if j == 0 else 0
                if m >= 2:
                    prev = SOFTMAXED[m - 2]
                    dve.wait_ge(t_full, CHUNK_NO[prev, chunks_of(prev) - 1] + 1)
                biased = prob[:, m % 2, 0:GQ * BAND].rearrange("p (h w) -> p h w", w=BAND)[:, :, lo:BAND]
                raw = psS[:, n % 2, :].rearrange("p (h w) -> p h w", w=256)[:, :, lo:BAND]
                V.tensor_tensor(biased, raw, alibi[:, h * GQ:(h + 1) * GQ, lo:BAND], ALU.add).then_inc(s_free[n % 2], 1)
                dve.wait_ge(s_free[n % 2], n // 2 + 1)
                hs = slice(h * GQ, (h + 1) * GQ)
                settle(V.tensor_reduce(rmax[:, 0:GQ], biased, X, ALU.max))
                settle(V.tensor_tensor(rmax[:, 0:GQ], rmax[:, 0:GQ], sink[:, j % 2, hs], ALU.max))
                settle(V.tensor_tensor(sink_d[:, j % 2, hs], sink[:, j % 2, hs], rmax[:, 0:GQ], ALU.subtract))
                V.tensor_scalar(neg_max[:, m % 4, :], rmax[:, 0:GQ], -1.0, None, ALU.mult).then_inc(mx_ready, 1)

            def evac_even(u):
                kind, j, h = u
                for c in range(chunks_of(u)):
                    n = CHUNK_NO[u, c]
                    if n % 2:
                        continue
                    m = N_SOFT.get(u)
                    if m is not None and m >= 2:
                        dve.wait_ge(pv_full, m - 1)
                    dve.wait_ge(t_full, n + 1)
                    src = four(psT[:, n % 2, :])
                    if kind == "m":
                        k = min(4, j + 1 - 4 * c)
                        ins = V.tensor_copy(probT[:, m % 2, 4 * c:4 * c + k, :], src[:, 0:k, :])
                    elif kind == "s" and c == 0:
                        ins = V.tensor_copy(probT[:, m % 2, 0:4, :], src)
                    elif kind == "s":
                        ins = V.tensor_copy(probT[CHUNK:P, m % 2, 4:8, :], src[0:CHUNK, :, :])
                    else:
                        ins = V.tensor_copy(yT[:, 4 * c:4 * c + 4, j * P:(j + 1) * P], src)
                    ins.then_inc(t_free[n % 2], 1)

            def divide(u):
                kind, j, h = u
                heads = lambda v: v.rearrange("p (h d) -> p h d", d=NOPE)
                rb = rinv[:, :].unsqueeze(2).to_broadcast([P, 8, NOPE])
                dve.wait_ge(pv_full, N_SOFT[u] + 1)
                if kind == "m" and h == MLA_HEADS - 1:
                    if j:
                        dve.wait_ge(t_full, CHUNK_NO[("y", j - 1, 0), 1] + 1)
                    settle(V.reciprocal(rinv[:, :], sums_m[:, j % 2, :]))
                    settle(V.tensor_tensor(heads(y[:, 0:512]), heads(psM[:, :]), rb, ALU.mult))
                elif kind == "s" and h == 1:
                    dve.wait_ge(p_ready, 2 * j + 2)
                    settle(V.tensor_tensor(rinv[:, :], sums_s[:, j % 2, :], sink_e[:, j % 2, :], ALU.add))
                    settle(V.reciprocal(rinv[:, :], rinv[:, :]))
                    V.tensor_tensor(heads(y[:, 512:D]), heads(psN[:, :]), rb, ALU.mult).then_inc(y_ready, 1)
                    dve.wait_ge(y_ready, j + 1)

            dve.wait_ge(ld_alibi, 16)
            dve.wait_ge(ld_small, 32)
            for t in range(len(UNITS) + 2):
                if t < len(UNITS) and UNITS[t] in N_SCORE:
                    scores(UNITS[t])
                if 0 < t <= len(UNITS):
                    evac_even(UNITS[t - 1])
                if t >= 2 and UNITS[t - 2][0] in "ms" and UNITS[t - 2][2] == (7 if UNITS[t - 2][0] == "m" else 1):
                    divide(UNITS[t - 2])

            def residual(key, gb):
                n, j = PROJ_NO[key], key[1]
                h = hring[:, j % 4, :]
                for c in range(2):
                    dve.wait_ge(ae_full, 2 * n + c + 1)
                    ins = V.scalar_tensor_tensor(h[:, c * 512:(c + 1) * 512], h[:, c * 512:(c + 1) * 512], ALPHA,
                                                 bank(4 + c), ALU.mult, ALU.add)
                ins.then_inc(ae_free, 1)
                dve.wait_ge(ae_free, n + 1)
                layer_norm(key, h, gb)

            V.memset(ones[:, :], 1.0)
            dve.wait_ge(ld_gb1, 64)
            for s in range(NT + 3):
                if s < NT:
                    dve.wait_ge(ld_h0[s % 4], 16 * (s // 4 + 1))
                    residual(("A", s), gb1)
                j = s - 2
                if 0 <= j < NT:
                    dve.wait_ge(o8_full, j + 1)
                    settle(V.reciprocal(rinv[:, 0:4], sums_x[:, :]))
                    V.tensor_tensor(four(om[:, :]), four(psN[:, :]), rinv[:, 0:4].unsqueeze(2).to_broadcast([P, 4, P]),
                                    ALU.mult).then_inc(om_ready, 1)
                    dve.wait_ge(om_ready, j + 1)
                j = s - 1
                if 0 <= j < NT:
                    dve.wait_ge(c_full, j + 1)
                    V.tensor_reduce(neg_max[:, j % 2, :], psS[:, 0, :].rearrange("p (h w) -> p h w", w=N_MEM), X, ALU.max,
                                    negate=True).then_inc(nm8_ready, 1)
                j = s - 2
                if 0 <= j < NT:
                    if j == 0:
                        dve.wait_ge(ld_gb2, 32)
                    residual(("E", j), gb2)

            dve.wait_ge(r_ready, NT)
            dve.wait_ge(ld_late, 16 * 7)
            over = lambda v, n: v.unsqueeze(2).to_broadcast([P, NT, n])
            ids = lambda n: iotas[:, 0:n].unsqueeze(1).to_broadcast([P, NT, n])
            settle(V.tensor_tensor(logits[:, :, :], logits[:, :, :], route_b[:, :].unsqueeze(1).to_broadcast([P, NT, ROUTE]), ALU.add))
            gmax, gid, behind, second_e, gprob, share = t8[0], t8[1], t8[2], t8[3], t8[8], t8[9]
            lg, le = logits[:, :, 0:N_GROUPS], logits[:, :, N_GROUPS:ROUTE]
            settle(V.tensor_reduce(gmax[:, :], lg, X, ALU.max))
            V.tensor_tensor(gl[:, :, :], lg, over(gmax[:, :], N_GROUPS), ALU.subtract).then_inc(g_exp_in, 1)

            def first_at(out, values, top, n, tmp, idx):
                settle(V.tensor_tensor(tmp, values, over(top, n), ALU.is_equal))
                settle(V.tensor_tensor(tmp, tmp, ids(n), ALU.mult))
                settle(V.tensor_reduce(idx, tmp, X, ALU.min))
                settle(V.tensor_tensor(out, ids(n), over(idx, n), ALU.is_equal))

            first_at(gpen[:, :, :], lg, gmax[:, :], N_GROUPS, gpen[:, :, :], gid[:, :])
            settle(V.tensor_scalar(gpen[:, :, :], gpen[:, :, :], 1.0, -MASKED, ALU.subtract, ALU.mult))
            for g in range(N_GROUPS):
                x = slice(g * PER_GROUP, (g + 1) * PER_GROUP)
                last = V.tensor_tensor(elm[:, :, x], le[:, :, x], gpen[:, :, g:g + 1].to_broadcast([P, NT, PER_GROUP]), ALU.add)
            settle(last)
            m1, i1, m2, i2 = t8[4], t8[5], t8[6], t8[7]
            settle(V.tensor_reduce(m1[:, :], elm[:, :, :], X, ALU.max))
            first_at(oh1[:, :, :], elm[:, :, :], m1[:, :], N_EXP, eqx[:, :, :], i1[:, :])
            settle(V.scalar_tensor_tensor(elm[:, :, :], oh1[:, :, :], 100 * MASKED, elm[:, :, :], ALU.mult, ALU.add))
            settle(V.tensor_reduce(m2[:, :], elm[:, :, :], X, ALU.max))
            first_at(oh2[:, :, :], elm[:, :, :], m2[:, :], N_EXP, eqx[:, :, :], i2[:, :])
            V.tensor_tensor(oh_sum[:, :, :], oh1[:, :, :], oh2[:, :, :], ALU.add).then_inc(oh_ready, 1)
            dve.wait_ge(g_exp_out, 1)
            V.tensor_tensor(behind[:, :], m2[:, :], m1[:, :], ALU.subtract).then_inc(g_exp_in, 1)
            settle(V.tensor_reduce(gprob[:, :], eg[:, :, :], X, ALU.add))
            settle(V.reciprocal(gprob[:, :], gprob[:, :]))
            dve.wait_ge(g_exp_out, 2)
            settle(V.tensor_scalar(share[:, :], second_e[:, :], 1.0, None, ALU.add))
            settle(V.reciprocal(share[:, :], share[:, :]))
            settle(V.tensor_tensor(gprob[:, :], gprob[:, :], share[:, :], ALU.mult))
            gates = rows[:, :, :, :].bitcast(F32)
            V.tensor_copy(gates[:, :, 0, 2], gprob[:, :])
            V.tensor_tensor(gates[:, :, 1, 2], gprob[:, :], second_e[:, :], ALU.mult)
            dve.wait_ge(rank_full, 2)
            V.tensor_copy(rank[:, :, :], bank(2)[:, 0:NT * N_EXP].rearrange("p (j e) -> p j e", e=N_EXP))
            settle(V.tensor_copy(tot[:, :, :], bank(3)[:, 0:NT * N_EXP].rearrange("p (j e) -> p j e", e=N_EXP)))
            settle(V.tensor_reduce(cnt[:, :], tot[:, :, :].rearrange("p j e -> p e j"), X, ALU.add))
            settle(V.tensor_scalar(nblk[:, :], cnt[:, :], 0.0, None, ALU.is_gt))
            for k in range(1, SEQ // P):
                settle(V.scalar_tensor_tensor(nblk[:, :], cnt[:, :], float(P * k), nblk[:, :], ALU.is_gt, ALU.add))
            settle(V.tensor_tensor_scan(incl[:, :], ones[:, 0:N_EXP], nblk[:, :], 0.0, ALU.mult, ALU.add))
            settle(V.tensor_tensor(cnt[:, :], incl[:, :], nblk[:, :], ALU.subtract))
            settle(V.tensor_scalar(place[:, 0, :], cnt[:, :], float(P), None, ALU.mult))
            for j in range(1, NT):
                settle(V.tensor_tensor(place[:, j, :], place[:, j - 1, :], tot[:, j - 1, :], ALU.add))
            settle(V.tensor_tensor(place[:, :, :], place[:, :, :], rank[:, :, :], ALU.add))
            for k, oh in enumerate((oh1, oh2)):
                settle(V.tensor_tensor(oh[:, :, :], oh[:, :, :], place[:, :, :], ALU.mult))
                settle(V.tensor_reduce(posf[:, :, k], oh[:, :, :], X, ALU.add))
            V.tensor_copy(posi[:, :, :], posf[:, :, :]).then_inc(pos_ready, 1)
            settle(V.tensor_tensor(item_cmp[:, :, :], incl[0:1, :].unsqueeze(1).to_broadcast([1, MAX_ITEMS, N_EXP]),
                                   iotas[0:1, N_EXP:].unsqueeze(2).to_broadcast([1, MAX_ITEMS, N_EXP]), ALU.is_le))
            settle(V.tensor_reduce(item_f[:, :], item_cmp[:, :, :], X, ALU.add))
            settle(V.tensor_scalar(item_exp[:, :], item_f[:, :], float(N_EXP - 1), None, ALU.min))
            V.tensor_copy(n_items_t[:, :], incl[0:1, N_EXP - 1:N_EXP]).then_inc(items_ready, 1)

            dve.wait_ge(items_ready, 1)
            n_items = dve.value_load(n_items_t[0:1, 0:1], min_val=1, max_val=MAX_ITEMS)

            def item_results(s, i, before):
                dve.wait_ge(silu_done, i + 1)
                V.tensor_tensor(act[s][:, :], gate_s[:, :], bank(3), ALU.mult).then_inc(act_ready, 1)
                if not isinstance(before, int):
                    dve.wait_ge(ye_stored[s], before * 16)
                gate = tab_y[s][:, 2:3].bitcast(F32)
                dve.wait_ge(places_loaded[s], (before + 1) * 16)
                dve.wait_ge(y_full, i * 2 + 1)
                V.tensor_scalar(ye[s][:, 0:512], bank(4), gate, None, ALU.mult)
                dve.wait_ge(y_full, i * 2 + 2)
                V.tensor_scalar(ye[s][:, 512:D], bank(5), gate, None, ALU.mult).then_inc(ye_ready[s], 1)

            for s in range(2):
                item_results(s, s, 0)
            with dve.Fori(1, MAX_ITEMS // 2) as r:
                for s in range(2):
                    with dve.If(r * 2 + s < n_items):
                        item_results(s, r * 2 + s, r)
            dve.wait_ge(ld_gb1, 96)
            for j in range(NT):
                h = hring[:, j % 4, :]
                dve.wait_ge(ld_h2[j % 4], 16 * (j // 4 + 1))
                dve.wait_ge(ld_pair[j % 2], 16 * (j // 2 + 1))
                settle(V.scalar_tensor_tensor(h, h, ALPHA, pair[j % 2][:, 0, :], ALU.mult, ALU.add))
                V.tensor_tensor(h, h, pair[j % 2][:, 1, :], ALU.add).then_inc(pair_free, 1)
                dve.wait_ge(pair_free, j + 1)
                layer_norm(("out", j), h, gb1)

        @block.tensor
        def _(pe):
            mm = nc.tensor.matmul
            T = nc.tensor.transpose

            def transposes(key, blocks, rows_out=P):
                n = CHUNK_NO[key]
                if n >= 2:
                    pe.wait_ge(t_free[n % 2], n // 2)
                for i, b in enumerate(blocks):
                    ins = T(psT[0:rows_out, n % 2, i * P:(i + 1) * P], b, ident[:, :])
                ins.then_inc(t_full, 1)

            def evacuated(key):
                n = CHUNK_NO[key]
                pe.wait_ge(t_free[n % 2], n // 2 + 1)

            pe.wait_ge(ld_ident, 16)
            pe.wait_ge(ld_mem, 16)
            for t in range(2):
                for c in range(2):
                    transposes(("mem", t, c), [mem_sb[:, t, (4 * c + i) * P:(4 * c + i + 1) * P] for i in range(4)])
            pe.wait_ge(ld_mk, 16)
            for b in range(2):
                pe.wait_ge(t_free[b], 2)
            for i in range(2):
                for hh in range(2):
                    h = 2 * i + hh
                    for k in range(KC):
                        ins = mm(bank(2 + i)[:, hh * N_MEM:(hh + 1) * N_MEM], w_mk[:, k, h * P:(h + 1) * P], memT[:, k, :],
                                 start=(k == 0), stop=(k == KC - 1))
                ins.then_inc(mem_full, 1)
            pe.wait_ge(ld_mv, 16)
            for t in range(2):
                for k in range(KC):
                    ins = mm(bank(4 + t), memT[:, k, t * P:(t + 1) * P], w_mv[:, k, :], start=(k == 0), stop=(k == KC - 1))
                ins.then_inc(mem_full, 1)
            for hf in range(2):
                for j in range(4 * hf, 4 * hf + 4):
                    pe.wait_ge(ln_done, LN_NO["in", j] + 1)
                    for c in range(2):
                        transposes(("x", j, c), [hring[:, j % 4, (4 * c + i) * P:(4 * c + i + 1) * P] for i in range(4)])
                for c in range(2):
                    n = CHUNK_NO["x", 4 * hf + 3, c]
                    pe.wait_ge(t_free[n % 2], n // 2 + 1)
                if hf == 0:
                    pe.wait_ge(ld_win, 64)
                cols = slice(hf * HALF, (hf + 1) * HALF)
                for c in range(8):
                    i = hf * 8 + c
                    if i < 4:
                        pe.wait_ge(mem_free, i + 1)
                    else:
                        pe.wait_ge(pj_free, i - 3)
                    for k in range(KC):
                        ins = mm(bank(2 + i % 4), w_in[:, k, c * P:(c + 1) * P], hT[:, k, cols], start=(k == 0), stop=(k == KC - 1))
                    ins.then_inc(pj_full, 1)
                for j in range(4 * hf, 4 * hf + 4):
                    if j >= 2:
                        pe.wait_ge(kv_free, j - 1)
                    for k in range(KC):
                        ins = mm(bank(6 + j % 2)[:, 0:ROPE + P], hT[:, k, j * P:(j + 1) * P], w_in[:, k, C_KR:IN_COLS],
                                 start=(k == 0), stop=(k == KC - 1))
                    ins.then_inc(kv_full, 1)
            pe.wait_ge(sq_ready, 6)
            pe.wait_ge(pj_free, 16)
            pe.wait_ge(pool_const, 3)
            for j in range(NT):
                tok = slice(j * P, (j + 1) * P)
                for c in range(2):
                    mm(bank(2)[:, j:j + 1], sq[:, c, tok], one_col[:, :], start=(c == 0), stop=(c == 1))
            for j in range(NT):
                ins = mm(bank(2)[:, 8 + j:9 + j], sq[:, 2, j * P:(j + 1) * P], one_col[:, :], start=True, stop=True)
            ins.then_inc(ss_full, 1)
            pe.wait_ge(rms_ready, 1)
            for hf in range(2):
                for kv in range(2):
                    for i in range(4):
                        c = kv * 8 + hf * 4 + i
                        ins = mm(bank(2 + 2 * hf + kv)[:, i * P:(i + 1) * P], rms[:, c:c + 1].to_broadcast([P, P]), ident[:, :],
                                 start=True, stop=True)
                    ins.then_inc(rb_full, 1)
            pe.wait_ge(wq_ready, 3)
            pe.wait_ge(kv_free, NT)
            pe.wait_ge(cqn_ready, 6)
            for i in range(8):
                p, hf = i // 2, i % 2
                if i >= 2:
                    pe.wait_ge(kn_free, i - 1)
                mm(bank(6 + i % 2), wukv[:, 0, 2 * p:2 * p + 2, :].rearrange("p h n -> p (h n)"), ckv[:, hf * HALF:(hf + 1) * HALF],
                   start=True, stop=True).then_inc(kn_full, 1)
            for j in range(NT):
                if j >= 4:
                    pe.wait_ge(vv_free, j - 3)
                mm(bank(2 + j % 4), ckv[:, j * P:(j + 1) * P], wukv[:, 1, :, :].rearrange("p h n -> p (h n)"), start=True, stop=True).then_inc(vv_full, 1)
            pe.wait_ge(krot_ready, 1)
            for c in range(2):
                transposes(("kpe", 0, c), [krot[:, 4 * c + i, :] for i in range(4)], rows_out=ROPE)
            pe.wait_ge(vv_free, NT)
            pe.wait_ge(kn_free, 8)
            for c in range(2):
                evacuated(("kpe", 0, c))

            def score(u):
                kind, j, h = u
                n = N_SCORE[u]
                tok = slice(j * P, (j + 1) * P)
                if n >= 2:
                    pe.wait_ge(s_free[n % 2], n // 2)
                ps = psS[:, n % 2, :]
                if kind == "q":
                    for g in range(MLA_HEADS):
                        for k in range(2):
                            ins = mm(ps[:, g * P:(g + 1) * P], wq[:, k, g, :], cq[:, k, tok], start=(k == 0), stop=(k == 1))
                elif kind == "m":
                    w = (j + 1) * P
                    if h == 0:
                        nq = N_SCORE["q", j, 0]
                        pe.wait_ge(s_free[nq % 2], nq // 2 + 1)
                        pe.wait_ge(rope_read, 2 * j + 2)
                    if j == 0 and h:
                        pe.wait_ge(kpe_all, h)
                    for c in range(0, w, 512):
                        e = min(w, c + 512)
                        ins = mm(ps[:, c:e], qcat[:, j % 2, h, :], kcat[:, h, c:e], start=True, stop=True)
                else:
                    lo = CHUNK if j == 0 else 0
                    rows_ = slice(h * SWA_DIM, (h + 1) * SWA_DIM)
                    for i in range(GQ):
                        ins = mm(ps[:, i * 256 + lo:i * 256 + BAND], qs[rows_, i, tok], ks[rows_, j * P - CHUNK + lo:(j + 1) * P],
                                 start=True, stop=True)
                ins.then_inc(s_full, 1)

            def turn(u):
                kind, j, h = u
                m = N_SOFT.get(u)
                if kind == "m":
                    n = N_SCORE[u]
                    pe.wait_ge(s_free[n % 2], n // 2 + 1)
                    for c in range(chunks_of(u)):
                        transposes((u, c), [prob[:, m % 2, k * P:(k + 1) * P] for k in range(4 * c, min(4 * c + 4, j + 1))])
                elif kind == "s":
                    pe.wait_ge(p_ready, 2 * j + h + 1)
                    transposes((u, 0), [prob[:, m % 2, i * BAND + CHUNK:(i + 1) * BAND] for i in range(GQ)])
                    if j:
                        transposes((u, 1), [prob[:, m % 2, i * BAND:i * BAND + CHUNK] for i in range(GQ)], rows_out=CHUNK)
                elif kind == "y":
                    pe.wait_ge(y_ready, j + 1)
                    for c in range(2):
                        transposes((u, c), [y[:, (4 * c + i) * P:(4 * c + i + 1) * P] for i in range(4)])

            def weigh(u):
                kind, j, h = u
                if kind not in "ms":
                    return
                m = N_SOFT[u]
                for c in range(chunks_of(u)):
                    evacuated((u, c))
                if kind == "m":
                    if h == 0 and j:
                        pe.wait_ge(y_ready, j)
                    for k in range(j + 1):
                        ins = mm(psM[:, h * MLA_V:(h + 1) * MLA_V], probT[:, m % 2, k, :], vmla[:, k, h * MLA_V:(h + 1) * MLA_V],
                                 start=(k == 0), stop=(k == j))
                else:
                    dims = slice(ROPE + h * SWA_DIM, ROPE + (h + 1) * SWA_DIM)
                    for i in range(GQ):
                        out = psN[:, (h * GQ + i) * SWA_DIM:(h * GQ + i + 1) * SWA_DIM]
                        ins = mm(out, probT[:, m % 2, i, :], krvs[:, j, dims], start=True, stop=(j == 0))
                        if j:
                            ins = mm(out, probT[CHUNK:P, m % 2, 4 + i, :], krvs[CHUNK:P, j - 1, dims], start=False, stop=True)
                ins.then_inc(pv_full, 1)

            for t in range(len(UNITS) + 2):
                if t < len(UNITS) and UNITS[t] in N_SCORE:
                    score(UNITS[t])
                if 0 < t <= len(UNITS):
                    turn(UNITS[t - 1])
                if t >= 2:
                    weigh(UNITS[t - 2])

            def project(key, stationary, weights, steps):
                n = PROJ_NO[key]
                if n:
                    pe.wait_ge(ae_free, n)
                for c in range(2):
                    for k in range(steps):
                        ins = mm(bank(4 + c), stationary(k), weights[:, k, c * 512:(c + 1) * 512], start=(k == 0), stop=(k == steps - 1))
                    ins.then_inc(ae_full, 1)

            for s in range(2):
                pe.wait_ge(s_free[s], FREE_S[s])
            pe.wait_ge(y_ready, NT)
            for c in range(2):
                evacuated((("y", NT - 1, 0), c))
            pe.wait_ge(ld_wo, 32)
            for s in range(NT + 3):
                if s < NT:
                    project(("A", s), lambda k: yT[:, k, s * P:(s + 1) * P], w_o, KC)
                j = s - 2
                if 0 <= j < NT:
                    pe.wait_ge(p8_ready, j + 1)
                    for c in range(2):
                        transposes(("p8", j, c), [prob[:, 0, (4 * c + i) * P:(4 * c + i + 1) * P] for i in range(4)])
                    for c in range(2):
                        evacuated(("p8", j, c))
                    if j:
                        pe.wait_ge(om_ready, j)
                    if j >= 2:
                        pe.wait_ge(r_ready, j - 1)
                    for h in range(MEM_HEADS):
                        for t in range(2):
                            ins = mm(psN[:, h * P:(h + 1) * P], probT[:, 0, 2 * h + t, :], vm[:, t, h * P:(h + 1) * P],
                                     start=(t == 0), stop=(t == 1))
                    ins.then_inc(o8_full, 1)
                j = s - 1
                if 0 <= j < NT:
                    if j == 0:
                        pe.wait_ge(ld_wmq, 16)
                    pe.wait_ge(ln_done, LN_NO["A", j] + 1)
                    for c in range(2):
                        transposes(("h1", j, c), [hring[:, j % 4, (4 * c + i) * P:(4 * c + i + 1) * P] for i in range(4)])
                    for c in range(2):
                        evacuated(("h1", j, c))
                    if j:
                        pe.wait_ge(qm_ready, j)
                    for h in range(MEM_HEADS):
                        for k in range(KC):
                            ins = mm(psM[:, h * P:(h + 1) * P], w_mq[:, k, h * P:(h + 1) * P], h1T[:, j % 2, k, :],
                                     start=(k == 0), stop=(k == KC - 1))
                    ins.then_inc(qm_full, 1)
                j = s - 2
                if 0 <= j < NT:
                    if j == 0:
                        pe.wait_ge(ld_wmo, 16)
                    pe.wait_ge(om_ready, j + 1)
                    transposes(("o8", j, 0), [om[:, i * P:(i + 1) * P] for i in range(4)])
                    evacuated(("o8", j, 0))
                    project(("E", j), lambda k: omT[:, k, :], w_mo, MEM_HEADS)
                j = s - 1
                if 0 <= j < NT:
                    pe.wait_ge(qm_ready, j + 1)
                    if j:
                        pe.wait_ge(p8_ready, j)
                    for h in range(MEM_HEADS):
                        ins = mm(psS[:, 0, h * N_MEM:(h + 1) * N_MEM], qm[:, h, :], kmT[:, h, :], start=True, stop=True)
                    ins.then_inc(c_full, 1)
                j = s - 3
                if 0 <= j < NT:
                    pe.wait_ge(ln_done, LN_NO["E", j] + 1)
                    for c in range(2):
                        transposes(("h2", j, c), [hring[:, j % 4, (4 * c + i) * P:(4 * c + i + 1) * P] for i in range(4)])
                    for c in range(2):
                        evacuated(("h2", j, c))
                    pe.wait_ge(om_ready, min(NT, j + 2))
                    if j == 0:
                        pe.wait_ge(ld_late, 16 * 7)
                    for k in range(KC):
                        ins = mm(psN[:, 0:ROUTE], h2T[:, k, :], w_route[:, k, :], start=(k == 0), stop=(k == KC - 1))
                    ins.then_inc(r_full, 1)
            pe.wait_ge(oh_ready, 1)
            flat = oh_sum[:, :, :].rearrange("p j e -> p (j e)")
            mm(bank(2)[:, 0:NT * N_EXP], tri[:, :], flat, start=True, stop=True).then_inc(rank_full, 1)
            mm(bank(3)[:, 0:NT * N_EXP], ones[:, :], flat, start=True, stop=True).then_inc(rank_full, 1)

            pe.wait_ge(items_ready, 1)
            n_items = pe.value_load(n_items_t[0:1, 0:1], min_val=1, max_val=MAX_ITEMS)

            def turn_x(s, count):
                pe.wait_ge(x_loaded[s], count * 16)
                for c in range(2):
                    for i in range(4):
                        k = 4 * c + i
                        ins = T(psT[:, c, i * P:(i + 1) * P], xg[s][:, k * P:(k + 1) * P], ident[:, :])
                    ins.then_inc(xT_full[s], 1)

            def gate_up(s, count):
                pe.wait_ge(xT_ready[s], count)
                for k in range(KC):
                    if k % 4 == 0:
                        pe.wait_ge(gu_loaded[s][k // 4], count * 16)
                    for c in range(2):
                        ins = mm(bank(2 + c), xgT[s][:, k, :], w_gu[s][:, k, c * 512:(c + 1) * 512], start=(k == 0), stop=(k == KC - 1))
                ins.then_inc(gu_full, 1)

            def turn_act(s, i):
                pe.wait_ge(act_ready, i + 1)
                for k in range(4):
                    ins = T(psM[:, k * P:(k + 1) * P], act[s][:, k * P:(k + 1) * P], ident[:, :])
                ins.then_inc(aT_full, 1)

            def down(s, i, count):
                pe.wait_ge(aT_ready, i + 1)
                pe.wait_ge(dn_loaded[s], count * 16)
                for c in range(2):
                    for k in range(4):
                        ins = mm(bank(4 + c), actT[s][:, k, :], w_dn[s][:, k, c * 512:(c + 1) * 512], start=(k == 0), stop=(k == 3))
                    ins.then_inc(y_full, 1)

            turn_x(0, 1)
            gate_up(0, 1)
            with pe.Fori(0, MAX_ITEMS // 2) as r:
                for s in range(2):
                    i = r * 2 + s
                    with pe.If(i + 1 < n_items):
                        turn_x(1 - s, r + (1 + s))
                    with pe.If(i < n_items):
                        turn_act(s, i)
                    with pe.If(i + 1 < n_items):
                        gate_up(1 - s, r + (1 + s))
                    with pe.If(i < n_items):
                        down(s, i, r + 1)


def constants():
    inv = (10000.0 ** (-np.arange(0, ROPE, 2) / ROPE)).astype(np.float32)
    ident = np.eye(P, dtype=np.float32)
    tri = np.triu(np.ones((P, P), np.float32), 1)
    i, w = np.arange(P)[:, None], np.arange(BAND)[None, :] - CHUNK
    seen = (w // CHUNK <= i // CHUNK) & (w // CHUNK >= i // CHUNK - 1)
    slopes = 2.0 ** (-8.0 * np.arange(1, SWA_HEADS + 1) / SWA_HEADS)
    alibi = np.where(seen[:, None, :], -slopes[None, :, None] * np.abs(i - w)[:, None, :], MASKED)
    rope = np.zeros((P, 4), np.float32)
    rope[:, 0] = inv[np.arange(P) % 16]
    rope[NOPE:QK, 1], rope[NOPE:QK, 2] = 0.25, np.pi / 2
    t = np.arange(NT)[None, :, None] * P + np.arange(P)[:, None, None]
    k = np.arange(TOP_K)[None, None, :]
    rows = np.zeros((P, NT, TOP_K, 4), np.int32)
    rows[..., 0], rows[..., 1] = t, TOP_K * t + k
    iotas = np.concatenate([np.arange(N_EXP) - 64.0, np.arange(MAX_ITEMS)])[None, :]
    return {"c_ident": ident, "c_tri": tri, "c_alibi": alibi.reshape(P, -1).astype(np.float32), "c_rope": rope,
            "c_inv": inv[None, :], "c_rows": rows.reshape(P, -1), "c_iotas": iotas.astype(np.float32)}


_TWO_DIM = ["x", "positions", "mem", "w_in", "w_uq", "w_ukv", "w_o", "w_mq", "w_mk", "w_mv", "w_mo", "w_group", "w_expert"]
_ROWS = ["ln_in_g", "ln_in_b", "g_q", "g_kv", "sinks", "ln1_g", "ln1_b", "ln2_g", "ln2_b", "b_group", "b_expert", "ln3_g", "ln3_b"]
_THREE_DIM = ["w_gate_up", "w_down"]


def kernel(**inputs):
    import concourse.bacc as bacc
    from concourse.bass_utils import run_bass_kernel_spmd

    arrays = dict(constants())
    for n in _TWO_DIM:
        v = np.asarray(inputs[n])
        arrays[n] = v if n == "positions" else v.reshape(v.shape[-2:])
    for n in _ROWS:
        arrays[n] = np.asarray(inputs[n]).reshape(1, -1)
    for n in _THREE_DIM:
        v = np.asarray(inputs[n])
        arrays[n] = v.reshape(v.shape[-3:])
    arrays = {f"in_{n}": np.ascontiguousarray(v) for n, v in arrays.items()}
    nc = bacc.Bacc("TRN2", target_bir_lowering=False, num_devices=1)
    a = {n[3:]: nc.dram_tensor(n, v.shape, mybir.dt.from_np(v.dtype), kind="ExternalInput").ap() for n, v in arrays.items()}
    out = nc.dram_tensor("out", [SEQ, D], F32, kind="ExternalOutput").ap()
    build_program(nc, a, out)
    r = run_bass_kernel_spmd(nc, [arrays], core_ids=[0])
    return r.results[0]["out"].reshape(np.asarray(inputs["x"]).shape)
```

```python
import numpy as np
from contextlib import ExitStack

import concourse.bass as bass
from concourse import mybir

F32 = mybir.dt.float32
I32 = mybir.dt.int32
ALU = mybir.AluOpType
ACT = mybir.ActivationFunctionType
X = mybir.AxisListType.X

P = 128
SEQ, D = 1024, 1024
NT, KC = SEQ // P, D // P
HALF = 512
N_MEM, MEM_HEADS, MEM_DIM = 256, 4, 128
MLA_HEADS, NOPE, ROPE, MLA_V = 8, 64, 32, 64
QK = NOPE + ROPE
Q_LORA, KV_LORA = 256, 128
SWA_HEADS, SWA_KV, SWA_DIM, CHUNK = 8, 2, 64, 64
GQ = SWA_HEADS // SWA_KV
BAND = 3 * CHUNK
N_GROUPS, PER_GROUP = 4, 8
N_EXP = N_GROUPS * PER_GROUP
F_EXP = 512
TOP_K = 2
ROUTE = N_GROUPS + N_EXP
MAX_ITEMS = SEQ * TOP_K // P + N_EXP
HALF_P = P // 2
NARROW, NO_ITEM, WIDE = 0, 1, 2
ALPHA = 2.0 ** 0.25
LN_EPS, RMS_EPS = 1e-5, 1e-6
MASKED = -1e30
NO_ROW = 1 << 20
IN_COLS = Q_LORA + KV_LORA + ROPE + (SWA_HEADS + 2 * SWA_KV) * SWA_DIM
TWO_PI_1 = 6.28125
TWO_PI_2 = 0.0019350051879882812
TWO_PI_3 = 2 * np.pi - TWO_PI_1 - TWO_PI_2
ROUNDER = 1.5 * 2.0 ** 23
C_KV, C_QS, C_KS, C_KR = Q_LORA, Q_LORA + KV_LORA, Q_LORA + KV_LORA + 512, Q_LORA + KV_LORA + 640


def attention_units():
    units = [("q", 0, 0)]
    for j in range(NT):
        for h in range(MLA_HEADS):
            units.append(("m", j, h))
            if h == 3 and j:
                units.append(("y", j - 1, 0))
            if h == 6 and j + 1 < NT:
                units.append(("q", j + 1, 0))
        units += [("s", j, 0), ("s", j, 1)]
    return units + [("gap", 0, 0), ("y", NT - 1, 0)]


UNITS = attention_units()
SCORED = [u for u in UNITS if u[0] in "qms"]
SOFTMAXED = [u for u in UNITS if u[0] in "ms"]
N_SCORE = {u: n for n, u in enumerate(SCORED)}
N_SOFT = {u: n for n, u in enumerate(SOFTMAXED)}


def chunks_of(u):
    kind, j, _ = u
    if kind == "m":
        return 1 if j < 4 else 2
    if kind == "s":
        return 1 if j == 0 else 2
    return 2 if kind == "y" else 0


def number_chunks():
    keys = [("mem", t, c) for t in range(2) for c in range(2)]
    keys += [("x", j, c) for j in range(NT) for c in range(2)]
    keys += [("kpe", 0, c) for c in range(2)]
    keys += [(u, c) for u in UNITS for c in range(chunks_of(u))]
    for s in range(NT + 3):
        if 0 <= s - 2 < NT:
            keys += [("p8", s - 2, c) for c in range(2)]
        if 0 <= s - 1 < NT:
            keys += [("h1", s - 1, c) for c in range(2)]
        if 0 <= s - 2 < NT:
            keys += [("o8", s - 2, 0)]
        if 0 <= s - 3 < NT:
            keys += [("h2", s - 3, c) for c in range(2)]
    return {k: n for n, k in enumerate(keys)}


CHUNK_NO = number_chunks()
N_CHUNKS = len(CHUNK_NO)


def number_projections():
    uses = []
    for s in range(NT + 3):
        if s < NT:
            uses.append(("A", s))
        if 0 <= s - 2 < NT:
            uses.append(("E", s - 2))
    return {k: n for n, k in enumerate(uses)}


PROJ_NO = number_projections()
LN_NO = {("in", j): j for j in range(NT)}
LN_NO |= {(k, j): NT + n for (k, j), n in PROJ_NO.items()}
LN_NO |= {("out", j): 3 * NT + j for j in range(NT)}



def build_program(nc, a, o):
    h0_d = nc.dram_tensor("h0_scratch", [SEQ, D], F32).ap()
    h2_d = nc.dram_tensor("h2_scratch", [SEQ, D], F32).ap()
    ye_d = nc.dram_tensor("expert_rows_scratch", [SEQ * TOP_K, D], F32).ap()
    ctx = ExitStack()
    with ctx:
        kib = 1024
        base = nc.sbuf_base + (-nc.sbuf_base) % 64

        def at(name, shape, off, dt=F32):
            return nc.alloc_sbuf_tensor_at(name, shape, dt, offset=base + int(off * kib))

        def sem(name):
            return ctx.enter_context(nc.semaphore(name))

        hring = at("hring", [P, 4, D], 0)
        hT = at("hT", [P, KC, SEQ], 16)
        yT = at("yT", [P, KC, SEQ], 16)
        w_in = at("w_in_sb", [P, KC, IN_COLS], 48)
        kcat = at("kcat", [QK, MLA_HEADS, SEQ], 48)
        w_mq = at("w_mq_sb", [P, KC, 512], 48)
        w_mo = at("w_mo_sb", [P, MEM_HEADS, D], 64)
        tri = at("tri", [P, P], 80)
        ones = at("ones", [P, P], 80.5)
        iotas = at("iotas", [P, N_EXP + P], 81)
        choice_no = at("choice_no", [P, NT, TOP_K], 81.75)
        item_no = at("item_no", [P, 2], 81.875)
        route_b = at("route_b", [P, ROUTE], 82)
        w_route = at("w_route_sb", [P, KC, ROUTE], 82.25)
        w_mk = at("w_mk_sb", [P, KC, 512], 85)
        w_mv = at("w_mv_sb", [P, KC, 512], 101)
        vmla = at("vmla", [P, NT, 512], 85)
        qs = at("qs", [P, GQ, SEQ], 101)
        w_o = at("w_o_sb", [P, KC, D], 85)
        wq = at("wq", [P, 2, MLA_HEADS, P], 117)
        wukv = at("wukv", [P, 2, MLA_HEADS, NOPE], 125)
        cq = at("cq", [P, 2, SEQ], 129)
        gb2 = at("gb2", [P, 2, D], 129)
        ckv = at("ckv", [P, SEQ], 137)
        om = at("om", [P, 512], 137)
        omT = at("omT", [P, MEM_HEADS, P], 139)
        memT = at("memT", [P, KC, N_MEM], 141)
        qcat = at("qcat", [QK, 2, MLA_HEADS, P], 141)
        h1T = at("h1T", [P, 2, KC, P], 141)
        ks = at("ks", [P, SEQ], 149)
        qm = at("qm", [P, MEM_HEADS, P], 149)
        krvs = at("krvs", [P, NT, ROPE + P], 153)
        h2T = at("h2T", [P, KC, P], 153)
        mem_sb = at("mem_sb", [P, 2, D], 158)
        prob = at("prob", [P, 2, D], 158)
        sq = at("sq", [P, 3, SEQ], 158)
        wuq = at("wuq_raw", [P, 2, MLA_HEADS, QK], 168)
        probT = at("probT", [P, 2, KC, P], 166)
        pos_all = at("pos_all", [P, SEQ], 174, I32)
        alibi = at("alibi", [P, SWA_HEADS, BAND], 174)
        trig_t = at("trig_t", [P, SEQ], 180)
        y = at("y", [P, D], 180)
        vm = at("vm", [P, 2, 512], 184)
        kmT = at("kmT", [P, MEM_HEADS, N_MEM], 188)
        cs = at("cos_sin", [P, SEQ], 192)
        gb1 = at("gb1", [P, 2, D], 196)
        w_gu = [at("w_gu0", [P, KC, 2 * F_EXP], 16), at("w_gu1", [P, KC, 2 * F_EXP], 85)]
        w_dn = [at("w_dn0", [P, 4, D], 48), at("w_dn1", [P, 4, D], 64)]
        xg = [at("xg0", [P, D], 129), at("xg1", [P, D], 133)]
        xgT = [at("xgT0", [P, KC, P], 141), at("xgT1", [P, KC, P], 145)]
        gate_s = at("gate_s", [P, F_EXP], 137)
        act = [at("act0", [P, F_EXP], 139), at("act1", [P, F_EXP], 149)]
        actT = [at("actT0", [P, 4, P], 151), at("actT1", [P, 4, P], 153)]
        ye = [at("ye0", [P, D], 158), at("ye1", [P, D], 162)]
        table = at("table", [P, MAX_ITEMS + 3, 3], 157, I32)
        tab_x = [at("tab_x0", [P, 1], 155, I32), at("tab_x1", [P, 1], 155.25, I32)]
        tab_y = [at("tab_y0", [P, 2], 155.5, I32), at("tab_y1", [P, 2], 155.75, I32)]
        h2_first = at("h2_first", [P, 4, D], 166)
        pair = [at(f"pair{j}", [P, 2, D], 16 + 8 * j if j < 4 else 85 + 8 * (j - 4)) for j in range(NT)]
        small_at = [117.0]

        def scratch(name, shape, dt=F32):
            off = small_at[0]
            small_at[0] += -(-int(np.prod(shape[1:])) * 4 // 64) * 64 / kib
            return at(name, shape, off, dt)

        TE = [P, NT, N_EXP]
        elm, eqx, oh1, oh2, rank, place = (scratch(n, TE) for n in ("elm", "eqx", "oh1", "oh2", "rank", "place"))
        oh_sum, tot = scratch("oh_sum", TE), scratch("tot", TE)
        gl, eg, gpen = (scratch(n, [P, NT, N_GROUPS]) for n in ("gl", "eg", "gpen"))
        t8 = [scratch(f"t8_{i}", [P, NT]) for i in range(10)]
        cnt, nblk, nblk_f, incl, first_block, row_end = (scratch(n, [P, N_EXP]) for n in (
            "cnt", "nblk", "nblk_f", "incl", "first_block", "row_end"))
        posf, posi = scratch("posf", [P, NT, TOP_K]), scratch("posi", [P, NT, TOP_K], I32)
        gates = scratch("gates", [P, NT, TOP_K])
        assert small_at[0] <= 129
        item_cmp, item_sum = at("item_cmp", [P, 3, N_EXP], 158), at("item_sum", [P, 4], 159)
        item_cols = at("item_cols", [P, 2], 159.25)
        posd = at("posd", [P, NT, TOP_K], 159.5)
        dest = at("dest", [P, MAX_ITEMS], 160)
        mark_row, mark_item = at("mark_row", [P, NT, TOP_K, P], 141), at("mark_item", [P, NT, TOP_K, 2, MAX_ITEMS], 184)
        small_at[0] = 204.0
        ident = scratch("ident", [P, P])
        logits = scratch("logits", [P, NT, ROUTE])
        stats, mv = scratch("stats", [P, 2, 2, 6]), scratch("mv", [P, 2, 2])
        var, rstd = scratch("var", [P, 4 * NT]), scratch("rstd", [P, 4 * NT])
        neghalf = scratch("neghalf", [P, 16])
        neg_max = scratch("neg_max", [P, 4, 4])
        sums_m, sums_s = scratch("sums_m", [P, 2, 8]), scratch("sums_s", [P, 2, 8])
        sums_x = scratch("sums_x", [P, 4])
        sink_e, sink_d, sink = (scratch(n, [P, 2, 8]) for n in ("sink_e", "sink_d", "sink"))
        rinv, rmax = scratch("rinv", [P, 8]), scratch("rmax", [P, 4])
        one_col = scratch("one_col", [P, 1])
        gq, gkv = scratch("gq", [P, 4]), scratch("gkv", [P, 1])
        rope_f = scratch("rope_f", [P, 4])
        ms, rms = scratch("ms", [P, 16]), scratch("rms", [P, 16])
        item_exp, n_items_t = scratch("item_exp", [1, MAX_ITEMS], I32), scratch("n_items_t", [1, 1], I32)
        item_kind = scratch("item_kind", [1, MAX_ITEMS + 2], I32)
        assert base + small_at[0] * kib <= nc.sbuf_usable_end, small_at
        pos_t, posf_t = at("pos_t", [P, NT], 178, I32), at("posf_t", [P, NT], 178.25)
        inv_b = at("inv_b", [P, 16], 178.5)
        kang, kang_t = at("kang", [P, 2, NT, 16], 180), at("kang_t", [P, NT, 16], 181)
        krot, krot_t = at("krot", [P, NT, ROPE], 182), at("krot_t", [P, NT, 16], 183)

        psT = ctx.enter_context(nc.psum_tensor("psT", [P, 2, 512], F32))
        psS = ctx.enter_context(nc.psum_tensor("psS", [P, 2, D], F32))
        psM = ctx.enter_context(nc.psum_tensor("psM", [P, 512], F32))
        psN = ctx.enter_context(nc.psum_tensor("psN", [P, 512], F32))

        def bank(i):
            return [psT[:, 0, :], psT[:, 1, :], psS[:, 0, 0:512], psS[:, 0, 512:D],
                    psS[:, 1, 0:512], psS[:, 1, 512:D], psM[:, :], psN[:, :]][i]

        ld_ident, ld_gb1, ld_gb2, ld_wup, ld_pos, ld_small = (sem(n) for n in (
            "ld_ident", "ld_gb1", "ld_gb2", "ld_wup", "ld_pos", "ld_small"))
        ld_mem, ld_mk, ld_mv, ld_win, ld_alibi, ld_late = (sem(n) for n in (
            "ld_mem", "ld_mk", "ld_mv", "ld_win", "ld_alibi", "ld_late"))
        ld_x = [sem(f"ld_x{s}") for s in range(4)]
        ld_h0 = [sem(f"ld_h0_{s}") for s in range(4)]
        st_h0 = [sem(f"st_h0_{s}") for s in range(4)]
        st_h2 = [sem(f"st_h2_{s}") for s in range(4)]
        ld_wo, ld_wmq, ld_wmo = sem("ld_wo"), sem("ld_wmq"), sem("ld_wmo")
        v_done, var_ready, rstd_ready, ln_done = (sem(n) for n in ("v_done", "var_ready", "rstd_ready", "ln_done"))
        t_full = sem("t_full")
        t_free = [sem("t_free0"), sem("t_free1")]
        mem_full, mem_free = sem("mem_full"), sem("mem_free")
        pj_full, pj_free, kv_full, kv_free = (sem(n) for n in ("pj_full", "pj_free", "kv_full", "kv_free"))
        pool_const, wq_ready, sq_ready, ss_full, ms_ready, rms_ready = (sem(n) for n in (
            "pool_const", "wq_ready", "sq_ready", "ss_full", "ms_ready", "rms_ready"))
        rb_full, cqn_ready, kn_full, kn_free, vv_full, vv_free = (sem(n) for n in (
            "rb_full", "cqn_ready", "kn_full", "kn_free", "vv_full", "vv_free"))
        trig_ready, trig_done, krot_ready, kpe_all = (sem(n) for n in ("trig_ready", "trig_done", "krot_ready", "kpe_all"))
        s_full = sem("s_full")
        s_free = [sem("s_free0"), sem("s_free1")]
        rope_read, rope_done, mx_ready, p_ready = (sem(n) for n in ("rope_read", "rope_done", "mx_ready", "p_ready"))
        pv_full, y_ready = sem("pv_full"), sem("y_ready")
        ae_full, ae_free, qm_full, qm_ready, c_full, nm8_ready, p8_ready = (sem(n) for n in (
            "ae_full", "ae_free", "qm_full", "qm_ready", "c_full", "nm8_ready", "p8_ready"))
        o8_full, om_ready, r_full, r_ready = (sem(n) for n in ("o8_full", "om_ready", "r_full", "r_ready"))
        oh_ready, rank_full, g_exp_in, g_exp_out, item_cols_ready, items_ready = (sem(n) for n in (
            "oh_ready", "rank_full", "g_exp_in", "g_exp_out", "item_cols_ready", "items_ready"))
        pool_ready = sem("pool_ready")
        rows_done, items_full, marks_ready = sem("rows_done"), sem("items_full"), sem("marks_ready")
        gu_loaded = [[sem(f"gu_loaded{s}{h}") for h in range(2)] for s in range(2)]
        dn_loaded = [sem(f"dn_loaded{s}") for s in range(2)]
        table_full, table_ready = sem("table_full"), sem("table_ready")
        tokens_ready = [sem("tokens_ready0"), sem("tokens_ready1")]
        places_ready = [sem("places_ready0"), sem("places_ready1")]
        x_loaded = [sem("x_loaded0"), sem("x_loaded1")]
        xT_full, xT_ready = [sem("xT_full0"), sem("xT_full1")], [sem("xT_ready0"), sem("xT_ready1")]
        gu_full, silu_done, act_ready = sem("gu_full"), sem("silu_done"), sem("act_ready")
        aT_full, aT_ready, y_full, ye_ready = sem("aT_full"), sem("aT_ready"), sem("y_full"), [sem("ye_ready0"), sem("ye_ready1")]
        ye_stored = [sem("ye_stored0"), sem("ye_stored1")]
        ld_pair = [sem(f"ld_pair{j}") for j in range(NT)]
        ld_h2, st_out, g_in_psum, out_ready = sem("ld_h2"), sem("st_out"), sem("g_in_psum"), sem("out_ready")
        first_added, both_added, scaled = sem("first_added"), sem("both_added"), sem("scaled")

        g_psum = psT[:, :, :].rearrange("p b n -> p (b n)")

        def h2_at(j):
            return h2_first[:, j, :] if j < 4 else hring[:, j - 4, :]

        def ktile(w):
            return w.rearrange("(k p) n -> p k n", p=P)

        def bcast(v):
            return v.to_broadcast([P, v.shape[1]])

        LAST_SOFT = len(SOFTMAXED)
        FREE_S = [(len(SCORED) + 1 - s) // 2 for s in range(2)]

        block = ctx.enter_context(nc.Block())

        @block.sync
        def _(sp):
            sp.dma_start(mem_sb[:, :, :], a["mem"].rearrange("(t p) d -> p t d", p=P)).then_inc(ld_mem, 16)
            sp.dma_start(w_mk[:, :, :], ktile(a["w_mk"])).then_inc(ld_mk, 16)
            sp.dma_start(hring[:, 0, :], a["x"][0:P, :]).then_inc(ld_x[0], 16)
            sp.dma_start(w_mv[:, :, :], ktile(a["w_mv"])).then_inc(ld_mv, 16)
            for j in range(1, 4):
                sp.dma_start(hring[:, j, :], a["x"][j * P:(j + 1) * P, :]).then_inc(ld_x[j], 16)
            w_src = ktile(a["w_in"])
            kr = Q_LORA + KV_LORA
            for dst, src, n in ((0, 0, kr), (C_QS, kr + ROPE, 640), (C_KR, kr, ROPE), (C_KR + ROPE, kr + ROPE + 640, P)):
                sp.dma_start(w_in[:, :, dst:dst + n], w_src[:, :, src:src + n]).then_inc(ld_win, 16)
            for j in range(NT):
                sp.wait_ge(ln_done, LN_NO["in", j] + 1)
                sp.dma_start(h0_d[j * P:(j + 1) * P, :], hring[:, j % 4, :]).then_inc(st_h0[j % 4], 16)
                if j + 4 < NT:
                    sp.wait_ge(st_h0[j % 4], 16)
                    sp.wait_ge(t_full, CHUNK_NO["x", j, 1] + 1)
                    sp.dma_start(hring[:, j % 4, :], a["x"][(j + 4) * P:(j + 5) * P, :]).then_inc(ld_x[j % 4], 16)
            sp.dma_start(gb1[:, 0, :], bcast(a["ln1_g"])).then_inc(ld_gb1, 16)
            sp.dma_start(gb1[:, 1, :], bcast(a["ln1_b"])).then_inc(ld_gb1, 16)
            for j in range(4):
                sp.wait_ge(t_full, CHUNK_NO["x", j + 4, 1] + 1)
                sp.wait_ge(st_h0[j], 32)
                sp.dma_start(hring[:, j, :], h0_d[j * P:(j + 1) * P, :]).then_inc(ld_h0[j], 16)
            sp.wait_ge(pj_full, 16)
            sp.wait_ge(kv_full, NT)
            sp.dma_start(tri[:, :], a["c_tri"]).then_inc(ld_late, 16)
            sp.dma_start(iotas[:, :], bcast(a["c_iotas"])).then_inc(ld_late, 16)
            sp.dma_start(choice_no[:, :, :], a["c_choice"].rearrange("p (j k) -> p j k", k=TOP_K)).then_inc(ld_late, 16)
            sp.dma_start(item_no[:, :], a["c_item"]).then_inc(ld_late, 16)
            sp.dma_start(route_b[:, 0:N_GROUPS], bcast(a["b_group"])).then_inc(ld_late, 16)
            sp.dma_start(route_b[:, N_GROUPS:ROUTE], bcast(a["b_expert"])).then_inc(ld_late, 16)
            sp.dma_start(w_route[:, :, 0:N_GROUPS], ktile(a["w_group"])).then_inc(ld_late, 16)
            sp.dma_start(w_route[:, :, N_GROUPS:ROUTE], ktile(a["w_expert"])).then_inc(ld_late, 16)
            sp.wait_ge(krot_ready, 1)
            sp.dma_start(alibi[:, :, :], a["c_alibi"].rearrange("p (h w) -> p h w", w=BAND)).then_inc(ld_alibi, 16)
            sp.wait_ge(pv_full, LAST_SOFT)
            sp.dma_start(w_o[:, 0:4, :], ktile(a["w_o"])[:, 0:4, :]).then_inc(ld_wo, 16)
            sp.dma_start(w_o[:, 4:8, :], ktile(a["w_o"])[:, 4:8, :]).then_inc(ld_wo, 16)
            sp.dma_start(w_mq[:, :, :], ktile(a["w_mq"])).then_inc(ld_wmq, 16)
            sp.dma_start(gb2[:, 0, :], bcast(a["ln2_g"])).then_inc(ld_gb2, 16)
            sp.dma_start(gb2[:, 1, :], bcast(a["ln2_b"])).then_inc(ld_gb2, 16)
            sp.dma_start(w_mo[:, :, :], ktile(a["w_mo"])).then_inc(ld_wmo, 16)
            for j in range(NT):
                s = j % 4
                sp.wait_ge(ln_done, LN_NO["E", j] + 1)
                sp.dma_start(h2_d[j * P:(j + 1) * P, :], hring[:, s, :]).then_inc(st_h2[s], 16)
                if j + 4 < NT:
                    sp.wait_ge(st_h2[s], 16)
                    sp.wait_ge(t_full, CHUNK_NO["h2", j, 1] + 1)
                    sp.dma_start(hring[:, s, :], h0_d[(j + 4) * P:(j + 5) * P, :]).then_inc(ld_h0[s], 16)
            sp.dma_start(gb1[:, 0, :], bcast(a["ln3_g"])).then_inc(ld_gb1, 16)
            sp.dma_start(gb1[:, 1, :], bcast(a["ln3_b"])).then_inc(ld_gb1, 16)
            for j in range(4):
                if j == 0:
                    sp.wait_ge(t_full, N_CHUNKS)
                sp.wait_ge(st_h2[j], 16)
                sp.dma_start(h2_first[:, j, :], h2_d[j * P:(j + 1) * P, :]).then_inc(ld_h2, 16)
            sp.wait_ge(items_ready, 1)
            n_items = sp.value_load(n_items_t[0:1, 0:1], min_val=1, max_val=MAX_ITEMS)

            def load_weights(s, item, earlier):
                e = sp.value_load(item_exp[0:1, bass.ds(item, 1)], min_val=0, max_val=N_EXP - 1)
                gu = a["w_gate_up"][bass.ds(e, 1), :, :].rearrange("e (k p) n -> (e p) k n", p=P)
                dn = a["w_down"][bass.ds(e, 1), :, :].rearrange("e (k p) n -> (e p) k n", p=P)
                if earlier:
                    sp.wait_ge(gu_full, item - 1)
                for h in range(2):
                    sp.dma_start(w_gu[s][:, 4 * h:4 * h + 4, :], gu[:, 4 * h:4 * h + 4, :]).then_inc(gu_loaded[s][h], 16)
                if earlier:
                    sp.wait_ge(y_full, item * 2 - 2)
                sp.dma_start(w_dn[s][:, :, :], dn).then_inc(dn_loaded[s], 16)

            load_weights(0, 0, False)
            sp.wait_ge(pool_ready, 2)
            load_weights(1, 1, False)
            with sp.Fori(1, MAX_ITEMS // 2) as r:
                for s in range(2):
                    with sp.If(r * 2 + s < n_items):
                        load_weights(s, r * 2 + s, True)
            sp.wait_ge(rows_done, 1)
            for j in range(NT):
                sp.dma_start(pair[j][:, :, :], ye_d[j * 2 * P:(j + 1) * 2 * P, :].rearrange("(p k) d -> p k d", k=TOP_K)).then_inc(ld_pair[j], 16)
            for j in range(NT):
                sp.wait_ge(out_ready, j + 1)
                sp.dma_start(o[j * P:(j + 1) * P, :], h2_at(j)).then_inc(st_out, 16)
            sp.wait_ge(st_out, 16 * NT)

        @block.gpsimd
        def _(pool):
            nc.gpsimd.memset(neghalf[:, :], -0.5).then_inc(pool_const, 1)
            nc.gpsimd.memset(one_col[:, :], 1.0).then_inc(pool_const, 1)
            pool.wait_ge(pool_const, 2)

            def rsqrt_of_variance(key):
                n = LN_NO[key]
                pool.wait_ge(var_ready, n + 1)
                nc.gpsimd.tensor_tensor(rstd[:, n:n + 1], var[:, n:n + 1], neghalf[:, 0:1], ALU.pow).then_inc(rstd_ready, 1)

            for j in range(NT):
                rsqrt_of_variance(("in", j))
            pool.wait_ge(ld_wup, 16 * 5)
            nc.gpsimd.tensor_scalar(gq[:, 0:2], gq[:, 0:2], QK ** -0.5, None, ALU.mult).then_inc(pool_const, 1)
            pool.wait_ge(pool_const, 3)
            nc.gpsimd.tensor_scalar(gq[:, 2:4], gq[:, 0:2], -1.0, None, ALU.mult).then_inc(pool_const, 1)
            pool.wait_ge(pool_const, 4)
            for k in range(2):
                nc.gpsimd.tensor_scalar(wq[:, k, :, 0:QK], wuq[:, k, :, :], gq[:, k:k + 1], None, ALU.mult)
                nc.gpsimd.tensor_scalar(wq[:, k, :, QK:QK + 16], wuq[:, k, :, NOPE + 16:QK], gq[:, 2 + k:3 + k], None, ALU.mult)
                nc.gpsimd.tensor_scalar(wq[:, k, :, QK + 16:P], wuq[:, k, :, NOPE:NOPE + 16], gq[:, k:k + 1], None, ALU.mult).then_inc(wq_ready, 1)
            nc.gpsimd.tensor_scalar(wukv[:, :, :, :], wukv[:, :, :, :], gkv[:, 0:1], None, ALU.mult).then_inc(wq_ready, 1)
            pool.wait_ge(wq_ready, 3)
            pool.wait_ge(t_full, CHUNK_NO["mem", 1, 1] + 1)
            for hf in range(2):
                cols = slice(hf * HALF, (hf + 1) * HALF)
                for c in range(3):
                    pool.wait_ge(pj_free, hf * 8 + c + 1)
                    src = cq[:, c, cols] if c < 2 else ckv[:, cols]
                    nc.gpsimd.tensor_tensor(sq[:, c, cols], src, src, ALU.mult).then_inc(sq_ready, 1)
            pool.wait_ge(ms_ready, 1)
            nc.gpsimd.tensor_tensor(rms[:, :], ms[:, :], neghalf[:, :], ALU.pow).then_inc(rms_ready, 1)
            for c in range(2):
                n = CHUNK_NO["kpe", 0, c]
                pool.wait_ge(t_free[n % 2], n // 2 + 1)
            for h in range(1, MLA_HEADS):
                nc.gpsimd.tensor_copy(kcat[NOPE:QK, h, :], kcat[NOPE:QK, 0, :]).then_inc(kpe_all, 1)
            for key in PROJ_NO:
                rsqrt_of_variance(key)
            pool.wait_ge(items_ready, 1)
            for s in range(2):
                nc.gpsimd.memset(xg[s][:, :], 0.0).then_inc(pool_const, 1)
            pool.wait_ge(pool_const, 6)
            for s in range(4):
                pool.wait_ge(st_h2[s], 32)
            pool.wait_ge(table_ready, 1)
            n_items = pool.value_load(n_items_t[0:1, 0:1], min_val=1, max_val=MAX_ITEMS)

            last_token, last_row = pool.to_reg(SEQ - 1), pool.to_reg(SEQ * TOP_K - 1)

            def gather(s, item, before):
                if not isinstance(before, int) or before:
                    pool.wait_ge(xT_ready[s], before)
                nc.gpsimd.tensor_copy(tab_x[s][:, :], table[:, bass.ds(item, 1), 0]).then_inc(tokens_ready[s], 1)
                pool.wait_ge(tokens_ready[s], before + 1)
                pool.sem_inc(pool_ready, 1)
                pool.indirect_dma_start(xg[s][:, :], None, h2_d, bass.IndirectOffsetOnAxis(ap=tab_x[s][:, 0:1], axis=0),
                                        bounds_check=last_token, oob_is_err=False).then_inc(x_loaded[s], 16)

            def places(s, item, before):
                if not isinstance(before, int) or before:
                    pool.wait_ge(ye_stored[s], before * 16)
                nc.gpsimd.tensor_copy(tab_y[s][:, :], table[:, bass.ds(item, 1), 1:3]).then_inc(places_ready[s], 1)

            def scatter(s, before):
                pool.wait_ge(places_ready[s], before + 1)
                pool.wait_ge(ye_ready[s], before + 1)
                pool.sem_inc(pool_ready, 1)
                pool.indirect_dma_start(ye_d, bass.IndirectOffsetOnAxis(ap=tab_y[s][:, 0:1], axis=0), ye[s][:, :], None,
                                        bounds_check=last_row, oob_is_err=False).then_inc(ye_stored[s], 16)

            gather(0, 0, 0)
            gather(1, 1, 0)
            for s in range(2):
                nc.gpsimd.memset(act[s][0:HALF_P, :], 0.0)
                nc.gpsimd.memset(ye[s][HALF_P:P, :], 0.0).then_inc(pool_const, 1)
            pool.wait_ge(pool_const, 8)
            for s in range(2):
                places(s, s, 0)
            gather(0, 2, 1)
            for s in range(2):
                gather(1 - s, s + 3, s + 1)
                scatter(s, 0)
            with pool.Fori(1, MAX_ITEMS // 2) as r:
                with pool.If(r * 2 < n_items):
                    for s in range(2):
                        with pool.If(r * 2 + (s + 3) < n_items):
                            gather(1 - s, r * 2 + (s + 3), r + (s + 1))
                        with pool.If(r * 2 + s < n_items):
                            places(s, r * 2 + s, r)
                            scatter(s, r)
            n0 = pool.snap((n_items + 1) // 2 * 16)
            n1 = pool.snap(n_items // 2 * 16)
            pool.wait_ge(ye_stored[0], n0)
            pool.wait_ge(ye_stored[1], n1)
            pool.sem_inc(rows_done, 1)
            for t in range(NT + 2):
                if t < NT:
                    pool.wait_ge(first_added, t + 1)
                    nc.gpsimd.tensor_tensor(h2_at(t), h2_at(t), pair[t][:, 1, :], ALU.add).then_inc(both_added, 1)
                if 0 <= t - 1 < NT:
                    rsqrt_of_variance(("out", t - 1))
                if t - 2 >= 0:
                    pool.wait_ge(scaled, t - 1)
                    nc.gpsimd.tensor_tensor(h2_at(t - 2), h2_at(t - 2), gb1[:, 1, :], ALU.add).then_inc(out_ready, 1)

        @block.scalar
        def _(actq):
            actq.dma_start(ident[:, :], a["c_ident"]).then_inc(ld_ident, 16)
            actq.dma_start(gb1[:, 0, :], bcast(a["ln_in_g"])).then_inc(ld_gb1, 16)
            actq.dma_start(gb1[:, 1, :], bcast(a["ln_in_b"])).then_inc(ld_gb1, 16)
            actq.dma_start(wuq[:, :, :, :], a["w_uq"].rearrange("(k p) (h n) -> p k h n", p=P, n=QK)).then_inc(ld_wup, 16)
            for t in range(2):
                actq.dma_start(wukv[:, t, :, :], a["w_ukv"].rearrange("p (h t n) -> p t h n", t=2, n=NOPE)[:, t, :, :]).then_inc(ld_wup, 16)
            actq.dma_start(gq[:, 0:2], a["g_q"].rearrange("a (k p) -> p (a k)", p=P), allow_slow_non_contiguous=True).then_inc(ld_wup, 16)
            actq.dma_start(gkv[:, :], a["g_kv"].rearrange("a p -> p a"), allow_slow_non_contiguous=True).then_inc(ld_wup, 16)
            actq.dma_start(pos_all[NOPE:P, :], a["positions"].to_broadcast([P - NOPE, SEQ])).then_inc(ld_pos, 16)
            actq.dma_start(pos_t[:, :], a["positions"].rearrange("a (j p) -> p (a j)", p=P), allow_slow_non_contiguous=True).then_inc(ld_pos, 16)
            actq.dma_start(rope_f[:, :], a["c_rope"]).then_inc(ld_pos, 16)
            actq.dma_start(inv_b[:, :], bcast(a["c_inv"])).then_inc(ld_pos, 16)
            for r in range(2):
                actq.dma_start(sink[:, r, :], bcast(a["sinks"])).then_inc(ld_small, 16)

            def evac(key, dst, src_cols=None):
                n = CHUNK_NO[key]
                actq.wait_ge(t_full, n + 1)
                src = psT[:, n % 2, :] if src_cols is None else src_cols(psT[:, n % 2, :])
                nc.scalar.copy(dst, src).then_inc(t_free[n % 2], 1)

            four = lambda v: v.rearrange("p (k n) -> p k n", n=P)
            for t in range(2):
                for c in range(2):
                    evac(("mem", t, c), memT[:, 4 * c:4 * c + 4, t * P:(t + 1) * P], four)
            for i in range(4):
                actq.wait_ge(mem_full, i + 1)
                dst = kmT[:, 2 * i:2 * i + 2, :] if i < 2 else vm[:, i - 2, :]
                src = bank(2 + i).rearrange("p (h n) -> p h n", h=2) if i < 2 else bank(2 + i)
                nc.scalar.copy(dst, src).then_inc(mem_free, 1)
            for hf in range(2):
                for j in range(4 * hf, 4 * hf + 4):
                    for c in range(2):
                        evac(("x", j, c), hT[:, 4 * c:4 * c + 4, j * P:(j + 1) * P], four)
                cols = slice(hf * HALF, (hf + 1) * HALF)
                for c in range(8):
                    i = hf * 8 + c
                    actq.wait_ge(pj_full, i + 1)
                    src = bank(2 + i % 4)
                    if c < 3:
                        nc.scalar.copy(cq[:, c, cols] if c < 2 else ckv[:, cols], src).then_inc(pj_free, 1)
                    elif c < 7:
                        g = (c - 3) // 2 * SWA_DIM
                        for b in range(2):
                            ins = nc.scalar.mul(qs[g:g + SWA_DIM, (2 * (c - 3) + b) % GQ, cols],
                                                src[b * SWA_DIM:(b + 1) * SWA_DIM, :], SWA_DIM ** -0.5)
                        ins.then_inc(pj_free, 1)
                    else:
                        nc.scalar.copy(ks[:, cols], src).then_inc(pj_free, 1)
                for j in range(4 * hf, 4 * hf + 4):
                    actq.wait_ge(kv_full, j + 1)
                    nc.scalar.copy(krvs[:, j, :], bank(6 + j % 2)[:, 0:ROPE + P]).then_inc(kv_free, 1)
            actq.wait_ge(trig_ready, 1)
            nc.scalar.activation(cs[NOPE:P, :], cs[NOPE:P, :], ACT.Sin).then_inc(trig_done, 1)
            actq.wait_ge(trig_ready, 2)
            nc.scalar.activation(kang[:, :, :, :], kang[:, :, :, :], ACT.Sin).then_inc(trig_done, 1)
            for i in range(8):
                p, hf = i // 2, i % 2
                actq.wait_ge(kn_full, i + 1)
                cols = slice(hf * HALF, (hf + 1) * HALF)
                nc.scalar.copy(kcat[0:NOPE, 2 * p, cols], bank(6 + i % 2)[0:NOPE, :])
                nc.scalar.copy(kcat[0:NOPE, 2 * p + 1, cols], bank(6 + i % 2)[NOPE:P, :]).then_inc(kn_free, 1)
            for c in range(2):
                n = CHUNK_NO["kpe", 0, c]
                actq.wait_ge(t_full, n + 1)
                nc.scalar.copy(kcat[NOPE:QK, 0, c * HALF:(c + 1) * HALF], psT[0:ROPE, n % 2, :]).then_inc(t_free[n % 2], 1)

            def softmax(u):
                kind, j, h = u
                n = N_SCORE[u]
                if kind == "q":
                    for c in range(2):
                        actq.wait_ge(rope_read, 2 * j + c + 1)
                        ins = nc.scalar.copy(qcat[0:NOPE, j % 2, 4 * c:4 * c + 4, :], four(psS[0:NOPE, n % 2, c * 512:(c + 1) * 512]))
                    ins.then_inc(s_free[n % 2], 1)
                    return
                m = N_SOFT[u]
                actq.wait_ge(mx_ready, m + 1)
                if m >= 2:
                    prev = SOFTMAXED[m - 2]
                    actq.wait_ge(t_full, CHUNK_NO[prev, chunks_of(prev) - 1] + 1)
                if kind == "m":
                    w = (j + 1) * P
                    nc.scalar.activation(prob[:, m % 2, 0:w], psS[:, n % 2, 0:w], ACT.Exp, bias=neg_max[:, m % 4, 0:1],
                                         accum_out=sums_m[:, j % 2, h:h + 1]).then_inc(s_free[n % 2], 1)
                else:
                    lo = CHUNK if j == 0 else 0
                    for i in range(GQ):
                        p = prob[:, m % 2, i * BAND + lo:(i + 1) * BAND]
                        nc.scalar.activation(p, p, ACT.Exp, bias=neg_max[:, m % 4, i:i + 1],
                                             accum_out=sums_s[:, j % 2, h * GQ + i:h * GQ + i + 1])
                    nc.scalar.activation(sink_e[:, j % 2, h * GQ:(h + 1) * GQ], sink_d[:, j % 2, h * GQ:(h + 1) * GQ],
                                         ACT.Exp).then_inc(p_ready, 1)

            def evac_odd(u):
                kind, j, h = u
                for c in range(chunks_of(u)):
                    n = CHUNK_NO[u, c]
                    if n % 2 == 0:
                        continue
                    m = N_SOFT.get(u)
                    if m is not None and m >= 2:
                        actq.wait_ge(pv_full, m - 1)
                    evac_attention(actq, nc.scalar.copy, u, c)

            def evac_attention(eng, copy, u, c):
                kind, j, h = u
                n = CHUNK_NO[u, c]
                m = N_SOFT.get(u)
                eng.wait_ge(t_full, n + 1)
                src = psT[:, n % 2, :]
                if kind == "m":
                    k = min(4, j + 1 - 4 * c)
                    copy(probT[:, m % 2, 4 * c:4 * c + k, :], four(src)[:, 0:k, :]).then_inc(t_free[n % 2], 1)
                elif kind == "s" and c == 0:
                    copy(probT[:, m % 2, 0:4, :], four(src)).then_inc(t_free[n % 2], 1)
                elif kind == "s":
                    copy(probT[CHUNK:P, m % 2, 4:8, :], four(src)[0:CHUNK, :, :]).then_inc(t_free[n % 2], 1)
                else:
                    copy(yT[:, 4 * c:4 * c + 4, j * P:(j + 1) * P], four(src)).then_inc(t_free[n % 2], 1)

            actq.wait_ge(ld_small, 32)
            for t in range(len(UNITS) + 1):
                if t < len(UNITS) and UNITS[t] in N_SCORE:
                    softmax(UNITS[t])
                if t:
                    evac_odd(UNITS[t - 1])

            for s in range(NT + 3):
                j = s - 2
                if 0 <= j < NT:
                    for c in range(2):
                        evac(("p8", j, c), probT[:, 0, 4 * c:4 * c + 4, :], four)
                j = s - 1
                if 0 <= j < NT:
                    for c in range(2):
                        evac(("h1", j, c), h1T[:, j % 2, 4 * c:4 * c + 4, :], four)
                    actq.wait_ge(qm_full, j + 1)
                    nc.scalar.mul(qm[:, :, :], four(psM[:, :]), MEM_DIM ** -0.5).then_inc(qm_ready, 1)
                j = s - 2
                if 0 <= j < NT:
                    evac(("o8", j, 0), omT[:, :, :], four)
                j = s - 1
                if 0 <= j < NT:
                    actq.wait_ge(nm8_ready, j + 1)
                    for h in range(MEM_HEADS):
                        ins = nc.scalar.activation(prob[:, 0, h * N_MEM:(h + 1) * N_MEM], psS[:, 0, h * N_MEM:(h + 1) * N_MEM], ACT.Exp,
                                                   bias=neg_max[:, j % 2, h:h + 1], accum_out=sums_x[:, h:h + 1])
                    ins.then_inc(p8_ready, 1)
                j = s - 3
                if 0 <= j < NT:
                    for c in range(2):
                        evac(("h2", j, c), h2T[:, 4 * c:4 * c + 4, :], four)
                    actq.wait_ge(r_full, j + 1)
                    nc.scalar.copy(logits[:, j, :], psN[:, 0:ROUTE]).then_inc(r_ready, 1)
            actq.wait_ge(g_exp_in, 1)
            nc.scalar.activation(eg[:, :, :], gl[:, :, :], ACT.Exp).then_inc(g_exp_out, 1)
            actq.wait_ge(g_exp_in, 2)
            nc.scalar.activation(t8[3][:, :], t8[2][:, :], ACT.Exp).then_inc(g_exp_out, 1)
            actq.wait_ge(items_ready, 1)
            n_items = actq.value_load(n_items_t[0:1, 0:1], min_val=1, max_val=MAX_ITEMS)

            def evac_x(s, count):
                actq.wait_ge(xT_full[s], count * 2 - 1)
                nc.scalar.copy(xgT[s][:, 0:4, :], four(psT[:, 0, :]))
                actq.wait_ge(xT_full[s], count * 2)
                nc.scalar.copy(xgT[s][:, 4:8, :], four(psT[:, 1, :])).then_inc(xT_ready[s], 1)

            evac_x(0, 1)
            with actq.Fori(0, MAX_ITEMS // 2) as r:
                for s in range(2):
                    i = r * 2 + s
                    kind = actq.value_load(item_kind[0:1, bass.ds(i, 1)], min_val=0, max_val=WIDE)
                    with actq.If(kind > NO_ITEM):
                        actq.wait_ge(gu_full, i + 1)
                        nc.scalar.activation(gate_s[:, :], bank(2), ACT.Silu).then_inc(silu_done, 1)
                    with actq.If(kind < NO_ITEM):
                        actq.wait_ge(gu_full, i + 1)
                        nc.scalar.activation(gate_s[HALF_P:P, :], bank(2)[0:HALF_P, :], ACT.Silu).then_inc(silu_done, 1)
                    with actq.If(i + 1 < n_items):
                        evac_x(1 - s, r + (1 + s))
                    with actq.If(i < n_items):
                        actq.wait_ge(aT_full, i + 1)
                        nc.scalar.copy(actT[s][:, :, :], four(psM[:, :])).then_inc(aT_ready, 1)
            actq.wait_ge(ld_gb1, 96)
            nc.scalar.copy(psT[:, :, :], gb1[:, 0, :].rearrange("p (b n) -> p b n", b=2)).then_inc(g_in_psum, 1)

        @block.vector
        def _(dve):
            settled = [0]

            def settle(ins):
                settled[0] += 1
                ins.then_inc(v_done, 1)
                dve.wait_ge(v_done, settled[0])

            V = nc.vector
            four = lambda v: v.rearrange("p (k n) -> p k n", n=P)

            def layer_norm(key, t, gb):
                n = LN_NO[key]
                r = n % 2
                V.bn_stats(stats[:, r, 0, :], t[:, 0:512])
                settle(V.bn_stats(stats[:, r, 1, :], t[:, 512:D]))
                settle(V.bn_aggr(mv[:, r, :], stats[:, r, :, :]))
                V.tensor_scalar(var[:, n:n + 1], mv[:, r, 1:2], LN_EPS, None, ALU.add).then_inc(var_ready, 1)
                settle(V.scalar_tensor_tensor(t, t, mv[:, r, 0:1], gb[:, 0, :], ALU.subtract, ALU.mult))
                dve.wait_ge(rstd_ready, n + 1)
                V.scalar_tensor_tensor(t, t, rstd[:, n:n + 1], gb[:, 1, :], ALU.mult, ALU.add).then_inc(ln_done, 1)

            def reduce_angle(ang, t, turns, phase):
                settle(V.tensor_scalar(t, ang, 1 / (2 * np.pi), turns, ALU.mult, ALU.add))
                settle(V.tensor_scalar(t, t, ROUNDER, None, ALU.add))
                settle(V.tensor_scalar(t, t, ROUNDER, None, ALU.subtract))
                for part in (TWO_PI_1, TWO_PI_2, TWO_PI_3):
                    settle(V.scalar_tensor_tensor(ang, t, -part, ang, ALU.mult, ALU.add))
                settle(V.tensor_scalar(ang, ang, phase, 3.1415925, ALU.add, ALU.min))
                return V.tensor_scalar(ang, ang, -3.1415925, None, ALU.max)

            dve.wait_ge(ld_gb1, 32)
            for j in range(NT):
                dve.wait_ge(ld_x[j % 4], 16 * (j // 4 + 1))
                layer_norm(("in", j), hring[:, j % 4, :], gb1)
            dve.wait_ge(ld_pos, 64)
            lo = slice(NOPE, P)
            settle(V.tensor_scalar(cs[lo, :], pos_all[lo, :], rope_f[lo, 0:1], None, ALU.mult))
            reduce_angle(cs[lo, :], trig_t[lo, :], rope_f[lo, 1:2], rope_f[lo, 2:3]).then_inc(trig_ready, 1)
            settle(V.tensor_copy(posf_t[:, :], pos_t[:, :]))
            for c, (turns, phase) in enumerate(((0.25, np.pi / 2), (0.0, 0.0))):
                settle(V.tensor_tensor(kang[:, c, :, :], posf_t[:, :].unsqueeze(2).to_broadcast([P, NT, 16]),
                                       inv_b[:, :].unsqueeze(1).to_broadcast([P, NT, 16]), ALU.mult))
                last = reduce_angle(kang[:, c, :, :], kang_t[:, :, :], turns, phase)
            last.then_inc(trig_ready, 1)
            dve.wait_ge(ss_full, 1)
            V.tensor_scalar(ms[:, 0:8], bank(2)[:, 0:8], 1.0 / Q_LORA, RMS_EPS, ALU.mult, ALU.add)
            V.tensor_scalar(ms[:, 8:16], bank(2)[:, 8:16], 1.0 / KV_LORA, RMS_EPS, ALU.mult, ALU.add).then_inc(ms_ready, 1)
            for hf in range(2):
                cols = slice(hf * HALF, (hf + 1) * HALF)
                dve.wait_ge(rb_full, 2 * hf + 1)
                for c in range(2):
                    V.tensor_tensor(cq[:, c, cols], cq[:, c, cols], bank(2 + 2 * hf), ALU.mult).then_inc(cqn_ready, 1)
                dve.wait_ge(rb_full, 2 * hf + 2)
                V.tensor_tensor(ckv[:, cols], ckv[:, cols], bank(3 + 2 * hf), ALU.mult).then_inc(cqn_ready, 1)
            dve.wait_ge(trig_done, 2)
            dve.wait_ge(kv_free, NT)
            x1, x2 = krvs[:, :, 0:16], krvs[:, :, 16:ROPE]
            V.tensor_tensor(krot[:, :, 0:16], x1, kang[:, 0, :, :], ALU.mult)
            settle(V.tensor_tensor(krot_t[:, :, :], x2, kang[:, 1, :, :], ALU.mult))
            settle(V.tensor_tensor(krot[:, :, 0:16], krot[:, :, 0:16], krot_t[:, :, :], ALU.subtract))
            V.tensor_tensor(krot[:, :, 16:ROPE], x1, kang[:, 1, :, :], ALU.mult)
            settle(V.tensor_tensor(krot_t[:, :, :], x2, kang[:, 0, :, :], ALU.mult))
            V.tensor_tensor(krot[:, :, 16:ROPE], krot[:, :, 16:ROPE], krot_t[:, :, :], ALU.add).then_inc(krot_ready, 1)
            for j in range(NT):
                dve.wait_ge(vv_full, j + 1)
                V.tensor_copy(vmla[:, j, :], bank(2 + j % 4)).then_inc(vv_free, 1)

            def scores(u):
                kind, j, h = u
                n = N_SCORE[u]
                dve.wait_ge(s_full, n + 1)
                if kind == "q":
                    cos, sin = (cs[x, j * P:(j + 1) * P].unsqueeze(1).to_broadcast([ROPE, 4, P]) for x in (slice(NOPE, QK), slice(QK, P)))
                    for c in range(2):
                        ps = psS[:, n % 2, c * 512:(c + 1) * 512]
                        dst = qcat[NOPE:QK, j % 2, 4 * c:4 * c + 4, :]
                        V.tensor_tensor(dst, four(ps[NOPE:QK, :]), cos, ALU.mult)
                        settle(V.tensor_tensor(four(ps[QK:P, :]), four(ps[QK:P, :]), sin, ALU.mult))
                        V.tensor_tensor(dst, dst, four(ps[QK:P, :]), ALU.add).then_inc(rope_read, 1)
                    return
                m = N_SOFT[u]
                if kind == "m":
                    w = (j + 1) * P
                    settle(V.memset(psS[0:CHUNK, n % 2, w - CHUNK:w], MASKED))
                    V.tensor_reduce(neg_max[:, m % 4, 0:1], psS[:, n % 2, 0:w], X, ALU.max, negate=True).then_inc(mx_ready, 1)
                    return
                lo = CHUNK if j == 0 else 0
                if m >= 2:
                    prev = SOFTMAXED[m - 2]
                    dve.wait_ge(t_full, CHUNK_NO[prev, chunks_of(prev) - 1] + 1)
                biased = prob[:, m % 2, 0:GQ * BAND].rearrange("p (h w) -> p h w", w=BAND)[:, :, lo:BAND]
                raw = psS[:, n % 2, :].rearrange("p (h w) -> p h w", w=256)[:, :, lo:BAND]
                V.tensor_tensor(biased, raw, alibi[:, h * GQ:(h + 1) * GQ, lo:BAND], ALU.add).then_inc(s_free[n % 2], 1)
                dve.wait_ge(s_free[n % 2], n // 2 + 1)
                hs = slice(h * GQ, (h + 1) * GQ)
                settle(V.tensor_reduce(rmax[:, 0:GQ], biased, X, ALU.max))
                settle(V.tensor_tensor(rmax[:, 0:GQ], rmax[:, 0:GQ], sink[:, j % 2, hs], ALU.max))
                settle(V.tensor_tensor(sink_d[:, j % 2, hs], sink[:, j % 2, hs], rmax[:, 0:GQ], ALU.subtract))
                V.tensor_scalar(neg_max[:, m % 4, :], rmax[:, 0:GQ], -1.0, None, ALU.mult).then_inc(mx_ready, 1)

            def evac_even(u):
                kind, j, h = u
                for c in range(chunks_of(u)):
                    n = CHUNK_NO[u, c]
                    if n % 2:
                        continue
                    m = N_SOFT.get(u)
                    if m is not None and m >= 2:
                        dve.wait_ge(pv_full, m - 1)
                    dve.wait_ge(t_full, n + 1)
                    src = four(psT[:, n % 2, :])
                    if kind == "m":
                        k = min(4, j + 1 - 4 * c)
                        ins = V.tensor_copy(probT[:, m % 2, 4 * c:4 * c + k, :], src[:, 0:k, :])
                    elif kind == "s" and c == 0:
                        ins = V.tensor_copy(probT[:, m % 2, 0:4, :], src)
                    elif kind == "s":
                        ins = V.tensor_copy(probT[CHUNK:P, m % 2, 4:8, :], src[0:CHUNK, :, :])
                    else:
                        ins = V.tensor_copy(yT[:, 4 * c:4 * c + 4, j * P:(j + 1) * P], src)
                    ins.then_inc(t_free[n % 2], 1)

            def divide(u):
                kind, j, h = u
                heads = lambda v: v.rearrange("p (h d) -> p h d", d=NOPE)
                rb = rinv[:, :].unsqueeze(2).to_broadcast([P, 8, NOPE])
                dve.wait_ge(pv_full, N_SOFT[u] + 1)
                if kind == "m" and h == MLA_HEADS - 1:
                    if j:
                        dve.wait_ge(t_full, CHUNK_NO[("y", j - 1, 0), 1] + 1)
                    settle(V.reciprocal(rinv[:, :], sums_m[:, j % 2, :]))
                    settle(V.tensor_tensor(heads(y[:, 0:512]), heads(psM[:, :]), rb, ALU.mult))
                elif kind == "s" and h == 1:
                    dve.wait_ge(p_ready, 2 * j + 2)
                    settle(V.tensor_tensor(rinv[:, :], sums_s[:, j % 2, :], sink_e[:, j % 2, :], ALU.add))
                    settle(V.reciprocal(rinv[:, :], rinv[:, :]))
                    V.tensor_tensor(heads(y[:, 512:D]), heads(psN[:, :]), rb, ALU.mult).then_inc(y_ready, 1)
                    dve.wait_ge(y_ready, j + 1)

            dve.wait_ge(ld_alibi, 16)
            dve.wait_ge(ld_small, 32)
            for t in range(len(UNITS) + 2):
                if t < len(UNITS) and UNITS[t] in N_SCORE:
                    scores(UNITS[t])
                if 0 < t <= len(UNITS):
                    evac_even(UNITS[t - 1])
                if t >= 2 and UNITS[t - 2][0] in "ms" and UNITS[t - 2][2] == (7 if UNITS[t - 2][0] == "m" else 1):
                    divide(UNITS[t - 2])

            def residual(key, gb):
                n, j = PROJ_NO[key], key[1]
                h = hring[:, j % 4, :]
                for c in range(2):
                    dve.wait_ge(ae_full, 2 * n + c + 1)
                    ins = V.scalar_tensor_tensor(h[:, c * 512:(c + 1) * 512], h[:, c * 512:(c + 1) * 512], ALPHA,
                                                 bank(4 + c), ALU.mult, ALU.add)
                ins.then_inc(ae_free, 1)
                dve.wait_ge(ae_free, n + 1)
                layer_norm(key, h, gb)

            V.memset(ones[:, :], 1.0)
            dve.wait_ge(ld_gb1, 64)
            for s in range(NT + 3):
                if s < NT:
                    dve.wait_ge(ld_h0[s % 4], 16 * (s // 4 + 1))
                    residual(("A", s), gb1)
                j = s - 2
                if 0 <= j < NT:
                    dve.wait_ge(o8_full, j + 1)
                    settle(V.reciprocal(rinv[:, 0:4], sums_x[:, :]))
                    V.tensor_tensor(four(om[:, :]), four(psN[:, :]), rinv[:, 0:4].unsqueeze(2).to_broadcast([P, 4, P]),
                                    ALU.mult).then_inc(om_ready, 1)
                    dve.wait_ge(om_ready, j + 1)
                j = s - 1
                if 0 <= j < NT:
                    dve.wait_ge(c_full, j + 1)
                    V.tensor_reduce(neg_max[:, j % 2, :], psS[:, 0, :].rearrange("p (h w) -> p h w", w=N_MEM), X, ALU.max,
                                    negate=True).then_inc(nm8_ready, 1)
                j = s - 2
                if 0 <= j < NT:
                    if j == 0:
                        dve.wait_ge(ld_gb2, 32)
                    residual(("E", j), gb2)

            dve.wait_ge(r_ready, NT)
            dve.wait_ge(ld_late, 16 * 8)
            over = lambda v, n: v.unsqueeze(2).to_broadcast([P, NT, n])
            ids = lambda n: iotas[:, 0:n].unsqueeze(1).to_broadcast([P, NT, n])
            settle(V.tensor_tensor(logits[:, :, :], logits[:, :, :], route_b[:, :].unsqueeze(1).to_broadcast([P, NT, ROUTE]), ALU.add))
            gmax, gid, behind, second_e, gprob, share = t8[0], t8[1], t8[2], t8[3], t8[8], t8[9]
            lg, le = logits[:, :, 0:N_GROUPS], logits[:, :, N_GROUPS:ROUTE]
            settle(V.tensor_reduce(gmax[:, :], lg, X, ALU.max))
            V.tensor_tensor(gl[:, :, :], lg, over(gmax[:, :], N_GROUPS), ALU.subtract).then_inc(g_exp_in, 1)

            def first_at(out, values, top, n, tmp, idx):
                settle(V.tensor_tensor(tmp, values, over(top, n), ALU.is_equal))
                settle(V.tensor_tensor(tmp, tmp, ids(n), ALU.mult))
                settle(V.tensor_reduce(idx, tmp, X, ALU.min))
                settle(V.tensor_tensor(out, ids(n), over(idx, n), ALU.is_equal))

            first_at(gpen[:, :, :], lg, gmax[:, :], N_GROUPS, gpen[:, :, :], gid[:, :])
            settle(V.tensor_scalar(gpen[:, :, :], gpen[:, :, :], 1.0, -MASKED, ALU.subtract, ALU.mult))
            for g in range(N_GROUPS):
                x = slice(g * PER_GROUP, (g + 1) * PER_GROUP)
                last = V.tensor_tensor(elm[:, :, x], le[:, :, x], gpen[:, :, g:g + 1].to_broadcast([P, NT, PER_GROUP]), ALU.add)
            settle(last)
            m1, i1, m2, i2 = t8[4], t8[5], t8[6], t8[7]
            settle(V.tensor_reduce(m1[:, :], elm[:, :, :], X, ALU.max))
            first_at(oh1[:, :, :], elm[:, :, :], m1[:, :], N_EXP, eqx[:, :, :], i1[:, :])
            settle(V.scalar_tensor_tensor(elm[:, :, :], oh1[:, :, :], 100 * MASKED, elm[:, :, :], ALU.mult, ALU.add))
            settle(V.tensor_reduce(m2[:, :], elm[:, :, :], X, ALU.max))
            first_at(oh2[:, :, :], elm[:, :, :], m2[:, :], N_EXP, eqx[:, :, :], i2[:, :])
            V.tensor_tensor(oh_sum[:, :, :], oh1[:, :, :], oh2[:, :, :], ALU.add).then_inc(oh_ready, 1)
            dve.wait_ge(g_exp_out, 1)
            V.tensor_tensor(behind[:, :], m2[:, :], m1[:, :], ALU.subtract).then_inc(g_exp_in, 1)
            settle(V.tensor_reduce(gprob[:, :], eg[:, :, :], X, ALU.add))
            settle(V.reciprocal(gprob[:, :], gprob[:, :]))
            dve.wait_ge(g_exp_out, 2)
            settle(V.tensor_scalar(share[:, :], second_e[:, :], 1.0, None, ALU.add))
            settle(V.reciprocal(share[:, :], share[:, :]))
            settle(V.tensor_tensor(gprob[:, :], gprob[:, :], share[:, :], ALU.mult))
            V.tensor_copy(gates[:, :, 0], gprob[:, :])
            V.tensor_tensor(gates[:, :, 1], gprob[:, :], second_e[:, :], ALU.mult)
            dve.wait_ge(rank_full, 2)
            V.tensor_copy(rank[:, :, :], bank(2)[:, 0:NT * N_EXP].rearrange("p (j e) -> p j e", e=N_EXP))
            settle(V.tensor_copy(tot[:, :, :], bank(3)[:, 0:NT * N_EXP].rearrange("p (j e) -> p j e", e=N_EXP)))
            settle(V.tensor_reduce(cnt[:, :], tot[:, :, :].rearrange("p j e -> p e j"), X, ALU.add))
            nblk_i = nblk[:, :].bitcast(I32)
            settle(V.tensor_scalar(nblk_i, cnt[:, :], float(P - 1), None, ALU.add))
            settle(V.tensor_scalar(nblk_i, nblk_i, 7, None, ALU.logical_shift_right))
            settle(V.tensor_copy(nblk_f[:, :], nblk_i))
            settle(V.tensor_tensor_scan(incl[:, :], ones[:, 0:N_EXP], nblk_f[:, :], 0.0, ALU.mult, ALU.add))
            settle(V.tensor_tensor(first_block[:, :], incl[:, :], nblk_f[:, :], ALU.subtract))
            V.tensor_scalar(item_cmp[:, 0, :], incl[:, :], item_no[:, 0:1], None, ALU.is_le)
            V.tensor_scalar(item_cmp[:, 2, :], first_block[:, :], item_no[:, 0:1], None, ALU.is_gt)
            settle(V.scalar_tensor_tensor(row_end[:, :], first_block[:, :], float(P), cnt[:, :], ALU.mult, ALU.add))
            settle(V.tensor_scalar(item_cmp[:, 1, :], row_end[:, :], item_no[:, 1:2], None, ALU.is_gt))
            settle(V.tensor_reduce(item_sum[:, 0:3], item_cmp[:, :, :], X, ALU.add))
            V.tensor_scalar(item_cols[:, 0:1], item_sum[:, 0:1], float(N_EXP - 1), None, ALU.min)
            V.tensor_tensor(item_sum[:, 1:2], item_sum[:, 1:2], item_sum[:, 2:3], ALU.subtract)
            settle(V.tensor_copy(item_sum[:, 3:4], item_cmp[:, 0, N_EXP - 1:N_EXP]))
            V.scalar_tensor_tensor(item_cols[:, 1:2], item_sum[:, 1:2], float(WIDE), item_sum[:, 3:4], ALU.mult, ALU.add).then_inc(item_cols_ready, 1)
            V.tensor_copy(n_items_t[:, :], incl[0:1, N_EXP - 1:N_EXP])
            settle(V.tensor_scalar(place[:, 0, :], first_block[:, :], float(P), None, ALU.mult))
            for j in range(1, NT):
                settle(V.tensor_tensor(place[:, j, :], place[:, j - 1, :], tot[:, j - 1, :], ALU.add))
                if j == 4:
                    dve.wait_ge(items_full, 1)
                    V.tensor_copy(item_exp[:, :], bank(5)[0:1, 0:MAX_ITEMS])
                    V.tensor_copy(item_kind[:, :], bank(5)[0:1, P:P + MAX_ITEMS + 2]).then_inc(items_ready, 1)
            settle(V.tensor_tensor(place[:, :, :], place[:, :, :], rank[:, :, :], ALU.add))
            for k, oh in enumerate((oh1, oh2)):
                settle(V.tensor_tensor(oh[:, :, :], oh[:, :, :], place[:, :, :], ALU.mult))
                settle(V.tensor_reduce(posf[:, :, k], oh[:, :, :], X, ALU.add))
            settle(V.tensor_copy(posi[:, :, :], posf[:, :, :]))
            settle(V.tensor_scalar(posi[:, :, :], posi[:, :, :], 7, None, ALU.logical_shift_right))
            settle(V.tensor_copy(posd[:, :, :], posi[:, :, :]))
            settle(V.scalar_tensor_tensor(posf[:, :, :], posd[:, :, :], -float(P), posf[:, :, :], ALU.mult, ALU.add))
            for j in range(NT):
                for k in range(TOP_K):
                    V.tensor_scalar(mark_row[:, j, k, :], iotas[:, N_EXP:], posf[:, j, k:k + 1], None, ALU.is_equal)
                    for f, v in enumerate((choice_no, gates)):
                        ins = V.tensor_scalar(mark_item[:, j, k, f, :], iotas[:, N_EXP:N_EXP + MAX_ITEMS], posd[:, j, k:k + 1],
                                              v[:, j, k:k + 1], ALU.is_equal, ALU.mult)
                    ins.then_inc(marks_ready, 1)
            dve.wait_ge(table_full, 1)
            numbers = bank(4)[:, 0:MAX_ITEMS]
            V.tensor_copy(table[:, 0:MAX_ITEMS, 2].bitcast(F32), bank(4)[:, MAX_ITEMS:2 * MAX_ITEMS])
            settle(V.tensor_scalar(dest[:, :], numbers, 0.0, float(NO_ROW), ALU.is_equal, ALU.mult))
            settle(V.scalar_tensor_tensor(table[:, 0:MAX_ITEMS, 1], numbers, -1.0, dest[:, :], ALU.add, ALU.add))
            V.tensor_scalar(table[:, 0:MAX_ITEMS, 0], table[:, 0:MAX_ITEMS, 1], 1, None, ALU.logical_shift_right).then_inc(table_ready, 1)

            dve.wait_ge(items_ready, 1)
            dve.wait_ge(pool_const, 8)
            n_items = dve.value_load(n_items_t[0:1, 0:1], min_val=1, max_val=MAX_ITEMS)

            def item_results(s, i, before):
                kind = dve.value_load(item_kind[0:1, bass.ds(i, 1)], min_val=0, max_val=WIDE)
                gate = tab_y[s][:, 1:2].bitcast(F32)

                def waits_for_result():
                    if not isinstance(before, int):
                        dve.wait_ge(ye_stored[s], before * 16)
                    dve.wait_ge(places_ready[s], before + 1)
                    dve.wait_ge(y_full, i * 2 + 1)

                with dve.If(kind > NO_ITEM):
                    dve.wait_ge(silu_done, i + 1)
                    V.tensor_tensor(act[s][:, :], gate_s[:, :], bank(3), ALU.mult).then_inc(act_ready, 1)
                    waits_for_result()
                    V.tensor_scalar(ye[s][:, 0:512], bank(4), gate, None, ALU.mult)
                    dve.wait_ge(y_full, i * 2 + 2)
                    V.tensor_scalar(ye[s][:, 512:D], bank(5), gate, None, ALU.mult).then_inc(ye_ready[s], 1)
                with dve.If(kind < NO_ITEM):
                    dve.wait_ge(silu_done, i + 1)
                    V.tensor_tensor(act[s][HALF_P:P, :], gate_s[HALF_P:P, :], bank(3)[HALF_P:P, :], ALU.mult).then_inc(act_ready, 1)
                    waits_for_result()
                    V.tensor_scalar(ye[s][0:HALF_P, 0:512], bank(4)[0:HALF_P, :], gate[0:HALF_P], None, ALU.mult)
                    dve.wait_ge(y_full, i * 2 + 2)
                    V.tensor_scalar(ye[s][0:HALF_P, 512:D], bank(5)[HALF_P:P, :], gate[0:HALF_P], None, ALU.mult).then_inc(ye_ready[s], 1)

            for s in range(2):
                item_results(s, s, 0)
            with dve.Fori(1, MAX_ITEMS // 2) as r:
                for s in range(2):
                    item_results(s, r * 2 + s, r)
            dve.wait_ge(ld_gb1, 96)
            dve.wait_ge(ld_h2, 64)
            dve.wait_ge(g_in_psum, 1)
            for t in range(NT + 2):
                if t < NT:
                    dve.wait_ge(ld_pair[t], 16)
                    V.scalar_tensor_tensor(h2_at(t), h2_at(t), ALPHA, pair[t][:, 0, :], ALU.mult, ALU.add).then_inc(first_added, 1)
                if 0 <= t - 1 < NT:
                    n = LN_NO["out", t - 1]
                    r = n % 2
                    dve.wait_ge(both_added, t)
                    V.bn_stats(stats[:, r, 0, :], h2_at(t - 1)[:, 0:512])
                    settle(V.bn_stats(stats[:, r, 1, :], h2_at(t - 1)[:, 512:D]))
                    settle(V.bn_aggr(mv[:, r, :], stats[:, r, :, :]))
                    V.tensor_scalar(var[:, n:n + 1], mv[:, r, 1:2], LN_EPS, None, ALU.add).then_inc(var_ready, 1)
                if t - 2 >= 0:
                    n = LN_NO["out", t - 2]
                    h = h2_at(t - 2)
                    dve.wait_ge(rstd_ready, n + 1)
                    settle(V.tensor_scalar(h, h, mv[:, n % 2, 0:1], rstd[:, n:n + 1], ALU.subtract, ALU.mult))
                    V.tensor_tensor(h, h, g_psum, ALU.mult).then_inc(scaled, 1)

        @block.tensor
        def _(pe):
            mm = nc.tensor.matmul
            T = nc.tensor.transpose

            def transposes(key, blocks, rows_out=P):
                n = CHUNK_NO[key]
                if n >= 2:
                    pe.wait_ge(t_free[n % 2], n // 2)
                for i, b in enumerate(blocks):
                    ins = T(psT[0:rows_out, n % 2, i * P:(i + 1) * P], b, ident[:, :])
                ins.then_inc(t_full, 1)

            def evacuated(key):
                n = CHUNK_NO[key]
                pe.wait_ge(t_free[n % 2], n // 2 + 1)

            pe.wait_ge(ld_ident, 16)
            pe.wait_ge(ld_mem, 16)
            for t in range(2):
                for c in range(2):
                    transposes(("mem", t, c), [mem_sb[:, t, (4 * c + i) * P:(4 * c + i + 1) * P] for i in range(4)])
            pe.wait_ge(ld_mk, 16)
            for b in range(2):
                pe.wait_ge(t_free[b], 2)
            for i in range(2):
                for hh in range(2):
                    h = 2 * i + hh
                    for k in range(KC):
                        ins = mm(bank(2 + i)[:, hh * N_MEM:(hh + 1) * N_MEM], w_mk[:, k, h * P:(h + 1) * P], memT[:, k, :],
                                 start=(k == 0), stop=(k == KC - 1))
                ins.then_inc(mem_full, 1)
            pe.wait_ge(ld_mv, 16)
            for t in range(2):
                for k in range(KC):
                    ins = mm(bank(4 + t), memT[:, k, t * P:(t + 1) * P], w_mv[:, k, :], start=(k == 0), stop=(k == KC - 1))
                ins.then_inc(mem_full, 1)
            for hf in range(2):
                for j in range(4 * hf, 4 * hf + 4):
                    pe.wait_ge(ln_done, LN_NO["in", j] + 1)
                    for c in range(2):
                        transposes(("x", j, c), [hring[:, j % 4, (4 * c + i) * P:(4 * c + i + 1) * P] for i in range(4)])
                for c in range(2):
                    n = CHUNK_NO["x", 4 * hf + 3, c]
                    pe.wait_ge(t_free[n % 2], n // 2 + 1)
                if hf == 0:
                    pe.wait_ge(ld_win, 64)
                cols = slice(hf * HALF, (hf + 1) * HALF)
                for c in range(8):
                    i = hf * 8 + c
                    if i < 4:
                        pe.wait_ge(mem_free, i + 1)
                    else:
                        pe.wait_ge(pj_free, i - 3)
                    for k in range(KC):
                        ins = mm(bank(2 + i % 4), w_in[:, k, c * P:(c + 1) * P], hT[:, k, cols], start=(k == 0), stop=(k == KC - 1))
                    ins.then_inc(pj_full, 1)
                for j in range(4 * hf, 4 * hf + 4):
                    if j >= 2:
                        pe.wait_ge(kv_free, j - 1)
                    for k in range(KC):
                        ins = mm(bank(6 + j % 2)[:, 0:ROPE + P], hT[:, k, j * P:(j + 1) * P], w_in[:, k, C_KR:IN_COLS],
                                 start=(k == 0), stop=(k == KC - 1))
                    ins.then_inc(kv_full, 1)
            pe.wait_ge(sq_ready, 6)
            pe.wait_ge(pj_free, 16)
            pe.wait_ge(pool_const, 2)
            for j in range(NT):
                tok = slice(j * P, (j + 1) * P)
                for c in range(2):
                    mm(bank(2)[:, j:j + 1], sq[:, c, tok], one_col[:, :], start=(c == 0), stop=(c == 1))
            for j in range(NT):
                ins = mm(bank(2)[:, 8 + j:9 + j], sq[:, 2, j * P:(j + 1) * P], one_col[:, :], start=True, stop=True)
            ins.then_inc(ss_full, 1)
            pe.wait_ge(rms_ready, 1)
            for hf in range(2):
                for kv in range(2):
                    for i in range(4):
                        c = kv * 8 + hf * 4 + i
                        ins = mm(bank(2 + 2 * hf + kv)[:, i * P:(i + 1) * P], rms[:, c:c + 1].to_broadcast([P, P]), ident[:, :],
                                 start=True, stop=True)
                    ins.then_inc(rb_full, 1)
            pe.wait_ge(wq_ready, 3)
            pe.wait_ge(kv_free, NT)
            pe.wait_ge(cqn_ready, 6)
            for i in range(8):
                p, hf = i // 2, i % 2
                if i >= 2:
                    pe.wait_ge(kn_free, i - 1)
                mm(bank(6 + i % 2), wukv[:, 0, 2 * p:2 * p + 2, :].rearrange("p h n -> p (h n)"), ckv[:, hf * HALF:(hf + 1) * HALF],
                   start=True, stop=True).then_inc(kn_full, 1)
            for j in range(NT):
                if j >= 4:
                    pe.wait_ge(vv_free, j - 3)
                mm(bank(2 + j % 4), ckv[:, j * P:(j + 1) * P], wukv[:, 1, :, :].rearrange("p h n -> p (h n)"), start=True, stop=True).then_inc(vv_full, 1)
            pe.wait_ge(krot_ready, 1)
            for c in range(2):
                transposes(("kpe", 0, c), [krot[:, 4 * c + i, :] for i in range(4)], rows_out=ROPE)
            pe.wait_ge(vv_free, NT)
            pe.wait_ge(kn_free, 8)
            for c in range(2):
                evacuated(("kpe", 0, c))

            def score(u):
                kind, j, h = u
                n = N_SCORE[u]
                tok = slice(j * P, (j + 1) * P)
                if n >= 2:
                    pe.wait_ge(s_free[n % 2], n // 2)
                ps = psS[:, n % 2, :]
                if kind == "q":
                    for g in range(MLA_HEADS):
                        for k in range(2):
                            ins = mm(ps[:, g * P:(g + 1) * P], wq[:, k, g, :], cq[:, k, tok], start=(k == 0), stop=(k == 1))
                elif kind == "m":
                    w = (j + 1) * P
                    if h == 0:
                        nq = N_SCORE["q", j, 0]
                        pe.wait_ge(s_free[nq % 2], nq // 2 + 1)
                        pe.wait_ge(rope_read, 2 * j + 2)
                    if j == 0 and h:
                        pe.wait_ge(kpe_all, h)
                    for c in range(0, w, 512):
                        e = min(w, c + 512)
                        ins = mm(ps[:, c:e], qcat[:, j % 2, h, :], kcat[:, h, c:e], start=True, stop=True)
                else:
                    lo = CHUNK if j == 0 else 0
                    rows_ = slice(h * SWA_DIM, (h + 1) * SWA_DIM)
                    for i in range(GQ):
                        ins = mm(ps[:, i * 256 + lo:i * 256 + BAND], qs[rows_, i, tok], ks[rows_, j * P - CHUNK + lo:(j + 1) * P],
                                 start=True, stop=True)
                ins.then_inc(s_full, 1)

            def turn(u):
                kind, j, h = u
                m = N_SOFT.get(u)
                if kind == "m":
                    n = N_SCORE[u]
                    pe.wait_ge(s_free[n % 2], n // 2 + 1)
                    for c in range(chunks_of(u)):
                        transposes((u, c), [prob[:, m % 2, k * P:(k + 1) * P] for k in range(4 * c, min(4 * c + 4, j + 1))])
                elif kind == "s":
                    pe.wait_ge(p_ready, 2 * j + h + 1)
                    transposes((u, 0), [prob[:, m % 2, i * BAND + CHUNK:(i + 1) * BAND] for i in range(GQ)])
                    if j:
                        transposes((u, 1), [prob[:, m % 2, i * BAND:i * BAND + CHUNK] for i in range(GQ)], rows_out=CHUNK)
                elif kind == "y":
                    pe.wait_ge(y_ready, j + 1)
                    for c in range(2):
                        transposes((u, c), [y[:, (4 * c + i) * P:(4 * c + i + 1) * P] for i in range(4)])

            def weigh(u):
                kind, j, h = u
                if kind not in "ms":
                    return
                m = N_SOFT[u]
                for c in range(chunks_of(u)):
                    evacuated((u, c))
                if kind == "m":
                    if h == 0 and j:
                        pe.wait_ge(y_ready, j)
                    for k in range(j + 1):
                        ins = mm(psM[:, h * MLA_V:(h + 1) * MLA_V], probT[:, m % 2, k, :], vmla[:, k, h * MLA_V:(h + 1) * MLA_V],
                                 start=(k == 0), stop=(k == j))
                else:
                    dims = slice(ROPE + h * SWA_DIM, ROPE + (h + 1) * SWA_DIM)
                    for i in range(GQ):
                        out = psN[:, (h * GQ + i) * SWA_DIM:(h * GQ + i + 1) * SWA_DIM]
                        ins = mm(out, probT[:, m % 2, i, :], krvs[:, j, dims], start=True, stop=(j == 0))
                        if j:
                            ins = mm(out, probT[CHUNK:P, m % 2, 4 + i, :], krvs[CHUNK:P, j - 1, dims], start=False, stop=True)
                ins.then_inc(pv_full, 1)

            for t in range(len(UNITS) + 2):
                if t < len(UNITS) and UNITS[t] in N_SCORE:
                    score(UNITS[t])
                if 0 < t <= len(UNITS):
                    turn(UNITS[t - 1])
                if t >= 2:
                    weigh(UNITS[t - 2])

            def project(key, stationary, weights, steps):
                n = PROJ_NO[key]
                if n:
                    pe.wait_ge(ae_free, n)
                for c in range(2):
                    for k in range(steps):
                        ins = mm(bank(4 + c), stationary(k), weights[:, k, c * 512:(c + 1) * 512], start=(k == 0), stop=(k == steps - 1))
                    ins.then_inc(ae_full, 1)

            for s in range(2):
                pe.wait_ge(s_free[s], FREE_S[s])
            pe.wait_ge(y_ready, NT)
            for c in range(2):
                evacuated((("y", NT - 1, 0), c))
            pe.wait_ge(ld_wo, 32)
            for s in range(NT + 3):
                if s < NT:
                    project(("A", s), lambda k: yT[:, k, s * P:(s + 1) * P], w_o, KC)
                j = s - 2
                if 0 <= j < NT:
                    pe.wait_ge(p8_ready, j + 1)
                    for c in range(2):
                        transposes(("p8", j, c), [prob[:, 0, (4 * c + i) * P:(4 * c + i + 1) * P] for i in range(4)])
                    for c in range(2):
                        evacuated(("p8", j, c))
                    if j:
                        pe.wait_ge(om_ready, j)
                    if j >= 2:
                        pe.wait_ge(r_ready, j - 1)
                    for h in range(MEM_HEADS):
                        for t in range(2):
                            ins = mm(psN[:, h * P:(h + 1) * P], probT[:, 0, 2 * h + t, :], vm[:, t, h * P:(h + 1) * P],
                                     start=(t == 0), stop=(t == 1))
                    ins.then_inc(o8_full, 1)
                j = s - 1
                if 0 <= j < NT:
                    if j == 0:
                        pe.wait_ge(ld_wmq, 16)
                    pe.wait_ge(ln_done, LN_NO["A", j] + 1)
                    for c in range(2):
                        transposes(("h1", j, c), [hring[:, j % 4, (4 * c + i) * P:(4 * c + i + 1) * P] for i in range(4)])
                    for c in range(2):
                        evacuated(("h1", j, c))
                    if j:
                        pe.wait_ge(qm_ready, j)
                    for h in range(MEM_HEADS):
                        for k in range(KC):
                            ins = mm(psM[:, h * P:(h + 1) * P], w_mq[:, k, h * P:(h + 1) * P], h1T[:, j % 2, k, :],
                                     start=(k == 0), stop=(k == KC - 1))
                    ins.then_inc(qm_full, 1)
                j = s - 2
                if 0 <= j < NT:
                    if j == 0:
                        pe.wait_ge(ld_wmo, 16)
                    pe.wait_ge(om_ready, j + 1)
                    transposes(("o8", j, 0), [om[:, i * P:(i + 1) * P] for i in range(4)])
                    evacuated(("o8", j, 0))
                    project(("E", j), lambda k: omT[:, k, :], w_mo, MEM_HEADS)
                j = s - 1
                if 0 <= j < NT:
                    pe.wait_ge(qm_ready, j + 1)
                    if j:
                        pe.wait_ge(p8_ready, j)
                    for h in range(MEM_HEADS):
                        ins = mm(psS[:, 0, h * N_MEM:(h + 1) * N_MEM], qm[:, h, :], kmT[:, h, :], start=True, stop=True)
                    ins.then_inc(c_full, 1)
                j = s - 3
                if 0 <= j < NT:
                    pe.wait_ge(ln_done, LN_NO["E", j] + 1)
                    for c in range(2):
                        transposes(("h2", j, c), [hring[:, j % 4, (4 * c + i) * P:(4 * c + i + 1) * P] for i in range(4)])
                    for c in range(2):
                        evacuated(("h2", j, c))
                    pe.wait_ge(om_ready, min(NT, j + 2))
                    if j == 0:
                        pe.wait_ge(ld_late, 16 * 8)
                    for k in range(KC):
                        ins = mm(psN[:, 0:ROUTE], h2T[:, k, :], w_route[:, k, :], start=(k == 0), stop=(k == KC - 1))
                    ins.then_inc(r_full, 1)
            pe.wait_ge(oh_ready, 1)
            flat = oh_sum[:, :, :].rearrange("p j e -> p (j e)")
            mm(bank(2)[:, 0:NT * N_EXP], tri[:, :], flat, start=True, stop=True).then_inc(rank_full, 1)
            mm(bank(3)[:, 0:NT * N_EXP], ones[:, :], flat, start=True, stop=True).then_inc(rank_full, 1)

            pe.wait_ge(item_cols_ready, 1)
            for c in range(2):
                ins = mm(bank(5)[0:1, c * P:(c + 1) * P], item_cols[:, c:c + 1], ident[:, :], start=True, stop=True)
            ins.then_inc(items_full, 1)
            for c in range(NT * TOP_K):
                j, k = divmod(c, TOP_K)
                pe.wait_ge(marks_ready, c + 1)
                ins = mm(bank(4)[:, 0:2 * MAX_ITEMS], mark_row[:, j, k, :], mark_item[:, j, k, :, :].rearrange("p f i -> p (f i)"),
                         start=(c == 0), stop=(c == NT * TOP_K - 1))
            ins.then_inc(table_full, 1)

            pe.wait_ge(items_ready, 1)
            n_items = pe.value_load(n_items_t[0:1, 0:1], min_val=1, max_val=MAX_ITEMS)

            def turn_x(s, count):
                pe.wait_ge(x_loaded[s], count * 16)
                for c in range(2):
                    for i in range(4):
                        k = 4 * c + i
                        ins = T(psT[:, c, i * P:(i + 1) * P], xg[s][:, k * P:(k + 1) * P], ident[:, :])
                    ins.then_inc(xT_full[s], 1)

            def gate_up(s, count, wide):
                pe.wait_ge(xT_ready[s], count)
                for k in range(KC):
                    if k % 4 == 0:
                        pe.wait_ge(gu_loaded[s][k // 4], count * 16)
                    for c in range(2):
                        out, x = (bank(2 + c), xgT[s][:, k, :]) if wide else (bank(2 + c)[c * HALF_P:(c + 1) * HALF_P, :], xgT[s][:, k, 0:HALF_P])
                        ins = mm(out, x, w_gu[s][:, k, c * 512:(c + 1) * 512], start=(k == 0), stop=(k == KC - 1))
                ins.then_inc(gu_full, 1)

            def turn_act(s, i):
                pe.wait_ge(act_ready, i + 1)
                for k in range(4):
                    ins = T(psM[:, k * P:(k + 1) * P], act[s][:, k * P:(k + 1) * P], ident[:, :])
                ins.then_inc(aT_full, 1)

            def down(s, i, count, wide):
                pe.wait_ge(aT_ready, i + 1)
                pe.wait_ge(dn_loaded[s], count * 16)
                for c, k in ([(c, k) for c in range(2) for k in range(4)] if wide else [(c, k) for k in range(4) for c in range(2)]):
                    out, h = (bank(4 + c), actT[s][:, k, :]) if wide else (bank(4 + c)[c * HALF_P:(c + 1) * HALF_P, :], actT[s][:, k, HALF_P:P])
                    ins = mm(out, h, w_dn[s][:, k, c * 512:(c + 1) * 512], start=(k == 0), stop=(k == 3))
                    if k == 3:
                        ins.then_inc(y_full, 1)

            def by_kind(kind, step):
                with pe.If(kind > NO_ITEM):
                    step(True)
                with pe.If(kind < NO_ITEM):
                    step(False)

            turn_x(0, 1)
            by_kind(pe.value_load(item_kind[0:1, 0:1], min_val=0, max_val=WIDE), lambda wide: gate_up(0, 1, wide))
            with pe.Fori(0, MAX_ITEMS // 2) as r:
                for s in range(2):
                    i = r * 2 + s
                    kind = pe.value_load(item_kind[0:1, bass.ds(i, 1)], min_val=0, max_val=WIDE)
                    next_kind = pe.value_load(item_kind[0:1, bass.ds(i + 1, 1)], min_val=0, max_val=WIDE)
                    with pe.If(i + 1 < n_items):
                        turn_x(1 - s, r + (1 + s))
                    with pe.If(i < n_items):
                        turn_act(s, i)
                    by_kind(next_kind, lambda wide: gate_up(1 - s, r + (1 + s), wide))
                    by_kind(kind, lambda wide: down(s, i, r + 1, wide))


def constants():
    inv = (10000.0 ** (-np.arange(0, ROPE, 2) / ROPE)).astype(np.float32)
    ident = np.eye(P, dtype=np.float32)
    tri = np.triu(np.ones((P, P), np.float32), 1)
    i, w = np.arange(P)[:, None], np.arange(BAND)[None, :] - CHUNK
    seen = (w // CHUNK <= i // CHUNK) & (w // CHUNK >= i // CHUNK - 1)
    slopes = 2.0 ** (-8.0 * np.arange(1, SWA_HEADS + 1) / SWA_HEADS)
    alibi = np.where(seen[:, None, :], -slopes[None, :, None] * np.abs(i - w)[:, None, :], MASKED)
    rope = np.zeros((P, 4), np.float32)
    rope[:, 0] = inv[np.arange(P) % 16]
    rope[NOPE:QK, 1], rope[NOPE:QK, 2] = 0.25, np.pi / 2
    p, j, k = np.arange(P)[:, None, None], np.arange(NT)[None, :, None], np.arange(TOP_K)[None, None, :]
    choice = (TOP_K * (j * P + p) + k + 1).astype(np.float32)
    item = np.stack([np.arange(P), P * np.arange(P) + P // 2], 1).astype(np.float32)
    iotas = np.concatenate([np.arange(N_EXP) - 64.0, np.arange(P)])[None, :]
    return {"c_ident": ident, "c_tri": tri, "c_alibi": alibi.reshape(P, -1).astype(np.float32), "c_rope": rope,
            "c_inv": inv[None, :], "c_choice": choice.reshape(P, -1), "c_item": item, "c_iotas": iotas.astype(np.float32)}


_TWO_DIM = ["x", "positions", "mem", "w_in", "w_uq", "w_ukv", "w_o", "w_mq", "w_mk", "w_mv", "w_mo", "w_group", "w_expert"]
_ROWS = ["ln_in_g", "ln_in_b", "g_q", "g_kv", "sinks", "ln1_g", "ln1_b", "ln2_g", "ln2_b", "b_group", "b_expert", "ln3_g", "ln3_b"]
_THREE_DIM = ["w_gate_up", "w_down"]


def kernel(**inputs):
    import concourse.bacc as bacc
    from concourse.bass_utils import run_bass_kernel_spmd

    arrays = dict(constants())
    for n in _TWO_DIM:
        v = np.asarray(inputs[n])
        arrays[n] = v if n == "positions" else v.reshape(v.shape[-2:])
    for n in _ROWS:
        arrays[n] = np.asarray(inputs[n]).reshape(1, -1)
    for n in _THREE_DIM:
        v = np.asarray(inputs[n])
        arrays[n] = v.reshape(v.shape[-3:])
    arrays = {f"in_{n}": np.ascontiguousarray(v) for n, v in arrays.items()}
    nc = bacc.Bacc("TRN2", target_bir_lowering=False, num_devices=1)
    a = {n[3:]: nc.dram_tensor(n, v.shape, mybir.dt.from_np(v.dtype), kind="ExternalInput").ap() for n, v in arrays.items()}
    out = nc.dram_tensor("out", [SEQ, D], F32, kind="ExternalOutput").ap()
    build_program(nc, a, out)
    r = run_bass_kernel_spmd(nc, [arrays], core_ids=[0])
    return r.results[0]["out"].reshape(np.asarray(inputs["x"]).shape)
```

```python
import numpy as np
from contextlib import ExitStack

import concourse.bass as bass
from concourse import mybir

F32 = mybir.dt.float32
I32 = mybir.dt.int32
ALU = mybir.AluOpType
ACT = mybir.ActivationFunctionType
X = mybir.AxisListType.X

P = 128
SEQ, D = 1024, 1024
NT, KC = SEQ // P, D // P
HALF = 512
N_MEM, MEM_HEADS, MEM_DIM = 256, 4, 128
MLA_HEADS, NOPE, ROPE, MLA_V = 8, 64, 32, 64
QK = NOPE + ROPE
Q_LORA, KV_LORA = 256, 128
SWA_HEADS, SWA_KV, SWA_DIM, CHUNK = 8, 2, 64, 64
GQ = SWA_HEADS // SWA_KV
BAND = 3 * CHUNK
N_GROUPS, PER_GROUP = 4, 8
N_EXP = N_GROUPS * PER_GROUP
F_EXP = 512
TOP_K = 2
ROUTE = N_GROUPS + N_EXP
MAX_ITEMS = SEQ * TOP_K // P + N_EXP
HALF_P = P // 2
NARROW, NO_ITEM, WIDE = 0, 1, 2
ALPHA = 2.0 ** 0.25
LN_EPS, RMS_EPS = 1e-5, 1e-6
MASKED = -1e30
NO_ROW = 1 << 20
IN_COLS = Q_LORA + KV_LORA + ROPE + (SWA_HEADS + 2 * SWA_KV) * SWA_DIM
TWO_PI_1 = 6.28125
TWO_PI_2 = 0.0019350051879882812
TWO_PI_3 = 2 * np.pi - TWO_PI_1 - TWO_PI_2
ROUNDER = 1.5 * 2.0 ** 23
C_QS, C_KR = Q_LORA + KV_LORA, Q_LORA + KV_LORA + 640


def attention_units():
    units = [("q", 0, 0), ("q", 0, 1)]
    for j in range(NT):
        units += [("s", j, 0), ("s", j, 1)]
        for h in range(MLA_HEADS):
            if h in (0, 4) and j + 1 < NT:
                units.append(("q", j + 1, h // 4))
            units.append(("m", j, h))
    return units


UNITS = attention_units()
SCORED = [u for u in UNITS if u[0] in "qms"]
SOFTMAXED = [u for u in UNITS if u[0] in "ms"]
N_SCORE = {u: n for n, u in enumerate(SCORED)}
N_SOFT = {u: n for n, u in enumerate(SOFTMAXED)}


def chunks_of(u):
    kind, j, _ = u
    if kind == "m":
        return 1 if j < 4 else 2
    if kind == "s":
        return 1 if j == 0 else 2
    return 0


def number_chunks():
    keys = [("mem", t, c) for t in range(2) for c in range(2)]
    keys += [("x", j, c) for j in range(NT) for c in range(2)]
    keys += [("kpe", 0, c) for c in range(2)]
    keys += [(u, c) for u in UNITS for c in range(chunks_of(u))]
    for s in range(NT + 4):
        if 0 <= s - 4 < NT:
            keys += [("h2", s - 4, c) for c in range(2)]
        if 0 <= s - 2 < NT:
            keys += [("p8", s - 2, c) for c in range(2)]
        if 0 <= s - 1 < NT:
            keys += [("h1", s - 1, c) for c in range(2)]
        if 0 <= s - 2 < NT:
            keys += [("o8", s - 2, 0)]
    return {k: n for n, k in enumerate(keys)}


CHUNK_NO = number_chunks()
N_CHUNKS = len(CHUNK_NO)


def number_projections():
    uses = []
    for s in range(NT + 3):
        if s < NT:
            uses.append(("A", s))
        if 0 <= s - 2 < NT:
            uses.append(("E", s - 2))
    return {k: n for n, k in enumerate(uses)}


PROJ_NO = number_projections()
LN_NO = {("in", j): j for j in range(NT)}
LN_NO |= {(k, j): NT + n for (k, j), n in PROJ_NO.items()}
LN_NO |= {("out", j): 3 * NT + j for j in range(NT)}



def build_program(nc, a, o):
    h0_d = nc.dram_tensor("h0_scratch", [SEQ, D], F32).ap()
    h2_d = nc.dram_tensor("h2_scratch", [SEQ, D], F32).ap()
    ye_d = nc.dram_tensor("expert_rows_scratch", [SEQ * TOP_K, D], F32).ap()
    ctx = ExitStack()
    with ctx:
        kib = 1024
        base = nc.sbuf_base + (-nc.sbuf_base) % 64

        def at(name, shape, off, dt=F32):
            return nc.alloc_sbuf_tensor_at(name, shape, dt, offset=base + int(off * kib))

        def sem(name):
            return ctx.enter_context(nc.semaphore(name))

        hring = at("hring", [P, 4, D], 0)
        hT = at("hT", [P, KC, SEQ], 16)
        yT = at("yT", [P, KC, SEQ], 16)
        w_in = at("w_in_sb", [P, KC, IN_COLS], 48)
        kcat = at("kcat", [QK, MLA_HEADS, SEQ], 48)
        w_mq = at("w_mq_sb", [P, KC, 512], 48)
        w_mo = at("w_mo_sb", [P, MEM_HEADS, D], 64)
        tri = at("tri", [P, P], 80)
        ones = at("ones", [P, P], 80.5)
        iotas = at("iotas", [P, N_EXP + P], 81)
        choice_no = at("choice_no", [P, NT, TOP_K], 81.75)
        item_no = at("item_no", [P, 2], 81.875)
        route_b = at("route_b", [P, ROUTE], 82)
        w_route = at("w_route_sb", [P, KC, ROUTE], 82.25)
        w_mk = at("w_mk_sb", [P, KC, 512], 85)
        w_mv = at("w_mv_sb", [P, KC, 512], 101)
        vmla = at("vmla", [P, NT, 512], 85)
        qs = at("qs", [P, GQ, SEQ], 101)
        w_o = {c: at(f"w_o{c}", [P, D], off) for c, off in ((4, 101), (5, 105), (6, 109), (7, 113), (0, 117), (1, 121), (2, 174), (3, 85))}
        wq = at("wq", [P, 2, MLA_HEADS, P], 117)
        wukv = at("wukv", [P, 2, MLA_HEADS, NOPE], 125)
        cq = at("cq", [P, 2, SEQ], 129)
        gb2 = at("gb2", [P, 2, D], 129)
        ckv = at("ckv", [P, SEQ], 137)
        om = at("om", [P, 512], 137)
        omT = at("omT", [P, MEM_HEADS, P], 139)
        memT = at("memT", [P, KC, N_MEM], 141)
        qcat = at("qcat", [QK, 2, MLA_HEADS, P], 141)
        h1T = at("h1T", [P, 2, KC, P], 141)
        ks = at("ks", [P, SEQ], 149)
        qm = at("qm", [P, MEM_HEADS, P], 149)
        krvs = at("krvs", [P, NT, ROPE + P], 153)
        h2T = at("h2T", [P, KC, P], 153)
        mem_sb = at("mem_sb", [P, 2, D], 158)
        prob = [at(f"prob{i}", [P, D], off) for i, off in enumerate((158, 162, 196))]
        sq = at("sq", [P, 3, SEQ], 158)
        wuq = at("wuq_raw", [P, 2, MLA_HEADS, QK], 168)
        probT = [at(f"probT{i}", [P, KC, P], off) for i, off in enumerate((166, 170, 180, 137))]
        diag = at("diag", [P, 2, GQ, P], 125)
        pos_all = at("pos_all", [P, SEQ], 174, I32)
        alibi = at("alibi", [P, SWA_HEADS, BAND], 174)
        trig_t = at("trig_t", [P, SEQ], 180)
        vm = at("vm", [P, 2, 512], 184)
        kmT = at("kmT", [P, MEM_HEADS, N_MEM], 188)
        cs = at("cos_sin", [P, SEQ], 192)
        gb1 = at("gb1", [P, 2, D], 196)
        w_gu = [at("w_gu0", [P, KC, 2 * F_EXP], 16), at("w_gu1", [P, KC, 2 * F_EXP], 85)]
        w_dn = [at("w_dn0", [P, 4, D], 48), at("w_dn1", [P, 4, D], 64)]
        xg = [at("xg0", [P, D], 129), at("xg1", [P, D], 133)]
        xgT = [at("xgT0", [P, KC, P], 141), at("xgT1", [P, KC, P], 145)]
        gate_s = at("gate_s", [P, F_EXP], 137)
        act = [at("act0", [P, F_EXP], 139), at("act1", [P, F_EXP], 149)]
        actT = [at("actT0", [P, 4, P], 151), at("actT1", [P, 4, P], 153)]
        ye = [at("ye0", [P, D], 158), at("ye1", [P, D], 162)]
        table = at("table", [P, MAX_ITEMS + 3, 3], 157, I32)
        tab_x = [at("tab_x0", [P, 1], 155, I32), at("tab_x1", [P, 1], 155.25, I32)]
        tab_y = [at("tab_y0", [P, 2], 155.5, I32), at("tab_y1", [P, 2], 155.75, I32)]
        h2_first = at("h2_first", [P, 4, D], 166)
        pair = [at(f"pair{j}", [P, 2, D], 16 + 8 * j if j < 4 else 85 + 8 * (j - 4)) for j in range(NT)]
        small_at = [117.0]

        def scratch(name, shape, dt=F32):
            off = small_at[0]
            small_at[0] += -(-int(np.prod(shape[1:])) * 4 // 64) * 64 / kib
            return at(name, shape, off, dt)

        TE = [P, NT, N_EXP]
        elm, eqx, oh1, oh2, rank, place = (scratch(n, TE) for n in ("elm", "eqx", "oh1", "oh2", "rank", "place"))
        oh_sum, tot = scratch("oh_sum", TE), scratch("tot", TE)
        gl, eg, gpen = (scratch(n, [P, NT, N_GROUPS]) for n in ("gl", "eg", "gpen"))
        t8 = [scratch(f"t8_{i}", [P, NT]) for i in range(10)]
        cnt, nblk, nblk_f, incl, first_block, row_end = (scratch(n, [P, N_EXP]) for n in (
            "cnt", "nblk", "nblk_f", "incl", "first_block", "row_end"))
        posf, posi = scratch("posf", [P, NT, TOP_K]), scratch("posi", [P, NT, TOP_K], I32)
        gates = scratch("gates", [P, NT, TOP_K])
        assert small_at[0] <= 129
        item_cmp, item_sum = at("item_cmp", [P, 3, N_EXP], 158), at("item_sum", [P, 4], 159)
        item_cols = at("item_cols", [P, 2], 159.25)
        posd = at("posd", [P, NT, TOP_K], 159.5)
        dest = at("dest", [P, MAX_ITEMS], 160)
        mark_row, mark_item = at("mark_row", [P, NT, TOP_K, P], 141), at("mark_item", [P, NT, TOP_K, 2, MAX_ITEMS], 184)
        small_at[0] = 204.0
        ident = scratch("ident", [P, P])
        logits = scratch("logits", [P, NT, ROUTE])
        stats, mv = scratch("stats", [P, 2, 2, 6]), scratch("mv", [P, 2, 2])
        var, rstd = scratch("var", [P, 4 * NT]), scratch("rstd", [P, 4 * NT])
        neghalf = scratch("neghalf", [P, 16])
        neg_max = scratch("neg_max", [P, 4, 4])
        sums_m, sums_s = scratch("sums_m", [P, 2, 8]), scratch("sums_s", [P, 2, 8])
        sums_x = scratch("sums_x", [P, 4])
        sink_e, sink_d, sink = (scratch(n, [P, 2, 8]) for n in ("sink_e", "sink_d", "sink"))
        rinv, rmax = scratch("rinv", [P, 8]), scratch("rmax", [P, 4])
        one_col = scratch("one_col", [P, 1])
        gq, gkv = scratch("gq", [P, 4]), scratch("gkv", [P, 1])
        rope_f = scratch("rope_f", [P, 4])
        ms, rms = scratch("ms", [P, 16]), scratch("rms", [P, 16])
        item_exp, n_items_t = scratch("item_exp", [1, MAX_ITEMS], I32), scratch("n_items_t", [1, 1], I32)
        item_kind = scratch("item_kind", [1, MAX_ITEMS + 2], I32)
        assert base + small_at[0] * kib <= nc.sbuf_usable_end, small_at
        pos_t, posf_t = at("pos_t", [P, NT], 178, I32), at("posf_t", [P, NT], 178.25)
        inv_b = at("inv_b", [P, 16], 178.5)
        kang, kang_t = at("kang", [P, 2, NT, 16], 180), at("kang_t", [P, NT, 16], 181)
        krot, krot_t = at("krot", [P, NT, ROPE], 182), at("krot_t", [P, NT, 16], 183)

        psT = ctx.enter_context(nc.psum_tensor("psT", [P, 2, 512], F32))
        psS = ctx.enter_context(nc.psum_tensor("psS", [P, 2, D], F32))
        psM = ctx.enter_context(nc.psum_tensor("psM", [P, 512], F32))
        psN = ctx.enter_context(nc.psum_tensor("psN", [P, 512], F32))

        def bank(i):
            return [psT[:, 0, :], psT[:, 1, :], psS[:, 0, 0:512], psS[:, 0, 512:D],
                    psS[:, 1, 0:512], psS[:, 1, 512:D], psM[:, :], psN[:, :]][i]

        ld_ident, ld_gb1, ld_gb2, ld_wup, ld_pos, ld_small = (sem(n) for n in (
            "ld_ident", "ld_gb1", "ld_gb2", "ld_wup", "ld_pos", "ld_small"))
        ld_mem, ld_mk, ld_mv, ld_win, ld_alibi, ld_late = (sem(n) for n in (
            "ld_mem", "ld_mk", "ld_mv", "ld_win", "ld_alibi", "ld_late"))
        ld_x = [sem(f"ld_x{s}") for s in range(4)]
        ld_h0 = [sem(f"ld_h0_{s}") for s in range(4)]
        st_h0 = [sem(f"st_h0_{s}") for s in range(4)]
        st_h2 = [sem(f"st_h2_{s}") for s in range(4)]
        ld_wo, ld_wmq, ld_wmo = sem("ld_wo"), sem("ld_wmq"), sem("ld_wmo")
        v_done, var_ready, rstd_ready, ln_done = (sem(n) for n in ("v_done", "var_ready", "rstd_ready", "ln_done"))
        t_full = sem("t_full")
        t_free = [sem("t_free0"), sem("t_free1")]
        mem_full, mem_free = sem("mem_full"), sem("mem_free")
        pj_full, pj_free, kv_full, kv_free = (sem(n) for n in ("pj_full", "pj_free", "kv_full", "kv_free"))
        pool_const, wq_ready, sq_ready, ss_full, ms_ready, rms_ready = (sem(n) for n in (
            "pool_const", "wq_ready", "sq_ready", "ss_full", "ms_ready", "rms_ready"))
        rb_full, cqn_ready, kn_full, vv_full = (sem(n) for n in (
            "rb_full", "cqn_ready", "kn_full", "vv_full"))
        vv_free = sem("vv_free")
        kn_free = [sem("kn_free0"), sem("kn_free1")]
        trig_ready, trig_done, krot_ready, kpe_all = (sem(n) for n in ("trig_ready", "trig_done", "krot_ready", "kpe_all"))
        s_full = sem("s_full")
        s_free = [sem("s_free0"), sem("s_free1")]
        rope_read, mx_ready, p_ready = (sem(n) for n in ("rope_read", "mx_ready", "p_ready"))
        pv_full, y_ready, diag_ready = (sem(n) for n in ("pv_full", "y_ready", "diag_ready"))
        ae_full, ae_free, qm_full, qm_ready, c_full, nm8_ready, p8_ready = (sem(n) for n in (
            "ae_full", "ae_free", "qm_full", "qm_ready", "c_full", "nm8_ready", "p8_ready"))
        o8_full, om_ready, r_full, r_ready = (sem(n) for n in ("o8_full", "om_ready", "r_full", "r_ready"))
        oh_ready, rank_full, g_exp_in, g_exp_out, item_cols_ready, items_ready = (sem(n) for n in (
            "oh_ready", "rank_full", "g_exp_in", "g_exp_out", "item_cols_ready", "items_ready"))
        pool_ready = sem("pool_ready")
        rows_done, items_full, marks_ready = sem("rows_done"), sem("items_full"), sem("marks_ready")
        gu_loaded = [[sem(f"gu_loaded{s}{h}") for h in range(2)] for s in range(2)]
        early_loaded = [sem("early_loaded0"), sem("early_loaded1")]
        dn_loaded = [sem(f"dn_loaded{s}") for s in range(2)]
        table_full, table_ready = sem("table_full"), sem("table_ready")
        tokens_ready = [sem("tokens_ready0"), sem("tokens_ready1")]
        places_ready = [sem("places_ready0"), sem("places_ready1")]
        x_loaded = [sem("x_loaded0"), sem("x_loaded1")]
        xT_full, xT_ready = [sem("xT_full0"), sem("xT_full1")], [sem("xT_ready0"), sem("xT_ready1")]
        gu_full, silu_done, act_ready = sem("gu_full"), sem("silu_done"), sem("act_ready")
        aT_full, aT_ready, y_full, ye_ready = sem("aT_full"), sem("aT_ready"), sem("y_full"), [sem("ye_ready0"), sem("ye_ready1")]
        ye_stored = [sem("ye_stored0"), sem("ye_stored1")]
        ld_pair = [sem(f"ld_pair{j}") for j in range(NT)]
        ld_h2, st_out, g_in_psum, out_ready = sem("ld_h2"), sem("st_out"), sem("g_in_psum"), sem("out_ready")
        first_added, both_added, scaled = sem("first_added"), sem("both_added"), sem("scaled")

        g_psum = psT[:, :, :].rearrange("p b n -> p (b n)")

        def h2_at(j):
            return h2_first[:, j, :] if j < 4 else hring[:, j - 4, :]

        def ktile(w):
            return w.rearrange("(k p) n -> p k n", p=P)

        def expert_tiles(w, e):
            return w[bass.ds(e, 1), :, :].rearrange("e (k p) n -> (e p) k n", p=P)

        def bcast(v):
            return v.to_broadcast([P, v.shape[1]])

        N_PAIRS = len(SOFTMAXED) // 2
        LAST_OF_TILE = {u for u in UNITS if u[0] in "ms" and u[2] == (MLA_HEADS if u[0] == "m" else SWA_KV) - 1}
        FREE_S = [(len(SCORED) + 1 - s) // 2 for s in range(2)]

        results = psM[0:MLA_V, :], psN[MLA_V:P, :]

        def evac_keys(eng, copy, odd):
            for p in range(4):
                eng.wait_ge(kn_full, 2 * p + odd + 1)
                cols = slice(odd * HALF, (odd + 1) * HALF)
                copy(kcat[0:NOPE, 2 * p, cols], bank(6 + odd)[0:NOPE, :])
                copy(kcat[0:NOPE, 2 * p + 1, cols], bank(6 + odd)[NOPE:P, :]).then_inc(kn_free[odd], 1)

        def turned(u, c):
            kind, j, h = u
            src = psT[:, CHUNK_NO[u, c] % 2, :].rearrange("p (k n) -> p k n", n=P)
            dst = probT[N_SOFT[u] % 4]
            if kind == "m":
                k = min(4, j + 1 - 4 * c)
                return dst[:, 4 * c:4 * c + k, :], src[:, 0:k, :]
            return (dst[:, 0:4, :], src) if c == 0 else (dst[CHUNK:P, 4:8, :], src[0:CHUNK, :, :])

        block = ctx.enter_context(nc.Block())

        @block.sync
        def _(sp):
            sp.dma_start(mem_sb[:, :, :], a["mem"].rearrange("(t p) d -> p t d", p=P)).then_inc(ld_mem, 16)
            sp.dma_start(w_mk[:, :, :], ktile(a["w_mk"])).then_inc(ld_mk, 16)
            sp.dma_start(hring[:, 0, :], a["x"][0:P, :]).then_inc(ld_x[0], 16)
            sp.dma_start(w_mv[:, :, :], ktile(a["w_mv"])).then_inc(ld_mv, 16)
            for j in range(1, 4):
                sp.dma_start(hring[:, j, :], a["x"][j * P:(j + 1) * P, :]).then_inc(ld_x[j], 16)
            w_src = ktile(a["w_in"])
            kr = Q_LORA + KV_LORA
            for dst, src, n in ((0, 0, kr), (C_QS, kr + ROPE, 640), (C_KR, kr, ROPE), (C_KR + ROPE, kr + ROPE + 640, P)):
                sp.dma_start(w_in[:, :, dst:dst + n], w_src[:, :, src:src + n]).then_inc(ld_win, 16)
            for j in range(NT):
                sp.wait_ge(ln_done, LN_NO["in", j] + 1)
                sp.dma_start(h0_d[j * P:(j + 1) * P, :], hring[:, j % 4, :]).then_inc(st_h0[j % 4], 16)
                if j + 4 < NT:
                    sp.wait_ge(st_h0[j % 4], 16)
                    sp.wait_ge(t_full, CHUNK_NO["x", j, 1] + 1)
                    sp.dma_start(hring[:, j % 4, :], a["x"][(j + 4) * P:(j + 5) * P, :]).then_inc(ld_x[j % 4], 16)
            for j in range(4):
                sp.wait_ge(t_full, CHUNK_NO["x", j + 4, 1] + 1)
                sp.wait_ge(st_h0[j], 32)
                sp.dma_start(hring[:, j, :], h0_d[j * P:(j + 1) * P, :]).then_inc(ld_h0[j], 16)
            sp.wait_ge(pj_full, 16)
            sp.wait_ge(kv_full, NT)
            sp.dma_start(tri[:, :], a["c_tri"]).then_inc(ld_late, 16)
            sp.dma_start(iotas[:, :], bcast(a["c_iotas"])).then_inc(ld_late, 16)
            sp.dma_start(choice_no[:, :, :], a["c_choice"].rearrange("p (j k) -> p j k", k=TOP_K)).then_inc(ld_late, 16)
            sp.dma_start(item_no[:, :], a["c_item"]).then_inc(ld_late, 16)
            sp.dma_start(route_b[:, 0:N_GROUPS], bcast(a["b_group"])).then_inc(ld_late, 16)
            sp.dma_start(route_b[:, N_GROUPS:ROUTE], bcast(a["b_expert"])).then_inc(ld_late, 16)
            sp.dma_start(w_route[:, :, 0:N_GROUPS], ktile(a["w_group"])).then_inc(ld_late, 16)
            sp.dma_start(w_route[:, :, N_GROUPS:ROUTE], ktile(a["w_expert"])).then_inc(ld_late, 16)
            sp.wait_ge(krot_ready, 1)
            sp.dma_start(alibi[:, :, :], a["c_alibi"].rearrange("p (h w) -> p h w", w=BAND)).then_inc(ld_alibi, 16)
            for c in range(2):
                n = CHUNK_NO["kpe", 0, c]
                sp.wait_ge(t_free[n % 2], n // 2 + 1)
            sp.dma_start(kcat[NOPE:QK, 1:MLA_HEADS, :], kcat[NOPE:QK, 0:1, :].to_broadcast([ROPE, MLA_HEADS - 1, SEQ])).then_inc(kpe_all, 16)
            sp.wait_ge(s_full, N_SCORE["s", NT - 1, 1] + 1)
            sp.wait_ge(mx_ready, N_SOFT["s", NT - 1, 1] + 1)

            def load_w_o(c):
                if c < 4:
                    sp.dma_start(w_o[c][:, :], a["w_o"][c * P:(c + 1) * P, :]).then_inc(ld_wo, 16)
                    return
                for g in range(SWA_KV):
                    row = MLA_HEADS * MLA_V + (g * GQ + c - 4) * SWA_DIM
                    sp.dma_start(w_o[c][g * SWA_DIM:(g + 1) * SWA_DIM, :], a["w_o"][row:row + SWA_DIM, :]).then_inc(ld_wo, 16)

            for c in (4, 5, 6, 7, 0, 1, 2):
                load_w_o(c)
            sp.wait_ge(pv_full, N_PAIRS)
            load_w_o(3)
            sp.dma_start(gb1[:, 0, :], bcast(a["ln1_g"])).then_inc(ld_gb1, 16)
            sp.dma_start(gb1[:, 1, :], bcast(a["ln1_b"])).then_inc(ld_gb1, 16)
            sp.dma_start(w_mq[:, :, :], ktile(a["w_mq"])).then_inc(ld_wmq, 16)
            sp.dma_start(gb2[:, 0, :], bcast(a["ln2_g"])).then_inc(ld_gb2, 16)
            sp.dma_start(gb2[:, 1, :], bcast(a["ln2_b"])).then_inc(ld_gb2, 16)
            sp.dma_start(w_mo[:, :, :], ktile(a["w_mo"])).then_inc(ld_wmo, 16)
            for j in range(NT):
                s = j % 4
                sp.wait_ge(ln_done, LN_NO["E", j] + 1)
                sp.dma_start(h2_d[j * P:(j + 1) * P, :], hring[:, s, :]).then_inc(st_h2[s], 16)
                if j + 4 < NT:
                    sp.wait_ge(st_h2[s], 16)
                    sp.wait_ge(t_full, CHUNK_NO["h2", j, 1] + 1)
                    sp.dma_start(hring[:, s, :], h0_d[(j + 4) * P:(j + 5) * P, :]).then_inc(ld_h0[s], 16)
                if j == NT - 3:
                    sp.wait_ge(ae_full, 2 * PROJ_NO["A", NT - 1] + 2)
                    for e in range(2):
                        sp.dma_start(w_gu[e][:, :, :], expert_tiles(a["w_gate_up"], e)).then_inc(early_loaded[e], 16)
                if j == NT - 2:
                    sp.wait_ge(qm_full, NT)
                    sp.dma_start(w_dn[0][:, :, :], expert_tiles(a["w_down"], 0)).then_inc(early_loaded[0], 16)
            sp.dma_start(gb1[:, 0, :], bcast(a["ln3_g"])).then_inc(ld_gb1, 16)
            sp.dma_start(gb1[:, 1, :], bcast(a["ln3_b"])).then_inc(ld_gb1, 16)
            for j in range(4):
                if j == 0:
                    sp.wait_ge(t_full, N_CHUNKS)
                sp.wait_ge(st_h2[j], 16)
                sp.dma_start(h2_first[:, j, :], h2_d[j * P:(j + 1) * P, :]).then_inc(ld_h2, 16)
            sp.wait_ge(items_ready, 1)
            n_items = sp.value_load(n_items_t[0:1, 0:1], min_val=1, max_val=MAX_ITEMS)

            def expert_of(item):
                return sp.value_load(item_exp[0:1, bass.ds(item, 1)], min_val=0, max_val=N_EXP - 1)

            def load_gate_up(s, gu):
                for h in range(2):
                    sp.dma_start(w_gu[s][:, 4 * h:4 * h + 4, :], gu[:, 4 * h:4 * h + 4, :]).then_inc(gu_loaded[s][h], 16)

            def load_weights(s, item, e, earlier):
                gu, dn = expert_tiles(a["w_gate_up"], e), expert_tiles(a["w_down"], e)
                if earlier:
                    sp.wait_ge(gu_full, item - 1)
                load_gate_up(s, gu)
                if earlier:
                    sp.wait_ge(y_full, item * 2 - 2)
                sp.dma_start(w_dn[s][:, :, :], dn).then_inc(dn_loaded[s], 16)

            e = expert_of(0)
            sp.wait_ge(early_loaded[0], 32)
            with sp.If(e > 0):
                load_weights(0, 0, e, False)
            with sp.If(e < 1):
                for loaded in (gu_loaded[0][0], gu_loaded[0][1], dn_loaded[0]):
                    sp.sem_inc(loaded, 16)
            e = expert_of(1)
            sp.wait_ge(early_loaded[1], 16)
            sp.wait_ge(pool_ready, 2)
            with sp.If(e > 1):
                load_gate_up(1, expert_tiles(a["w_gate_up"], e))
            with sp.If(e < 1):
                load_gate_up(1, expert_tiles(a["w_gate_up"], e))
            with sp.If(e > 0):
                with sp.If(e < 2):
                    for h in range(2):
                        sp.sem_inc(gu_loaded[1][h], 16)
            sp.dma_start(w_dn[1][:, :, :], expert_tiles(a["w_down"], e)).then_inc(dn_loaded[1], 16)
            with sp.Fori(1, MAX_ITEMS // 2) as r:
                for s in range(2):
                    with sp.If(r * 2 + s < n_items):
                        load_weights(s, r * 2 + s, expert_of(r * 2 + s), True)
            sp.wait_ge(rows_done, 1)
            for j in range(NT):
                sp.dma_start(pair[j][:, :, :], ye_d[j * 2 * P:(j + 1) * 2 * P, :].rearrange("(p k) d -> p k d", k=TOP_K)).then_inc(ld_pair[j], 16)
            for j in range(NT):
                sp.wait_ge(out_ready, j + 1)
                sp.dma_start(o[j * P:(j + 1) * P, :], h2_at(j)).then_inc(st_out, 16)
            sp.wait_ge(st_out, 16 * NT)

        @block.gpsimd
        def _(pool):
            nc.gpsimd.memset(neghalf[:, :], -0.5).then_inc(pool_const, 1)
            nc.gpsimd.memset(one_col[:, :], 1.0).then_inc(pool_const, 1)
            pool.wait_ge(pool_const, 2)

            def rsqrt_of_variance(key):
                n = LN_NO[key]
                pool.wait_ge(var_ready, n + 1)
                nc.gpsimd.tensor_tensor(rstd[:, n:n + 1], var[:, n:n + 1], neghalf[:, 0:1], ALU.pow).then_inc(rstd_ready, 1)

            for j in range(NT):
                rsqrt_of_variance(("in", j))
            pool.wait_ge(ld_wup, 16 * 5)
            nc.gpsimd.tensor_scalar(gq[:, 0:2], gq[:, 0:2], QK ** -0.5, None, ALU.mult).then_inc(pool_const, 1)
            pool.wait_ge(pool_const, 3)
            nc.gpsimd.tensor_scalar(gq[:, 2:4], gq[:, 0:2], -1.0, None, ALU.mult).then_inc(pool_const, 1)
            pool.wait_ge(pool_const, 4)
            for k in range(2):
                nc.gpsimd.tensor_scalar(wq[:, k, :, 0:QK], wuq[:, k, :, :], gq[:, k:k + 1], None, ALU.mult)
                nc.gpsimd.tensor_scalar(wq[:, k, :, QK:QK + 16], wuq[:, k, :, NOPE + 16:QK], gq[:, 2 + k:3 + k], None, ALU.mult)
                nc.gpsimd.tensor_scalar(wq[:, k, :, QK + 16:P], wuq[:, k, :, NOPE:NOPE + 16], gq[:, k:k + 1], None, ALU.mult).then_inc(wq_ready, 1)
            nc.gpsimd.tensor_scalar(wukv[:, :, :, :], wukv[:, :, :, :], gkv[:, 0:1], None, ALU.mult).then_inc(wq_ready, 1)
            pool.wait_ge(wq_ready, 3)
            pool.wait_ge(t_full, CHUNK_NO["mem", 1, 1] + 1)
            for hf in range(2):
                cols = slice(hf * HALF, (hf + 1) * HALF)
                for c in range(3):
                    pool.wait_ge(pj_free, hf * 8 + c + 1)
                    src = cq[:, c, cols] if c < 2 else ckv[:, cols]
                    nc.gpsimd.tensor_tensor(sq[:, c, cols], src, src, ALU.mult).then_inc(sq_ready, 1)
            pool.wait_ge(ms_ready, 1)
            nc.gpsimd.tensor_tensor(rms[:, :], ms[:, :], neghalf[:, :], ALU.pow).then_inc(rms_ready, 1)
            for key in PROJ_NO:
                rsqrt_of_variance(key)
            pool.wait_ge(items_ready, 1)
            for s in range(2):
                nc.gpsimd.memset(xg[s][:, :], 0.0).then_inc(pool_const, 1)
            pool.wait_ge(pool_const, 6)
            for s in range(4):
                pool.wait_ge(st_h2[s], 32)
            pool.wait_ge(table_ready, 1)
            n_items = pool.value_load(n_items_t[0:1, 0:1], min_val=1, max_val=MAX_ITEMS)

            last_token, last_row = pool.to_reg(SEQ - 1), pool.to_reg(SEQ * TOP_K - 1)

            def gather(s, item, before):
                if not isinstance(before, int) or before:
                    pool.wait_ge(xT_ready[s], before)
                nc.gpsimd.tensor_copy(tab_x[s][:, :], table[:, bass.ds(item, 1), 0]).then_inc(tokens_ready[s], 1)
                pool.wait_ge(tokens_ready[s], before + 1)
                pool.sem_inc(pool_ready, 1)
                pool.indirect_dma_start(xg[s][:, :], None, h2_d, bass.IndirectOffsetOnAxis(ap=tab_x[s][:, 0:1], axis=0),
                                        bounds_check=last_token, oob_is_err=False).then_inc(x_loaded[s], 16)

            def places(s, item, before):
                if not isinstance(before, int) or before:
                    pool.wait_ge(ye_stored[s], before * 16)
                nc.gpsimd.tensor_copy(tab_y[s][:, :], table[:, bass.ds(item, 1), 1:3]).then_inc(places_ready[s], 1)

            def scatter(s, before):
                pool.wait_ge(places_ready[s], before + 1)
                pool.wait_ge(ye_ready[s], before + 1)
                pool.sem_inc(pool_ready, 1)
                pool.indirect_dma_start(ye_d, bass.IndirectOffsetOnAxis(ap=tab_y[s][:, 0:1], axis=0), ye[s][:, :], None,
                                        bounds_check=last_row, oob_is_err=False).then_inc(ye_stored[s], 16)

            gather(0, 0, 0)
            gather(1, 1, 0)
            for s in range(2):
                nc.gpsimd.memset(act[s][0:HALF_P, :], 0.0)
                nc.gpsimd.memset(ye[s][HALF_P:P, :], 0.0).then_inc(pool_const, 1)
            pool.wait_ge(pool_const, 8)
            for s in range(2):
                places(s, s, 0)
            gather(0, 2, 1)
            for s in range(2):
                gather(1 - s, s + 3, s + 1)
                scatter(s, 0)
            with pool.Fori(1, MAX_ITEMS // 2) as r:
                with pool.If(r * 2 < n_items):
                    for s in range(2):
                        with pool.If(r * 2 + (s + 3) < n_items):
                            gather(1 - s, r * 2 + (s + 3), r + (s + 1))
                        with pool.If(r * 2 + s < n_items):
                            places(s, r * 2 + s, r)
                            scatter(s, r)
            n0 = pool.snap((n_items + 1) // 2 * 16)
            n1 = pool.snap(n_items // 2 * 16)
            pool.wait_ge(ye_stored[0], n0)
            pool.wait_ge(ye_stored[1], n1)
            pool.sem_inc(rows_done, 1)
            for t in range(NT + 2):
                if t < NT:
                    pool.wait_ge(first_added, t + 1)
                    nc.gpsimd.tensor_tensor(h2_at(t), h2_at(t), pair[t][:, 1, :], ALU.add).then_inc(both_added, 1)
                if 0 <= t - 1 < NT:
                    rsqrt_of_variance(("out", t - 1))
                if t - 2 >= 0:
                    pool.wait_ge(scaled, t - 1)
                    nc.gpsimd.tensor_tensor(h2_at(t - 2), h2_at(t - 2), gb1[:, 1, :], ALU.add).then_inc(out_ready, 1)

        @block.scalar
        def _(actq):
            actq.dma_start(ident[:, :], a["c_ident"]).then_inc(ld_ident, 16)
            actq.dma_start(gb1[:, 0, :], bcast(a["ln_in_g"])).then_inc(ld_gb1, 16)
            actq.dma_start(gb1[:, 1, :], bcast(a["ln_in_b"])).then_inc(ld_gb1, 16)
            actq.dma_start(wuq[:, :, :, :], a["w_uq"].rearrange("(k p) (h n) -> p k h n", p=P, n=QK)).then_inc(ld_wup, 16)
            for t in range(2):
                actq.dma_start(wukv[:, t, :, :], a["w_ukv"].rearrange("p (h t n) -> p t h n", t=2, n=NOPE)[:, t, :, :]).then_inc(ld_wup, 16)
            actq.dma_start(gq[:, 0:2], a["g_q"].rearrange("a (k p) -> p (a k)", p=P), allow_slow_non_contiguous=True).then_inc(ld_wup, 16)
            actq.dma_start(gkv[:, :], a["g_kv"].rearrange("a p -> p a"), allow_slow_non_contiguous=True).then_inc(ld_wup, 16)
            actq.dma_start(pos_all[NOPE:P, :], a["positions"].to_broadcast([P - NOPE, SEQ])).then_inc(ld_pos, 16)
            actq.dma_start(pos_t[:, :], a["positions"].rearrange("a (j p) -> p (a j)", p=P), allow_slow_non_contiguous=True).then_inc(ld_pos, 16)
            actq.dma_start(rope_f[:, :], a["c_rope"]).then_inc(ld_pos, 16)
            actq.dma_start(inv_b[:, :], bcast(a["c_inv"])).then_inc(ld_pos, 16)
            for r in range(2):
                actq.dma_start(sink[:, r, :], bcast(a["sinks"])).then_inc(ld_small, 16)

            def evac(key, dst, src_cols=None):
                n = CHUNK_NO[key]
                actq.wait_ge(t_full, n + 1)
                src = psT[:, n % 2, :] if src_cols is None else src_cols(psT[:, n % 2, :])
                nc.scalar.copy(dst, src).then_inc(t_free[n % 2], 1)

            four = lambda v: v.rearrange("p (k n) -> p k n", n=P)
            for t in range(2):
                for c in range(2):
                    evac(("mem", t, c), memT[:, 4 * c:4 * c + 4, t * P:(t + 1) * P], four)
            for i in range(4):
                actq.wait_ge(mem_full, i + 1)
                dst = kmT[:, 2 * i:2 * i + 2, :] if i < 2 else vm[:, i - 2, :]
                src = bank(2 + i).rearrange("p (h n) -> p h n", h=2) if i < 2 else bank(2 + i)
                nc.scalar.copy(dst, src).then_inc(mem_free, 1)
            for hf in range(2):
                for j in range(4 * hf, 4 * hf + 4):
                    for c in range(2):
                        evac(("x", j, c), hT[:, 4 * c:4 * c + 4, j * P:(j + 1) * P], four)
                cols = slice(hf * HALF, (hf + 1) * HALF)
                for c in range(8):
                    i = hf * 8 + c
                    actq.wait_ge(pj_full, i + 1)
                    src = bank(2 + i % 4)
                    if c < 3:
                        nc.scalar.copy(cq[:, c, cols] if c < 2 else ckv[:, cols], src).then_inc(pj_free, 1)
                    elif c < 7:
                        g = (c - 3) // 2 * SWA_DIM
                        for b in range(2):
                            ins = nc.scalar.mul(qs[g:g + SWA_DIM, (2 * (c - 3) + b) % GQ, cols],
                                                src[b * SWA_DIM:(b + 1) * SWA_DIM, :], SWA_DIM ** -0.5)
                        ins.then_inc(pj_free, 1)
                    else:
                        nc.scalar.copy(ks[:, cols], src).then_inc(pj_free, 1)
                    if i == 12:
                        actq.wait_ge(trig_ready, 1)
                        nc.scalar.activation(cs[NOPE:P, :], cs[NOPE:P, :], ACT.Sin).then_inc(trig_done, 1)
                        actq.wait_ge(trig_ready, 2)
                        nc.scalar.activation(kang[:, :, :, :], kang[:, :, :, :], ACT.Sin).then_inc(trig_done, 1)
                for j in range(4 * hf, 4 * hf + 4):
                    actq.wait_ge(kv_full, j + 1)
                    nc.scalar.copy(krvs[:, j, :], bank(6 + j % 2)[:, 0:ROPE + P]).then_inc(kv_free, 1)
            evac_keys(actq, nc.scalar.copy, 0)
            for c in range(2):
                n = CHUNK_NO["kpe", 0, c]
                actq.wait_ge(t_full, n + 1)
                nc.scalar.copy(kcat[NOPE:QK, 0, c * HALF:(c + 1) * HALF], psT[0:ROPE, n % 2, :]).then_inc(t_free[n % 2], 1)

            def softmax(u):
                kind, j, h = u
                n = N_SCORE[u]
                if kind == "q":
                    actq.wait_ge(rope_read, 2 * j + h + 1)
                    nc.scalar.copy(qcat[0:NOPE, j % 2, 4 * h:4 * h + 4, :], four(psS[0:NOPE, n % 2, 0:512])).then_inc(s_free[n % 2], 1)
                    return
                m = N_SOFT[u]
                actq.wait_ge(mx_ready, m + 1)
                if m >= 3:
                    prev = SOFTMAXED[m - 3]
                    actq.wait_ge(t_full, CHUNK_NO[prev, chunks_of(prev) - 1] + 1)
                if kind == "m":
                    w = (j + 1) * P
                    nc.scalar.activation(prob[m % 3][:, 0:w], psS[:, n % 2, 0:w], ACT.Exp, bias=neg_max[:, m % 4, 0:1],
                                         accum_out=sums_m[:, j % 2, h:h + 1]).then_inc(s_free[n % 2], 1)
                else:
                    lo = CHUNK if j == 0 else 0
                    for i in range(GQ):
                        p = prob[m % 3][:, i * BAND + lo:(i + 1) * BAND]
                        nc.scalar.activation(p, p, ACT.Exp, bias=neg_max[:, m % 4, i:i + 1],
                                             accum_out=sums_s[:, j % 2, h * GQ + i:h * GQ + i + 1])
                    nc.scalar.activation(sink_e[:, j % 2, h * GQ:(h + 1) * GQ], sink_d[:, j % 2, h * GQ:(h + 1) * GQ],
                                         ACT.Exp).then_inc(p_ready, 1)

            def evac_odd(u):
                for c in range(chunks_of(u)):
                    n = CHUNK_NO[u, c]
                    if n % 2:
                        m = N_SOFT[u]
                        if m >= 4:
                            actq.wait_ge(pv_full, m // 2 - 1)
                        actq.wait_ge(t_full, n + 1)
                        dst, src = turned(u, c)
                        nc.scalar.copy(dst, src).then_inc(t_free[1], 1)

            def evac_result(u):
                kind, j, h = u
                actq.wait_ge(pv_full, N_SOFT[u] // 2 + 1)
                tok = slice(j * P, (j + 1) * P)
                chunks = slice(0, 4) if kind == "m" else slice(4, 8)
                nc.scalar.copy(yT[0:MLA_V, chunks, tok], four(results[0]))
                nc.scalar.copy(yT[MLA_V:P, chunks, tok], four(results[1])).then_inc(y_ready, 1)

            for j in range(NT):
                actq.wait_ge(vv_full, j + 1)
                nc.scalar.copy(vmla[:, j, :], bank(4 + j % 2)).then_inc(vv_free, 1)
            actq.wait_ge(ld_small, 32)
            for t in range(len(UNITS) + 3):
                if t < len(UNITS):
                    softmax(UNITS[t])
                if 0 <= t - 2 < len(UNITS):
                    evac_odd(UNITS[t - 2])
                if t >= 3 and UNITS[t - 3] in LAST_OF_TILE:
                    evac_result(UNITS[t - 3])

            for s in range(NT + 4):
                j = s - 4
                if 0 <= j < NT:
                    for c in range(2):
                        evac(("h2", j, c), h2T[:, 4 * c:4 * c + 4, :], four)
                    actq.wait_ge(r_full, j + 1)
                    nc.scalar.copy(logits[:, j, :], psN[:, 0:ROUTE]).then_inc(r_ready, 1)
                j = s - 2
                if 0 <= j < NT:
                    for c in range(2):
                        evac(("p8", j, c), probT[0][:, 4 * c:4 * c + 4, :], four)
                j = s - 1
                if 0 <= j < NT:
                    for c in range(2):
                        evac(("h1", j, c), h1T[:, j % 2, 4 * c:4 * c + 4, :], four)
                    actq.wait_ge(qm_full, j + 1)
                    nc.scalar.mul(qm[:, :, :], four(psM[:, :]), MEM_DIM ** -0.5).then_inc(qm_ready, 1)
                j = s - 2
                if 0 <= j < NT:
                    evac(("o8", j, 0), omT[:, :, :], four)
                j = s - 1
                if 0 <= j < NT:
                    actq.wait_ge(nm8_ready, j + 1)
                    for h in range(MEM_HEADS):
                        ins = nc.scalar.activation(prob[0][:, h * N_MEM:(h + 1) * N_MEM], psS[:, 0, h * N_MEM:(h + 1) * N_MEM], ACT.Exp,
                                                   bias=neg_max[:, j % 2, h:h + 1], accum_out=sums_x[:, h:h + 1])
                    ins.then_inc(p8_ready, 1)
            actq.wait_ge(g_exp_in, 1)
            nc.scalar.activation(eg[:, :, :], gl[:, :, :], ACT.Exp).then_inc(g_exp_out, 1)
            actq.wait_ge(g_exp_in, 2)
            nc.scalar.activation(t8[3][:, :], t8[2][:, :], ACT.Exp).then_inc(g_exp_out, 1)
            actq.wait_ge(items_ready, 1)
            n_items = actq.value_load(n_items_t[0:1, 0:1], min_val=1, max_val=MAX_ITEMS)

            def evac_x(s, count):
                actq.wait_ge(xT_full[s], count * 2 - 1)
                nc.scalar.copy(xgT[s][:, 0:4, :], four(psT[:, 0, :]))
                actq.wait_ge(xT_full[s], count * 2)
                nc.scalar.copy(xgT[s][:, 4:8, :], four(psT[:, 1, :])).then_inc(xT_ready[s], 1)

            evac_x(0, 1)
            with actq.Fori(0, MAX_ITEMS // 2) as r:
                with actq.If(r * 2 < n_items):
                    for s in range(2):
                        i = r * 2 + s
                        kind = actq.value_load(item_kind[0:1, bass.ds(i, 1)], min_val=0, max_val=WIDE)
                        with actq.If(kind > NO_ITEM):
                            actq.wait_ge(gu_full, i + 1)
                            nc.scalar.activation(gate_s[:, :], bank(2), ACT.Silu).then_inc(silu_done, 1)
                        with actq.If(kind < NO_ITEM):
                            actq.wait_ge(gu_full, i + 1)
                            nc.scalar.activation(gate_s[HALF_P:P, :], bank(2)[0:HALF_P, :], ACT.Silu).then_inc(silu_done, 1)
                        with actq.If(i + 1 < n_items):
                            evac_x(1 - s, r + (1 + s))
                        with actq.If(i < n_items):
                            actq.wait_ge(aT_full, i + 1)
                            nc.scalar.copy(actT[s][:, :, :], four(psM[:, :])).then_inc(aT_ready, 1)
            actq.wait_ge(ld_gb1, 96)
            nc.scalar.copy(psT[:, :, :], gb1[:, 0, :].rearrange("p (b n) -> p b n", b=2)).then_inc(g_in_psum, 1)

        @block.vector
        def _(dve):
            settled = [0]

            def settle(ins):
                settled[0] += 1
                ins.then_inc(v_done, 1)
                dve.wait_ge(v_done, settled[0])

            V = nc.vector
            four = lambda v: v.rearrange("p (k n) -> p k n", n=P)

            def layer_norm(key, t, gb):
                n = LN_NO[key]
                r = n % 2
                V.bn_stats(stats[:, r, 0, :], t[:, 0:512])
                settle(V.bn_stats(stats[:, r, 1, :], t[:, 512:D]))
                settle(V.bn_aggr(mv[:, r, :], stats[:, r, :, :]))
                V.tensor_scalar(var[:, n:n + 1], mv[:, r, 1:2], LN_EPS, None, ALU.add).then_inc(var_ready, 1)
                settle(V.scalar_tensor_tensor(t, t, mv[:, r, 0:1], gb[:, 0, :], ALU.subtract, ALU.mult))
                dve.wait_ge(rstd_ready, n + 1)
                V.scalar_tensor_tensor(t, t, rstd[:, n:n + 1], gb[:, 1, :], ALU.mult, ALU.add).then_inc(ln_done, 1)

            def reduce_angle(ang, t, turns, phase):
                settle(V.tensor_scalar(t, ang, 1 / (2 * np.pi), turns, ALU.mult, ALU.add))
                settle(V.tensor_scalar(t, t, ROUNDER, None, ALU.add))
                settle(V.tensor_scalar(t, t, ROUNDER, None, ALU.subtract))
                for part in (TWO_PI_1, TWO_PI_2, TWO_PI_3):
                    settle(V.scalar_tensor_tensor(ang, t, -part, ang, ALU.mult, ALU.add))
                settle(V.tensor_scalar(ang, ang, phase, 3.1415925, ALU.add, ALU.min))
                return V.tensor_scalar(ang, ang, -3.1415925, None, ALU.max)

            dve.wait_ge(ld_gb1, 32)
            for j in range(NT):
                dve.wait_ge(ld_x[j % 4], 16 * (j // 4 + 1))
                layer_norm(("in", j), hring[:, j % 4, :], gb1)
            dve.wait_ge(ld_pos, 64)
            lo = slice(NOPE, P)
            settle(V.tensor_scalar(cs[lo, :], pos_all[lo, :], rope_f[lo, 0:1], None, ALU.mult))
            reduce_angle(cs[lo, :], trig_t[lo, :], rope_f[lo, 1:2], rope_f[lo, 2:3]).then_inc(trig_ready, 1)
            settle(V.tensor_copy(posf_t[:, :], pos_t[:, :]))
            for c, (turns, phase) in enumerate(((0.25, np.pi / 2), (0.0, 0.0))):
                settle(V.tensor_tensor(kang[:, c, :, :], posf_t[:, :].unsqueeze(2).to_broadcast([P, NT, 16]),
                                       inv_b[:, :].unsqueeze(1).to_broadcast([P, NT, 16]), ALU.mult))
                last = reduce_angle(kang[:, c, :, :], kang_t[:, :, :], turns, phase)
            last.then_inc(trig_ready, 1)
            dve.wait_ge(ss_full, 1)
            V.tensor_scalar(ms[:, 0:8], bank(0)[:, 0:8], 1.0 / Q_LORA, RMS_EPS, ALU.mult, ALU.add)
            V.tensor_scalar(ms[:, 8:16], bank(0)[:, 8:16], 1.0 / KV_LORA, RMS_EPS, ALU.mult, ALU.add).then_inc(ms_ready, 1)
            for hf in range(2):
                cols = slice(hf * HALF, (hf + 1) * HALF)
                dve.wait_ge(rb_full, 2 * hf + 1)
                for c in range(2):
                    V.tensor_tensor(cq[:, c, cols], cq[:, c, cols], bank(0), ALU.mult).then_inc(cqn_ready, 1)
                dve.wait_ge(rb_full, 2 * hf + 2)
                V.tensor_tensor(ckv[:, cols], ckv[:, cols], bank(1), ALU.mult).then_inc(cqn_ready, 1)
            dve.wait_ge(trig_done, 2)
            dve.wait_ge(kv_free, NT)
            x1, x2 = krvs[:, :, 0:16], krvs[:, :, 16:ROPE]
            V.tensor_tensor(krot[:, :, 0:16], x1, kang[:, 0, :, :], ALU.mult)
            settle(V.tensor_tensor(krot_t[:, :, :], x2, kang[:, 1, :, :], ALU.mult))
            settle(V.tensor_tensor(krot[:, :, 0:16], krot[:, :, 0:16], krot_t[:, :, :], ALU.subtract))
            V.tensor_tensor(krot[:, :, 16:ROPE], x1, kang[:, 1, :, :], ALU.mult)
            settle(V.tensor_tensor(krot_t[:, :, :], x2, kang[:, 0, :, :], ALU.mult))
            V.tensor_tensor(krot[:, :, 16:ROPE], krot[:, :, 16:ROPE], krot_t[:, :, :], ALU.add).then_inc(krot_ready, 1)
            evac_keys(dve, V.tensor_copy, 1)
            def scores(u):
                kind, j, h = u
                n = N_SCORE[u]
                dve.wait_ge(s_full, n + 1)
                if kind == "q":
                    cos, sin = (cs[x, j * P:(j + 1) * P].unsqueeze(1).to_broadcast([ROPE, 4, P]) for x in (slice(NOPE, QK), slice(QK, P)))
                    ps = psS[:, n % 2, 0:512]
                    dst = qcat[NOPE:QK, j % 2, 4 * h:4 * h + 4, :]
                    V.tensor_tensor(dst, four(ps[NOPE:QK, :]), cos, ALU.mult)
                    settle(V.tensor_tensor(four(ps[QK:P, :]), four(ps[QK:P, :]), sin, ALU.mult))
                    V.tensor_tensor(dst, dst, four(ps[QK:P, :]), ALU.add).then_inc(rope_read, 1)
                    return
                m = N_SOFT[u]
                if kind == "m":
                    w = (j + 1) * P
                    settle(V.memset(psS[0:CHUNK, n % 2, w - CHUNK:w], MASKED))
                    V.tensor_reduce(neg_max[:, m % 4, 0:1], psS[:, n % 2, 0:w], X, ALU.max, negate=True).then_inc(mx_ready, 1)
                    return
                lo = CHUNK if j == 0 else 0
                if m >= 3:
                    prev = SOFTMAXED[m - 3]
                    dve.wait_ge(t_full, CHUNK_NO[prev, chunks_of(prev) - 1] + 1)
                biased = prob[m % 3][:, 0:GQ * BAND].rearrange("p (h w) -> p h w", w=BAND)[:, :, lo:BAND]
                raw = psS[:, n % 2, :].rearrange("p (h w) -> p h w", w=256)[:, :, lo:BAND]
                V.tensor_tensor(biased, raw, alibi[:, h * GQ:(h + 1) * GQ, lo:BAND], ALU.add).then_inc(s_free[n % 2], 1)
                dve.wait_ge(s_free[n % 2], n // 2 + 1)
                hs = slice(h * GQ, (h + 1) * GQ)
                settle(V.tensor_reduce(rmax[:, 0:GQ], biased, X, ALU.max))
                settle(V.tensor_tensor(rmax[:, 0:GQ], rmax[:, 0:GQ], sink[:, j % 2, hs], ALU.max))
                settle(V.tensor_tensor(sink_d[:, j % 2, hs], sink[:, j % 2, hs], rmax[:, 0:GQ], ALU.subtract))
                V.tensor_scalar(neg_max[:, m % 4, :], rmax[:, 0:GQ], -1.0, None, ALU.mult).then_inc(mx_ready, 1)

            def evac_even(u):
                for c in range(chunks_of(u)):
                    n = CHUNK_NO[u, c]
                    if n % 2 == 0:
                        m = N_SOFT[u]
                        if m >= 4:
                            dve.wait_ge(pv_full, m // 2 - 1)
                        dve.wait_ge(t_full, n + 1)
                        dst, src = turned(u, c)
                        V.tensor_copy(dst, src).then_inc(t_free[0], 1)

            def diagonals(u):
                kind, j, h = u
                n, m = N_SCORE[u], N_SOFT[u]
                if kind == "m":
                    dve.wait_ge(s_free[n % 2], n // 2 + 1)
                    settle(V.reciprocal(rinv[:, 0:1], sums_m[:, j % 2, h:h + 1]))
                else:
                    dve.wait_ge(p_ready, 2 * j + h + 1)
                    hs = slice(h * GQ, (h + 1) * GQ)
                    settle(V.tensor_tensor(rinv[:, 0:GQ], sums_s[:, j % 2, hs], sink_e[:, j % 2, hs], ALU.add))
                    settle(V.reciprocal(rinv[:, 0:GQ], rinv[:, 0:GQ]))
                if m >= 2:
                    prev = SOFTMAXED[m - 2]
                    dve.wait_ge(t_full, CHUNK_NO[prev, chunks_of(prev) - 1] + 1)
                for i in range(GQ if kind == "s" else 1):
                    ins = V.tensor_scalar(diag[:, m % 2, i, :], ident[:, :], rinv[:, i:i + 1], None, ALU.mult)
                ins.then_inc(diag_ready, 1)
                dve.wait_ge(diag_ready, m + 1)

            scores(UNITS[0])
            dve.wait_ge(ld_alibi, 16)
            dve.wait_ge(ld_small, 32)
            for t in range(len(UNITS) + 2):
                if 0 < t < len(UNITS):
                    scores(UNITS[t])
                if 0 <= t - 1 < len(UNITS) and UNITS[t - 1] in N_SOFT:
                    diagonals(UNITS[t - 1])
                if t >= 2:
                    evac_even(UNITS[t - 2])

            def residual(key, gb):
                n, j = PROJ_NO[key], key[1]
                h = hring[:, j % 4, :]
                for c in range(2):
                    dve.wait_ge(ae_full, 2 * n + c + 1)
                    ins = V.scalar_tensor_tensor(h[:, c * 512:(c + 1) * 512], h[:, c * 512:(c + 1) * 512], ALPHA,
                                                 bank(4 + c), ALU.mult, ALU.add)
                    ins.then_inc(ae_free, 1)
                dve.wait_ge(ae_free, 2 * n + 2)
                layer_norm(key, h, gb)

            V.memset(ones[:, :], 1.0)
            dve.wait_ge(ld_gb1, 64)
            for s in range(NT + 3):
                if s < NT:
                    dve.wait_ge(ld_h0[s % 4], 16 * (s // 4 + 1))
                    residual(("A", s), gb1)
                j = s - 2
                if 0 <= j < NT:
                    dve.wait_ge(o8_full, j + 1)
                    settle(V.reciprocal(rinv[:, 0:4], sums_x[:, :]))
                    V.tensor_tensor(four(om[:, :]), four(psN[:, :]), rinv[:, 0:4].unsqueeze(2).to_broadcast([P, 4, P]),
                                    ALU.mult).then_inc(om_ready, 1)
                    dve.wait_ge(om_ready, j + 1)
                j = s - 1
                if 0 <= j < NT:
                    dve.wait_ge(c_full, j + 1)
                    V.tensor_reduce(neg_max[:, j % 2, :], psS[:, 0, :].rearrange("p (h w) -> p h w", w=N_MEM), X, ALU.max,
                                    negate=True).then_inc(nm8_ready, 1)
                j = s - 2
                if 0 <= j < NT:
                    if j == 0:
                        dve.wait_ge(ld_gb2, 32)
                    residual(("E", j), gb2)

            dve.wait_ge(r_ready, NT)
            dve.wait_ge(ld_late, 16 * 8)
            over = lambda v, n: v.unsqueeze(2).to_broadcast([P, NT, n])
            ids = lambda n: iotas[:, 0:n].unsqueeze(1).to_broadcast([P, NT, n])
            settle(V.tensor_tensor(logits[:, :, :], logits[:, :, :], route_b[:, :].unsqueeze(1).to_broadcast([P, NT, ROUTE]), ALU.add))
            gmax, gid, behind, second_e, gprob, share = t8[0], t8[1], t8[2], t8[3], t8[8], t8[9]
            lg, le = logits[:, :, 0:N_GROUPS], logits[:, :, N_GROUPS:ROUTE]
            settle(V.tensor_reduce(gmax[:, :], lg, X, ALU.max))
            V.tensor_tensor(gl[:, :, :], lg, over(gmax[:, :], N_GROUPS), ALU.subtract).then_inc(g_exp_in, 1)

            def first_at(out, values, top, n, tmp, idx):
                settle(V.tensor_tensor(tmp, values, over(top, n), ALU.is_equal))
                settle(V.tensor_tensor(tmp, tmp, ids(n), ALU.mult))
                settle(V.tensor_reduce(idx, tmp, X, ALU.min))
                settle(V.tensor_tensor(out, ids(n), over(idx, n), ALU.is_equal))

            first_at(gpen[:, :, :], lg, gmax[:, :], N_GROUPS, gpen[:, :, :], gid[:, :])
            settle(V.tensor_scalar(gpen[:, :, :], gpen[:, :, :], 1.0, -MASKED, ALU.subtract, ALU.mult))
            for g in range(N_GROUPS):
                x = slice(g * PER_GROUP, (g + 1) * PER_GROUP)
                last = V.tensor_tensor(elm[:, :, x], le[:, :, x], gpen[:, :, g:g + 1].to_broadcast([P, NT, PER_GROUP]), ALU.add)
            settle(last)
            m1, i1, m2, i2 = t8[4], t8[5], t8[6], t8[7]
            settle(V.tensor_reduce(m1[:, :], elm[:, :, :], X, ALU.max))
            first_at(oh1[:, :, :], elm[:, :, :], m1[:, :], N_EXP, eqx[:, :, :], i1[:, :])
            settle(V.scalar_tensor_tensor(elm[:, :, :], oh1[:, :, :], 100 * MASKED, elm[:, :, :], ALU.mult, ALU.add))
            settle(V.tensor_reduce(m2[:, :], elm[:, :, :], X, ALU.max))
            first_at(oh2[:, :, :], elm[:, :, :], m2[:, :], N_EXP, eqx[:, :, :], i2[:, :])
            V.tensor_tensor(oh_sum[:, :, :], oh1[:, :, :], oh2[:, :, :], ALU.add).then_inc(oh_ready, 1)
            dve.wait_ge(g_exp_out, 1)
            V.tensor_tensor(behind[:, :], m2[:, :], m1[:, :], ALU.subtract).then_inc(g_exp_in, 1)
            settle(V.tensor_reduce(gprob[:, :], eg[:, :, :], X, ALU.add))
            settle(V.reciprocal(gprob[:, :], gprob[:, :]))
            dve.wait_ge(g_exp_out, 2)
            settle(V.tensor_scalar(share[:, :], second_e[:, :], 1.0, None, ALU.add))
            settle(V.reciprocal(share[:, :], share[:, :]))
            settle(V.tensor_tensor(gprob[:, :], gprob[:, :], share[:, :], ALU.mult))
            V.tensor_copy(gates[:, :, 0], gprob[:, :])
            V.tensor_tensor(gates[:, :, 1], gprob[:, :], second_e[:, :], ALU.mult)
            dve.wait_ge(rank_full, 2)
            V.tensor_copy(rank[:, :, :], bank(2)[:, 0:NT * N_EXP].rearrange("p (j e) -> p j e", e=N_EXP))
            settle(V.tensor_copy(tot[:, :, :], bank(3)[:, 0:NT * N_EXP].rearrange("p (j e) -> p j e", e=N_EXP)))
            settle(V.tensor_reduce(cnt[:, :], tot[:, :, :].rearrange("p j e -> p e j"), X, ALU.add))
            nblk_i = nblk[:, :].bitcast(I32)
            settle(V.tensor_scalar(nblk_i, cnt[:, :], float(P - 1), None, ALU.add))
            settle(V.tensor_scalar(nblk_i, nblk_i, 7, None, ALU.logical_shift_right))
            settle(V.tensor_copy(nblk_f[:, :], nblk_i))
            settle(V.tensor_tensor_scan(incl[:, :], ones[:, 0:N_EXP], nblk_f[:, :], 0.0, ALU.mult, ALU.add))
            settle(V.tensor_tensor(first_block[:, :], incl[:, :], nblk_f[:, :], ALU.subtract))
            V.tensor_scalar(item_cmp[:, 0, :], incl[:, :], item_no[:, 0:1], None, ALU.is_le)
            V.tensor_scalar(item_cmp[:, 2, :], first_block[:, :], item_no[:, 0:1], None, ALU.is_gt)
            settle(V.scalar_tensor_tensor(row_end[:, :], first_block[:, :], float(P), cnt[:, :], ALU.mult, ALU.add))
            settle(V.tensor_scalar(item_cmp[:, 1, :], row_end[:, :], item_no[:, 1:2], None, ALU.is_gt))
            settle(V.tensor_reduce(item_sum[:, 0:3], item_cmp[:, :, :], X, ALU.add))
            V.tensor_scalar(item_cols[:, 0:1], item_sum[:, 0:1], float(N_EXP - 1), None, ALU.min)
            V.tensor_tensor(item_sum[:, 1:2], item_sum[:, 1:2], item_sum[:, 2:3], ALU.subtract)
            settle(V.tensor_copy(item_sum[:, 3:4], item_cmp[:, 0, N_EXP - 1:N_EXP]))
            V.scalar_tensor_tensor(item_cols[:, 1:2], item_sum[:, 1:2], float(WIDE), item_sum[:, 3:4], ALU.mult, ALU.add).then_inc(item_cols_ready, 1)
            V.tensor_copy(n_items_t[:, :], incl[0:1, N_EXP - 1:N_EXP])
            settle(V.tensor_scalar(place[:, 0, :], first_block[:, :], float(P), None, ALU.mult))
            for j in range(1, NT):
                settle(V.tensor_tensor(place[:, j, :], place[:, j - 1, :], tot[:, j - 1, :], ALU.add))
                if j == 4:
                    dve.wait_ge(items_full, 1)
                    V.tensor_copy(item_exp[:, :], bank(5)[0:1, 0:MAX_ITEMS])
                    V.tensor_copy(item_kind[:, :], bank(5)[0:1, P:P + MAX_ITEMS + 2]).then_inc(items_ready, 1)
            settle(V.tensor_tensor(place[:, :, :], place[:, :, :], rank[:, :, :], ALU.add))
            for k, oh in enumerate((oh1, oh2)):
                settle(V.tensor_tensor(oh[:, :, :], oh[:, :, :], place[:, :, :], ALU.mult))
                settle(V.tensor_reduce(posf[:, :, k], oh[:, :, :], X, ALU.add))
            settle(V.tensor_copy(posi[:, :, :], posf[:, :, :]))
            settle(V.tensor_scalar(posi[:, :, :], posi[:, :, :], 7, None, ALU.logical_shift_right))
            settle(V.tensor_copy(posd[:, :, :], posi[:, :, :]))
            settle(V.scalar_tensor_tensor(posf[:, :, :], posd[:, :, :], -float(P), posf[:, :, :], ALU.mult, ALU.add))
            for j in range(NT):
                for k in range(TOP_K):
                    V.tensor_scalar(mark_row[:, j, k, :], iotas[:, N_EXP:], posf[:, j, k:k + 1], None, ALU.is_equal)
                    for f, v in enumerate((choice_no, gates)):
                        ins = V.tensor_scalar(mark_item[:, j, k, f, :], iotas[:, N_EXP:N_EXP + MAX_ITEMS], posd[:, j, k:k + 1],
                                              v[:, j, k:k + 1], ALU.is_equal, ALU.mult)
                    ins.then_inc(marks_ready, 1)
            dve.wait_ge(table_full, 1)
            numbers = bank(4)[:, 0:MAX_ITEMS]
            V.tensor_copy(table[:, 0:MAX_ITEMS, 2].bitcast(F32), bank(4)[:, MAX_ITEMS:2 * MAX_ITEMS])
            settle(V.tensor_scalar(dest[:, :], numbers, 0.0, float(NO_ROW), ALU.is_equal, ALU.mult))
            settle(V.scalar_tensor_tensor(table[:, 0:MAX_ITEMS, 1], numbers, -1.0, dest[:, :], ALU.add, ALU.add))
            V.tensor_scalar(table[:, 0:MAX_ITEMS, 0], table[:, 0:MAX_ITEMS, 1], 1, None, ALU.logical_shift_right).then_inc(table_ready, 1)

            dve.wait_ge(items_ready, 1)
            dve.wait_ge(pool_const, 8)
            n_items = dve.value_load(n_items_t[0:1, 0:1], min_val=1, max_val=MAX_ITEMS)

            def item_results(s, i, before):
                kind = dve.value_load(item_kind[0:1, bass.ds(i, 1)], min_val=0, max_val=WIDE)
                gate = tab_y[s][:, 1:2].bitcast(F32)

                def waits_for_result():
                    if not isinstance(before, int):
                        dve.wait_ge(ye_stored[s], before * 16)
                    dve.wait_ge(places_ready[s], before + 1)
                    dve.wait_ge(y_full, i * 2 + 1)

                with dve.If(kind > NO_ITEM):
                    dve.wait_ge(silu_done, i + 1)
                    V.tensor_tensor(act[s][:, :], gate_s[:, :], bank(3), ALU.mult).then_inc(act_ready, 1)
                    waits_for_result()
                    V.tensor_scalar(ye[s][:, 0:512], bank(4), gate, None, ALU.mult)
                    dve.wait_ge(y_full, i * 2 + 2)
                    V.tensor_scalar(ye[s][:, 512:D], bank(5), gate, None, ALU.mult).then_inc(ye_ready[s], 1)
                with dve.If(kind < NO_ITEM):
                    dve.wait_ge(silu_done, i + 1)
                    V.tensor_tensor(act[s][HALF_P:P, :], gate_s[HALF_P:P, :], bank(3)[HALF_P:P, :], ALU.mult).then_inc(act_ready, 1)
                    waits_for_result()
                    V.tensor_scalar(ye[s][0:HALF_P, 0:512], bank(4)[0:HALF_P, :], gate[0:HALF_P], None, ALU.mult)
                    dve.wait_ge(y_full, i * 2 + 2)
                    V.tensor_scalar(ye[s][0:HALF_P, 512:D], bank(5)[HALF_P:P, :], gate[0:HALF_P], None, ALU.mult).then_inc(ye_ready[s], 1)

            for s in range(2):
                item_results(s, s, 0)
            with dve.Fori(1, MAX_ITEMS // 2) as r:
                with dve.If(r * 2 < n_items):
                    for s in range(2):
                        item_results(s, r * 2 + s, r)
            dve.wait_ge(ld_gb1, 96)
            dve.wait_ge(ld_h2, 64)
            dve.wait_ge(g_in_psum, 1)
            for t in range(NT + 2):
                if t < NT:
                    dve.wait_ge(ld_pair[t], 16)
                    V.scalar_tensor_tensor(h2_at(t), h2_at(t), ALPHA, pair[t][:, 0, :], ALU.mult, ALU.add).then_inc(first_added, 1)
                if 0 <= t - 1 < NT:
                    n = LN_NO["out", t - 1]
                    r = n % 2
                    dve.wait_ge(both_added, t)
                    V.bn_stats(stats[:, r, 0, :], h2_at(t - 1)[:, 0:512])
                    settle(V.bn_stats(stats[:, r, 1, :], h2_at(t - 1)[:, 512:D]))
                    settle(V.bn_aggr(mv[:, r, :], stats[:, r, :, :]))
                    V.tensor_scalar(var[:, n:n + 1], mv[:, r, 1:2], LN_EPS, None, ALU.add).then_inc(var_ready, 1)
                if t - 2 >= 0:
                    n = LN_NO["out", t - 2]
                    h = h2_at(t - 2)
                    dve.wait_ge(rstd_ready, n + 1)
                    settle(V.tensor_scalar(h, h, mv[:, n % 2, 0:1], rstd[:, n:n + 1], ALU.subtract, ALU.mult))
                    V.tensor_tensor(h, h, g_psum, ALU.mult).then_inc(scaled, 1)

        @block.tensor
        def _(pe):
            mm = nc.tensor.matmul
            T = nc.tensor.transpose

            def transposes(key, blocks, rows_out=P):
                n = CHUNK_NO[key]
                if n >= 2:
                    pe.wait_ge(t_free[n % 2], n // 2)
                for i, b in enumerate(blocks):
                    ins = T(psT[0:rows_out, n % 2, i * P:(i + 1) * P], b, ident[:, :])
                ins.then_inc(t_full, 1)

            def evacuated(key):
                n = CHUNK_NO[key]
                pe.wait_ge(t_free[n % 2], n // 2 + 1)

            pe.wait_ge(ld_ident, 16)
            pe.wait_ge(ld_mem, 16)
            for t in range(2):
                for c in range(2):
                    transposes(("mem", t, c), [mem_sb[:, t, (4 * c + i) * P:(4 * c + i + 1) * P] for i in range(4)])
            pe.wait_ge(ld_mk, 16)
            for b in range(2):
                pe.wait_ge(t_free[b], 2)
            for i in range(2):
                for hh in range(2):
                    h = 2 * i + hh
                    for k in range(KC):
                        ins = mm(bank(2 + i)[:, hh * N_MEM:(hh + 1) * N_MEM], w_mk[:, k, h * P:(h + 1) * P], memT[:, k, :],
                                 start=(k == 0), stop=(k == KC - 1))
                ins.then_inc(mem_full, 1)
            pe.wait_ge(ld_mv, 16)
            for t in range(2):
                for k in range(KC):
                    ins = mm(bank(4 + t), memT[:, k, t * P:(t + 1) * P], w_mv[:, k, :], start=(k == 0), stop=(k == KC - 1))
                ins.then_inc(mem_full, 1)
            def squares():
                pe.wait_ge(sq_ready, 6)
                pe.wait_ge(pool_const, 2)
                for j in range(NT):
                    tok = slice(j * P, (j + 1) * P)
                    for c in range(2):
                        mm(bank(0)[:, j:j + 1], sq[:, c, tok], one_col[:, :], start=(c == 0), stop=(c == 1))
                for j in range(NT):
                    ins = mm(bank(0)[:, 8 + j:9 + j], sq[:, 2, j * P:(j + 1) * P], one_col[:, :], start=True, stop=True)
                ins.then_inc(ss_full, 1)

            def spread_rms(hf):
                pe.wait_ge(rms_ready, 1)
                if hf:
                    pe.wait_ge(cqn_ready, 3)
                for kv in range(2):
                    for i in range(4):
                        c = kv * 8 + hf * 4 + i
                        ins = mm(bank(kv)[:, i * P:(i + 1) * P], rms[:, c:c + 1].to_broadcast([P, P]), ident[:, :],
                                 start=True, stop=True)
                    ins.then_inc(rb_full, 1)

            for hf in range(2):
                for j in range(4 * hf, 4 * hf + 4):
                    pe.wait_ge(ln_done, LN_NO["in", j] + 1)
                    for c in range(2):
                        transposes(("x", j, c), [hring[:, j % 4, (4 * c + i) * P:(4 * c + i + 1) * P] for i in range(4)])
                for c in range(2):
                    n = CHUNK_NO["x", 4 * hf + 3, c]
                    pe.wait_ge(t_free[n % 2], n // 2 + 1)
                if hf == 0:
                    pe.wait_ge(ld_win, 64)
                cols = slice(hf * HALF, (hf + 1) * HALF)
                for c in range(8):
                    i = hf * 8 + c
                    if i < 4:
                        pe.wait_ge(mem_free, i + 1)
                    else:
                        pe.wait_ge(pj_free, i - 3)
                    for k in range(KC):
                        ins = mm(bank(2 + i % 4), w_in[:, k, c * P:(c + 1) * P], hT[:, k, cols], start=(k == 0), stop=(k == KC - 1))
                    ins.then_inc(pj_full, 1)
                    if hf and c == 4:
                        squares()
                    if hf and c >= 6:
                        spread_rms(c - 6)
                for j in range(4 * hf, 4 * hf + 4):
                    if j >= 2:
                        pe.wait_ge(kv_free, j - 1)
                    for k in range(KC):
                        ins = mm(bank(6 + j % 2)[:, 0:ROPE + P], hT[:, k, j * P:(j + 1) * P], w_in[:, k, C_KR:IN_COLS],
                                 start=(k == 0), stop=(k == KC - 1))
                    ins.then_inc(kv_full, 1)
            pe.wait_ge(wq_ready, 3)
            pe.wait_ge(kv_free, NT)
            pe.wait_ge(cqn_ready, 6)
            for i in range(8):
                p, hf = i // 2, i % 2
                if i >= 2:
                    pe.wait_ge(kn_free[i % 2], i // 2)
                mm(bank(6 + i % 2), wukv[:, 0, 2 * p:2 * p + 2, :].rearrange("p h n -> p (h n)"), ckv[:, hf * HALF:(hf + 1) * HALF],
                   start=True, stop=True).then_inc(kn_full, 1)
            pe.wait_ge(krot_ready, 1)
            for c in range(2):
                transposes(("kpe", 0, c), [krot[:, 4 * c + i, :] for i in range(4)], rows_out=ROPE)
            for c in range(2):
                evacuated(("kpe", 0, c))

            def score(u):
                kind, j, h = u
                n = N_SCORE[u]
                tok = slice(j * P, (j + 1) * P)
                if n >= 2:
                    pe.wait_ge(s_free[n % 2], n // 2)
                ps = psS[:, n % 2, :]
                if kind == "q":
                    for g in range(4):
                        for k in range(2):
                            ins = mm(ps[:, g * P:(g + 1) * P], wq[:, k, 4 * h + g, :], cq[:, k, tok], start=(k == 0), stop=(k == 1))
                elif kind == "m":
                    w = (j + 1) * P
                    if h == 0:
                        for half in range(2):
                            nq = N_SCORE["q", j, half]
                            pe.wait_ge(s_free[nq % 2], nq // 2 + 1)
                        pe.wait_ge(rope_read, 2 * j + 2)
                    if j == 0 and h:
                        pe.wait_ge(kpe_all, 16)
                    for c in range(0, w, 512):
                        e = min(w, c + 512)
                        ins = mm(ps[:, c:e], qcat[:, j % 2, h, :], kcat[:, h, c:e], start=True, stop=True)
                else:
                    lo = CHUNK if j == 0 else 0
                    rows_ = slice(h * SWA_DIM, (h + 1) * SWA_DIM)
                    for i in range(GQ):
                        ins = mm(ps[:, i * 256 + lo:i * 256 + BAND], qs[rows_, i, tok], ks[rows_, j * P - CHUNK + lo:(j + 1) * P],
                                 start=True, stop=True)
                ins.then_inc(s_full, 1)

            def turn(u):
                kind, j, h = u
                if kind == "q":
                    return
                m = N_SOFT[u]
                pe.wait_ge(diag_ready, m + 1)
                for c in range(chunks_of(u)):
                    n = CHUNK_NO[u, c]
                    if n >= 2:
                        pe.wait_ge(t_free[n % 2], n // 2)
                    if kind == "m":
                        blocks = [(prob[m % 3][:, k * P:(k + 1) * P], 0) for k in range(4 * c, min(4 * c + 4, j + 1))]
                    elif c == 0:
                        blocks = [(prob[m % 3][:, i * BAND + CHUNK:(i + 1) * BAND], i) for i in range(GQ)]
                    else:
                        blocks = [(prob[m % 3][:, i * BAND:i * BAND + CHUNK], i) for i in range(GQ)]
                    keys = CHUNK if kind == "s" and c else P
                    for i, (block_, d) in enumerate(blocks):
                        ins = mm(psT[0:keys, n % 2, i * P:(i + 1) * P], block_, diag[:, m % 2, d, :], start=True, stop=True)
                    ins.then_inc(t_full, 1)

            def weigh(u):
                kind, j, h = u
                if kind == "q" or h % 2 == 0:
                    return
                m = N_SOFT[u]
                for v in (SOFTMAXED[m - 1], u):
                    for c in range(chunks_of(v)):
                        evacuated((v, c))
                if h == 1 and (j or kind == "m"):
                    pe.wait_ge(y_ready, 2 * j + (kind == "m"))
                if kind == "m":
                    for k in range(j + 1):
                        for b in range(2):
                            g = h - 1 + b
                            ins = mm(results[b][:, h // 2 * P:(h // 2 + 1) * P], vmla[:, k, g * MLA_V:(g + 1) * MLA_V],
                                     probT[(m - 1 + b) % 4][:, k, :], start=(k == 0), stop=(k == j))
                else:
                    dims = [slice(ROPE + g * SWA_DIM, ROPE + (g + 1) * SWA_DIM) for g in range(SWA_KV)]
                    out = [r.rearrange("p (k n) -> p k n", n=P) for r in results]
                    for g in range(SWA_KV):
                        ins = mm(out[g], krvs[:, j, dims[g]], probT[(m - 1 + g) % 4][:, 0:4, :], start=True, stop=(j == 0))
                    for g in range(SWA_KV if j else 0):
                        ins = mm(out[g], krvs[CHUNK:P, j - 1, dims[g]], probT[(m - 1 + g) % 4][CHUNK:P, 4:8, :], start=False, stop=True)
                ins.then_inc(pv_full, 1)

            pe.wait_ge(pj_free, 16)
            score(UNITS[0])
            for j in range(NT):
                if j >= 2:
                    pe.wait_ge(vv_free, j - 1)
                mm(bank(4 + j % 2), ckv[:, j * P:(j + 1) * P], wukv[:, 1, :, :].rearrange("p h n -> p (h n)"), start=True, stop=True).then_inc(vv_full, 1)
            for b in range(2):
                pe.wait_ge(kn_free[b], 4)
            pe.wait_ge(vv_free, NT)
            for t in range(len(UNITS) + 3):
                if 0 < t < len(UNITS):
                    score(UNITS[t])
                if 0 <= t - 2 < len(UNITS):
                    turn(UNITS[t - 2])
                if t >= 3:
                    weigh(UNITS[t - 3])

            def project(key, c, stationary, weights, steps):
                n = PROJ_NO[key]
                if n:
                    pe.wait_ge(ae_free, 2 * n - 1 + c)
                for k in range(steps):
                    ins = mm(bank(4 + c), stationary(k), weights(k, slice(c * 512, (c + 1) * 512)), start=(k == 0), stop=(k == steps - 1))
                ins.then_inc(ae_full, 1)

            def output_projection(s, c):
                project(("A", s), c, lambda k: yT[:, k, s * P:(s + 1) * P], lambda k, cols: w_o[k][:, cols], KC)

            for s in range(2):
                pe.wait_ge(s_free[s], FREE_S[s])
            pe.wait_ge(y_ready, 2 * NT)
            pe.wait_ge(ld_wo, 16 * 12)
            for s in range(NT + 4):
                j = s - 4
                if 0 <= j < NT:
                    pe.wait_ge(ln_done, LN_NO["E", j] + 1)
                    for c in range(2):
                        transposes(("h2", j, c), [hring[:, j % 4, (4 * c + i) * P:(4 * c + i + 1) * P] for i in range(4)])
                if s < NT:
                    output_projection(s, 0)
                if 0 <= j < NT:
                    for c in range(2):
                        evacuated(("h2", j, c))
                    pe.wait_ge(om_ready, min(NT, j + 2))
                    if j == 0:
                        pe.wait_ge(ld_late, 16 * 8)
                    for k in range(KC):
                        ins = mm(psN[:, 0:ROUTE], h2T[:, k, :], w_route[:, k, :], start=(k == 0), stop=(k == KC - 1))
                    ins.then_inc(r_full, 1)
                j = s - 2
                if 0 <= j < NT:
                    pe.wait_ge(p8_ready, j + 1)
                    for c in range(2):
                        transposes(("p8", j, c), [prob[0][:, (4 * c + i) * P:(4 * c + i + 1) * P] for i in range(4)])
                if s < NT:
                    output_projection(s, 1)
                j = s - 1
                if 0 <= j < NT:
                    pe.wait_ge(ln_done, LN_NO["A", j] + 1)
                    for c in range(2):
                        transposes(("h1", j, c), [hring[:, j % 4, (4 * c + i) * P:(4 * c + i + 1) * P] for i in range(4)])
                j = s - 2
                if 0 <= j < NT:
                    for c in range(2):
                        evacuated(("p8", j, c))
                    if j:
                        pe.wait_ge(om_ready, j)
                    if j >= 2:
                        pe.wait_ge(r_ready, j - 1)
                    for h in range(MEM_HEADS):
                        for t in range(2):
                            ins = mm(psN[:, h * P:(h + 1) * P], probT[0][:, 2 * h + t, :], vm[:, t, h * P:(h + 1) * P],
                                     start=(t == 0), stop=(t == 1))
                    ins.then_inc(o8_full, 1)
                j = s - 1
                if 0 <= j < NT:
                    if j == 0:
                        pe.wait_ge(ld_wmq, 16)
                    for c in range(2):
                        evacuated(("h1", j, c))
                    if j:
                        pe.wait_ge(qm_ready, j)
                    for h in range(MEM_HEADS):
                        for k in range(KC):
                            ins = mm(psM[:, h * P:(h + 1) * P], w_mq[:, k, h * P:(h + 1) * P], h1T[:, j % 2, k, :],
                                     start=(k == 0), stop=(k == KC - 1))
                    ins.then_inc(qm_full, 1)
                j = s - 2
                if 0 <= j < NT:
                    pe.wait_ge(om_ready, j + 1)
                    transposes(("o8", j, 0), [om[:, i * P:(i + 1) * P] for i in range(4)])
                j = s - 1
                if 0 <= j < NT:
                    pe.wait_ge(qm_ready, j + 1)
                    if j:
                        pe.wait_ge(p8_ready, j)
                    for h in range(MEM_HEADS):
                        ins = mm(psS[:, 0, h * N_MEM:(h + 1) * N_MEM], qm[:, h, :], kmT[:, h, :], start=True, stop=True)
                    ins.then_inc(c_full, 1)
                j = s - 2
                if 0 <= j < NT:
                    if j == 0:
                        pe.wait_ge(ld_wmo, 16)
                    evacuated(("o8", j, 0))
                    for c in range(2):
                        project(("E", j), c, lambda k: omT[:, k, :], lambda k, cols: w_mo[:, k, cols], MEM_HEADS)
            pe.wait_ge(oh_ready, 1)
            flat = oh_sum[:, :, :].rearrange("p j e -> p (j e)")
            mm(bank(2)[:, 0:NT * N_EXP], tri[:, :], flat, start=True, stop=True).then_inc(rank_full, 1)
            mm(bank(3)[:, 0:NT * N_EXP], ones[:, :], flat, start=True, stop=True).then_inc(rank_full, 1)

            pe.wait_ge(item_cols_ready, 1)
            for c in range(2):
                ins = mm(bank(5)[0:1, c * P:(c + 1) * P], item_cols[:, c:c + 1], ident[:, :], start=True, stop=True)
            ins.then_inc(items_full, 1)
            for c in range(NT * TOP_K):
                j, k = divmod(c, TOP_K)
                pe.wait_ge(marks_ready, c + 1)
                ins = mm(bank(4)[:, 0:2 * MAX_ITEMS], mark_row[:, j, k, :], mark_item[:, j, k, :, :].rearrange("p f i -> p (f i)"),
                         start=(c == 0), stop=(c == NT * TOP_K - 1))
            ins.then_inc(table_full, 1)

            pe.wait_ge(items_ready, 1)
            n_items = pe.value_load(n_items_t[0:1, 0:1], min_val=1, max_val=MAX_ITEMS)

            def turn_x(s, count):
                pe.wait_ge(x_loaded[s], count * 16)
                for c in range(2):
                    for i in range(4):
                        k = 4 * c + i
                        ins = T(psT[:, c, i * P:(i + 1) * P], xg[s][:, k * P:(k + 1) * P], ident[:, :])
                    ins.then_inc(xT_full[s], 1)

            def gate_up(s, count, wide):
                pe.wait_ge(xT_ready[s], count)
                for k in range(KC):
                    if k % 4 == 0:
                        pe.wait_ge(gu_loaded[s][k // 4], count * 16)
                    for c in range(2):
                        out, x = (bank(2 + c), xgT[s][:, k, :]) if wide else (bank(2 + c)[c * HALF_P:(c + 1) * HALF_P, :], xgT[s][:, k, 0:HALF_P])
                        ins = mm(out, x, w_gu[s][:, k, c * 512:(c + 1) * 512], start=(k == 0), stop=(k == KC - 1))
                ins.then_inc(gu_full, 1)

            def turn_act(s, i):
                pe.wait_ge(act_ready, i + 1)
                for k in range(4):
                    ins = T(psM[:, k * P:(k + 1) * P], act[s][:, k * P:(k + 1) * P], ident[:, :])
                ins.then_inc(aT_full, 1)

            def down(s, i, count, wide):
                pe.wait_ge(aT_ready, i + 1)
                pe.wait_ge(dn_loaded[s], count * 16)
                for c, k in ([(c, k) for c in range(2) for k in range(4)] if wide else [(c, k) for k in range(4) for c in range(2)]):
                    out, h = (bank(4 + c), actT[s][:, k, :]) if wide else (bank(4 + c)[c * HALF_P:(c + 1) * HALF_P, :], actT[s][:, k, HALF_P:P])
                    ins = mm(out, h, w_dn[s][:, k, c * 512:(c + 1) * 512], start=(k == 0), stop=(k == 3))
                    if k == 3:
                        ins.then_inc(y_full, 1)

            def by_kind(kind, step):
                with pe.If(kind > NO_ITEM):
                    step(True)
                with pe.If(kind < NO_ITEM):
                    step(False)

            turn_x(0, 1)
            by_kind(pe.value_load(item_kind[0:1, 0:1], min_val=0, max_val=WIDE), lambda wide: gate_up(0, 1, wide))
            with pe.Fori(0, MAX_ITEMS // 2) as r:
                for s in range(2):
                    i = r * 2 + s
                    kind = pe.value_load(item_kind[0:1, bass.ds(i, 1)], min_val=0, max_val=WIDE)
                    next_kind = pe.value_load(item_kind[0:1, bass.ds(i + 1, 1)], min_val=0, max_val=WIDE)
                    with pe.If(i + 1 < n_items):
                        turn_x(1 - s, r + (1 + s))
                    with pe.If(i < n_items):
                        turn_act(s, i)
                    by_kind(next_kind, lambda wide: gate_up(1 - s, r + (1 + s), wide))
                    by_kind(kind, lambda wide: down(s, i, r + 1, wide))


def constants():
    inv = (10000.0 ** (-np.arange(0, ROPE, 2) / ROPE)).astype(np.float32)
    ident = np.eye(P, dtype=np.float32)
    tri = np.triu(np.ones((P, P), np.float32), 1)
    i, w = np.arange(P)[:, None], np.arange(BAND)[None, :] - CHUNK
    seen = (w // CHUNK <= i // CHUNK) & (w // CHUNK >= i // CHUNK - 1)
    slopes = 2.0 ** (-8.0 * np.arange(1, SWA_HEADS + 1) / SWA_HEADS)
    alibi = np.where(seen[:, None, :], -slopes[None, :, None] * np.abs(i - w)[:, None, :], MASKED)
    rope = np.zeros((P, 4), np.float32)
    rope[:, 0] = inv[np.arange(P) % 16]
    rope[NOPE:QK, 1], rope[NOPE:QK, 2] = 0.25, np.pi / 2
    p, j, k = np.arange(P)[:, None, None], np.arange(NT)[None, :, None], np.arange(TOP_K)[None, None, :]
    choice = (TOP_K * (j * P + p) + k + 1).astype(np.float32)
    item = np.stack([np.arange(P), P * np.arange(P) + P // 2], 1).astype(np.float32)
    iotas = np.concatenate([np.arange(N_EXP) - 64.0, np.arange(P)])[None, :]
    return {"c_ident": ident, "c_tri": tri, "c_alibi": alibi.reshape(P, -1).astype(np.float32), "c_rope": rope,
            "c_inv": inv[None, :], "c_choice": choice.reshape(P, -1), "c_item": item, "c_iotas": iotas.astype(np.float32)}


_TWO_DIM = ["x", "positions", "mem", "w_in", "w_uq", "w_ukv", "w_o", "w_mq", "w_mk", "w_mv", "w_mo", "w_group", "w_expert"]
_ROWS = ["ln_in_g", "ln_in_b", "g_q", "g_kv", "sinks", "ln1_g", "ln1_b", "ln2_g", "ln2_b", "b_group", "b_expert", "ln3_g", "ln3_b"]
_THREE_DIM = ["w_gate_up", "w_down"]


def kernel(**inputs):
    import concourse.bacc as bacc
    from concourse.bass_utils import run_bass_kernel_spmd

    arrays = dict(constants())
    for n in _TWO_DIM:
        v = np.asarray(inputs[n])
        arrays[n] = v if n == "positions" else v.reshape(v.shape[-2:])
    for n in _ROWS:
        arrays[n] = np.asarray(inputs[n]).reshape(1, -1)
    for n in _THREE_DIM:
        v = np.asarray(inputs[n])
        arrays[n] = v.reshape(v.shape[-3:])
    arrays = {f"in_{n}": np.ascontiguousarray(v) for n, v in arrays.items()}
    nc = bacc.Bacc("TRN2", target_bir_lowering=False, num_devices=1)
    a = {n[3:]: nc.dram_tensor(n, v.shape, mybir.dt.from_np(v.dtype), kind="ExternalInput").ap() for n, v in arrays.items()}
    out = nc.dram_tensor("out", [SEQ, D], F32, kind="ExternalOutput").ap()
    build_program(nc, a, out)
    r = run_bass_kernel_spmd(nc, [arrays], core_ids=[0])
    return r.results[0]["out"].reshape(np.asarray(inputs["x"]).shape)
```
